# Optimizing a Trainium2 kernel written in Bass

```python
import math
import jax, jax.numpy as jnp
from jax import lax
import numpy as np

D_MODEL = 2048
BATCH = 1
SEQ = 256
DEPTH = 1

A_HEADS = 16
A_KV_HEADS = 4
A_HEAD_DIM = 64
A_GROUP = A_HEADS // A_KV_HEADS
WINDOW = 128
A_BLOCK = 128
A_Q_WIDTH = A_HEADS * A_HEAD_DIM
A_KV_WIDTH = A_KV_HEADS * A_HEAD_DIM
N_BUCKETS = 32
MAX_DISTANCE = 128
B_HEADS = 4
B_KEY_DIM = 128
B_VAL_DIM = 256
B_QK_WIDTH = B_HEADS * B_KEY_DIM
B_V_WIDTH = B_HEADS * B_VAL_DIM
B_GATE_RANK = 16
B_GATE_TAU = 16.0
B_CHUNK = 64
D_FF = -(-(8 * D_MODEL) // (3 * 256)) * 256
EPS = 1e-6
NEG_INF = -1e30

IN_SPLITS = (A_Q_WIDTH, A_KV_WIDTH, A_KV_WIDTH,
             B_QK_WIDTH, B_QK_WIDTH, B_V_WIDTH, B_GATE_RANK, B_V_WIDTH,
             D_MODEL, D_MODEL)
IN_WIDTH = sum(IN_SPLITS)


def rmsnorm(x, g):
    xf = x.astype(jnp.float32)
    y = xf * lax.rsqrt(jnp.mean(xf * xf, axis=-1, keepdims=True) + EPS)
    return (y * g.astype(jnp.float32)).astype(x.dtype)

def t5_causal_bucket(dist):
    max_exact = N_BUCKETS // 2
    d = jnp.maximum(dist, 0)
    large = max_exact + (jnp.log(jnp.maximum(d, 1).astype(jnp.float32) / max_exact)
                         / math.log(MAX_DISTANCE / max_exact)
                         * (N_BUCKETS - max_exact)).astype(jnp.int32)
    large = jnp.minimum(large, N_BUCKETS - 1)
    return jnp.where(d < max_exact, d, large)

def sliding_window_attention(q, k, v, sinks, rel_bias):
    B, S = q.shape[0], q.shape[1]
    nb = S // A_BLOCK
    qb = (q * (A_HEAD_DIM ** -0.5)).reshape(B, nb, A_BLOCK, A_KV_HEADS, A_GROUP, A_HEAD_DIM)
    pad = ((0, 0), (A_BLOCK, 0), (0, 0), (0, 0))
    kp = jnp.pad(k, pad).reshape(B, nb + 1, A_BLOCK, A_KV_HEADS, A_HEAD_DIM)
    vp = jnp.pad(v, pad).reshape(B, nb + 1, A_BLOCK, A_KV_HEADS, A_HEAD_DIM)
    kb = jnp.concatenate([kp[:, :-1], kp[:, 1:]], axis=2)
    vb = jnp.concatenate([vp[:, :-1], vp[:, 1:]], axis=2)
    s = jnp.einsum('bnqkgd,bnskd->bnkgqs', qb, kb).astype(jnp.float32)
    q_loc = jnp.arange(A_BLOCK)[:, None] + A_BLOCK
    k_loc = jnp.arange(2 * A_BLOCK)[None, :]
    dist = q_loc - k_loc
    band = (dist >= 0) & (dist < WINDOW)
    k_abs = jnp.arange(nb)[:, None, None] * A_BLOCK + k_loc[None] - A_BLOCK
    mask = band[None] & (k_abs >= 0)
    bias = rel_bias.astype(jnp.float32)[t5_causal_bucket(dist)]
    bias = bias.transpose(2, 0, 1).reshape(A_KV_HEADS, A_GROUP, A_BLOCK, 2 * A_BLOCK)
    s = jnp.where(mask[None, :, None, None], s + bias[None, None], NEG_INF)
    sink = sinks.astype(jnp.float32).reshape(A_KV_HEADS, A_GROUP)[None, None, :, :, None, None]
    m = jnp.maximum(jnp.max(s, axis=-1, keepdims=True), sink)
    p = jnp.exp(s - m)
    denom = jnp.sum(p, axis=-1, keepdims=True) + jnp.exp(sink - m)
    o = jnp.einsum('bnkgqs,bnskd->bnqkgd', (p / denom).astype(v.dtype), vb)
    return o.reshape(B, S, A_Q_WIDTH)

def gated_linear_attention(q, k, v, log_a):
    B, S = q.shape[0], q.shape[1]
    nc = S // B_CHUNK

    def chunks(t):
        return t.astype(jnp.float32).reshape(B, nc, B_CHUNK, B_HEADS, -1).transpose(0, 3, 1, 2, 4)

    qc = chunks(q) * (B_KEY_DIM ** -0.5)
    kc, vc, gc = chunks(k), chunks(v), chunks(log_a)
    b = jnp.cumsum(gc, axis=3)
    b_last = b[:, :, :, -1:, :]
    q_dec = qc * jnp.exp(b)
    k_dec = kc * jnp.exp(-b)
    k_state = kc * jnp.exp(b_last - b)
    causal = jnp.tril(jnp.ones((B_CHUNK, B_CHUNK), dtype=bool))
    att = jnp.where(causal, jnp.einsum('bhncd,bhnsd->bhncs', q_dec, k_dec), 0.0)
    o_intra = jnp.einsum('bhncs,bhnsv->bhncv', att, vc)
    dS = jnp.einsum('bhncd,bhncv->bhndv', k_state, vc)
    decay = jnp.exp(b_last[:, :, :, 0, :])

    def step(state, inp):
        dS_n, decay_n = inp
        return decay_n[..., None] * state + dS_n, state

    s0 = jnp.zeros((B, B_HEADS, B_KEY_DIM, B_VAL_DIM), jnp.float32)
    _, s_prev = lax.scan(step, s0, (dS.transpose(2, 0, 1, 3, 4), decay.transpose(2, 0, 1, 3)))
    s_prev = s_prev.transpose(1, 2, 0, 3, 4)
    o_inter = jnp.einsum('bhncd,bhndv->bhncv', q_dec, s_prev)
    o = o_intra + o_inter
    return o.transpose(0, 2, 3, 1, 4).reshape(B, S, B_HEADS, B_VAL_DIM)

def first_inputs(seed: int = 0) -> dict:
    key = jax.random.key(seed)
    ks = jax.random.split(key, 20)
    L = DEPTH

    def w(k, shape, fan_in):
        return jax.random.normal(k, shape, jnp.float32) * (fan_in ** -0.5)

    def gain(k, shape):
        return 1.0 + 0.02 * jax.random.normal(k, shape, jnp.float32)

    return {
        "x": jax.random.normal(ks[0], (BATCH, SEQ, D_MODEL), jnp.float32),
        "norm_mix_g": gain(ks[1], (L, D_MODEL)),
        "w_in": w(ks[2], (L, D_MODEL, IN_WIDTH), D_MODEL),
        "sinks": 0.5 * jax.random.normal(ks[3], (L, A_HEADS), jnp.float32),
        "rel_bias": 0.5 * jax.random.normal(ks[4], (N_BUCKETS, A_HEADS), jnp.float32),
        "w_gate_up": w(ks[5], (L, B_GATE_RANK, B_QK_WIDTH), B_GATE_RANK),
        "b_gate": 0.1 * jax.random.normal(ks[6], (L, B_QK_WIDTH), jnp.float32),
        "gla_norm_g": gain(ks[7], (L, B_VAL_DIM)),
        "w_proj_a": w(ks[8], (L, A_Q_WIDTH, D_MODEL), A_Q_WIDTH),
        "w_proj_b": w(ks[9], (L, B_V_WIDTH, D_MODEL), B_V_WIDTH),
        "w_out": w(ks[10], (L, D_MODEL, D_MODEL), D_MODEL),
        "norm_ffn_g": gain(ks[11], (L, D_MODEL)),
        "w_ffn_gate": w(ks[12], (L, D_MODEL, D_FF), D_MODEL),
        "w_ffn_up": w(ks[13], (L, D_MODEL, D_FF), D_MODEL),
        "w_ffn_down": w(ks[14], (L, D_FF, D_MODEL), D_FF),
        "norm_final_g": gain(ks[15], (D_MODEL,)),
    }

def first_block(x, norm_mix_g, w_in, sinks, rel_bias, w_gate_up, b_gate, gla_norm_g,
              w_proj_a, w_proj_b, w_out, norm_ffn_g, w_ffn_gate, w_ffn_up, w_ffn_down,
              norm_final_g):
    B, S = x.shape[0], x.shape[1]
    split_idx = [int(i) for i in np.cumsum(IN_SPLITS)[:-1]]
    h = x
    for l in range(DEPTH):
        u = rmsnorm(h, norm_mix_g[l])
        proj = u @ w_in[l]
        qa, ka, va, qb, kb, vb, g_low, ob_gate, gate_a, gate_b = jnp.split(proj, split_idx, axis=-1)
        ya = sliding_window_attention(
            qa.reshape(B, S, A_HEADS, A_HEAD_DIM),
            ka.reshape(B, S, A_KV_HEADS, A_HEAD_DIM),
            va.reshape(B, S, A_KV_HEADS, A_HEAD_DIM),
            sinks[l], rel_bias)
        ya = ya @ w_proj_a[l]
        log_a = jax.nn.log_sigmoid((g_low @ w_gate_up[l] + b_gate[l]).astype(jnp.float32)) / B_GATE_TAU
        ob = gated_linear_attention(
            qb.reshape(B, S, B_HEADS, B_KEY_DIM),
            kb.reshape(B, S, B_HEADS, B_KEY_DIM),
            vb.reshape(B, S, B_HEADS, B_VAL_DIM),
            log_a.reshape(B, S, B_HEADS, B_KEY_DIM))
        ob = rmsnorm(ob, gla_norm_g[l]).reshape(B, S, B_V_WIDTH).astype(x.dtype)
        yb = (ob * jax.nn.silu(ob_gate)) @ w_proj_b[l]
        merged = jax.nn.sigmoid(gate_a) * ya + jax.nn.sigmoid(gate_b) * yb
        h = h + (merged @ w_out[l]).astype(h.dtype)
        z = rmsnorm(h, norm_ffn_g[l])
        ff = (jax.nn.silu(z @ w_ffn_gate[l]) * (z @ w_ffn_up[l])) @ w_ffn_down[l]
        h = h + ff.astype(h.dtype)
    return rmsnorm(h, norm_final_g)


HEAD_DIM = 128
SB_HEADS = D_MODEL // (2 * HEAD_DIM)
GDN_HEADS = D_MODEL // (2 * HEAD_DIM)
SB_WIDTH = SB_HEADS * HEAD_DIM
GDN_WIDTH = GDN_HEADS * HEAD_DIM
D_MIX = SB_WIDTH + GDN_WIDTH
N_IN = 3 * SB_WIDTH + 4 * GDN_WIDTH + 2 * GDN_HEADS
SB_BLOCK = 128
SHORT_CONV = 4
CHUNK = 64
N_MEM = 256
X_HEADS = 4
X_HEAD_DIM = 128
X_WIDTH = X_HEADS * X_HEAD_DIM
D_FF_2 = (11 * D_MODEL) // 4
FFN_CONV = 3


def rmsnorm_2(x, g):
    xf = x.astype(jnp.float32)
    y = xf * lax.rsqrt(jnp.mean(xf * xf, axis=-1, keepdims=True) + EPS)
    return (y * g.astype(jnp.float32)).astype(x.dtype)

def l2norm(x):
    return x * lax.rsqrt(jnp.sum(x * x, axis=-1, keepdims=True) + EPS)

def causal_dwconv(x, w):
    k = w.shape[0]
    return lax.conv_general_dilated(
        x, w[:, None, :].astype(x.dtype), window_strides=(1,), padding=[(k - 1, 0)],
        dimension_numbers=('NWC', 'WIO', 'NWC'), feature_group_count=x.shape[-1])

def stick_breaking_attention(q, k, v):
    b, s, h, dh = q.shape
    scale = dh ** -0.5
    n_blk = s // SB_BLOCK
    qb = jnp.moveaxis(q.reshape(b, n_blk, SB_BLOCK, h, dh), 1, 0)
    key_pos = jnp.arange(s)

    def block(args):
        q_blk, blk_idx = args
        z = jnp.einsum('bqhd,bshd->bhqs', q_blk, k) * scale
        q_pos = blk_idx * SB_BLOCK + jnp.arange(SB_BLOCK)
        valid = key_pos[None, :] < q_pos[:, None]
        log_beta = jax.nn.log_sigmoid(z)
        log_stay = jnp.where(valid, jax.nn.log_sigmoid(-z), 0.0)
        later = lax.cumsum(log_stay, axis=3, reverse=True) - log_stay
        weights = jnp.where(valid, jnp.exp(log_beta + later), 0.0)
        return jnp.einsum('bhqs,bshd->bqhd', weights, v)

    out = lax.map(block, (qb, jnp.arange(n_blk)))
    return jnp.moveaxis(out, 0, 1).reshape(b, s, h, dh)

def gated_delta_rule(q, k, v, beta, g):
    b, s, h, dk = q.shape
    dv = v.shape[-1]
    n = s // CHUNK

    def chunks(t):
        t = jnp.swapaxes(t, 1, 2)
        return t.reshape(b, h, n, CHUNK, *t.shape[3:])

    q, k, v, beta, g = chunks(q), chunks(k), chunks(v), chunks(beta), chunks(g)
    g_cum = jnp.cumsum(g, axis=-1)
    idx = jnp.arange(CHUNK)
    lower_incl = idx[:, None] >= idx[None, :]
    strict = idx[:, None] > idx[None, :]
    decay = jnp.exp(jnp.where(lower_incl, g_cum[..., :, None] - g_cum[..., None, :], -jnp.inf))
    k_beta = k * beta[..., None]
    v_beta = v * beta[..., None]
    lmat = jnp.where(strict, jnp.einsum('bhnid,bhnjd->bhnij', k_beta, k) * decay, 0.0)
    eye = jnp.eye(CHUNK, dtype=jnp.float32)
    t_inv = lax.linalg.triangular_solve(eye + lmat, jnp.broadcast_to(eye, lmat.shape),
                                        left_side=True, lower=True, unit_diagonal=True)
    u = t_inv @ v_beta
    w = t_inv @ (k_beta * jnp.exp(g_cum)[..., None])
    attn_intra = jnp.where(lower_incl, jnp.einsum('bhnid,bhnjd->bhnij', q, k) * decay, 0.0)
    q_decay = q * jnp.exp(g_cum)[..., None]
    k_tail = k * jnp.exp(g_cum[..., -1:] - g_cum)[..., None]
    chunk_decay = jnp.exp(g_cum[..., -1])

    def step(state, xs):
        u_c, w_c, qd_c, a_c, kt_c, cd_c = xs
        v_new = u_c - w_c @ state
        o = qd_c @ state + a_c @ v_new
        state = state * cd_c[..., None, None] + jnp.swapaxes(kt_c, -1, -2) @ v_new
        return state, o

    xs = tuple(jnp.moveaxis(t, 2, 0) for t in (u, w, q_decay, attn_intra, k_tail, chunk_decay))
    state0 = jnp.zeros((b, h, dk, dv), jnp.float32)
    _, o = lax.scan(step, state0, xs)
    o = jnp.moveaxis(o, 0, 2).reshape(b, h, s, dv)
    return jnp.swapaxes(o, 1, 2)

def gated_deltanet(q, k, v, z, b_logit, a_logit, conv_w, a_log, dt_bias, norm_g):
    bsz, s, _ = q.shape
    qkv = jnp.concatenate([q, k, v], axis=-1).astype(jnp.float32)
    qkv = jax.nn.silu(causal_dwconv(qkv, conv_w.astype(jnp.float32)))
    q, k, v = jnp.split(qkv, 3, axis=-1)
    heads = lambda t: t.reshape(bsz, s, GDN_HEADS, HEAD_DIM)
    q = l2norm(heads(q)) * (HEAD_DIM ** -0.5)
    k = l2norm(heads(k))
    v = heads(v)
    beta = jax.nn.sigmoid(b_logit.astype(jnp.float32))
    g = -jnp.exp(a_log.astype(jnp.float32)) * jax.nn.softplus(
        a_logit.astype(jnp.float32) + dt_bias.astype(jnp.float32))
    o = gated_delta_rule(q, k, v, beta, g)
    o = rmsnorm_2(o, norm_g) * jax.nn.silu(heads(z.astype(jnp.float32)))
    return o.reshape(bsz, s, GDN_WIDTH)

def memory_cross_attention(h, mem_n, w_q, w_kv, w_o):
    bsz, s, _ = h.shape
    m = mem_n.shape[1]
    q = (h @ w_q).reshape(bsz, s, X_HEADS, X_HEAD_DIM)
    k, v = jnp.split(mem_n @ w_kv, 2, axis=-1)
    k = k.reshape(bsz, m, X_HEADS, X_HEAD_DIM)
    v = v.reshape(bsz, m, X_HEADS, X_HEAD_DIM)
    logits = jnp.einsum('bshd,bmhd->bhsm', q.astype(jnp.float32), k.astype(jnp.float32)) * (X_HEAD_DIM ** -0.5)
    p = jax.nn.softmax(logits, axis=-1)
    o = jnp.einsum('bhsm,bmhd->bshd', p, v.astype(jnp.float32))
    return o.reshape(bsz, s, X_WIDTH).astype(h.dtype) @ w_o

def conv_ffn(h, w_up, conv_w, conv_b, w_down):
    u = causal_dwconv(h @ w_up, conv_w) + conv_b
    gate, up = jnp.split(u, 2, axis=-1)
    return (jax.nn.silu(gate) * up) @ w_down

def second_inputs(seed: int = 0) -> dict:
    key = jax.random.key(seed)
    ks = iter(jax.random.split(key, 32))
    f32 = jnp.float32
    nrm = lambda shape, scale: jax.random.normal(next(ks), shape, f32) * scale
    gain = lambda shape: 1.0 + 0.02 * jax.random.normal(next(ks), shape, f32)
    dt = jnp.exp(jax.random.uniform(next(ks), (DEPTH, GDN_HEADS), f32, np.log(1e-3), np.log(1e-1)))
    return {
        "x": jax.random.normal(next(ks), (BATCH, SEQ, D_MODEL), f32),
        "mem": jax.random.normal(next(ks), (BATCH, N_MEM, D_MODEL), f32),
        "mix_norm": gain((DEPTH, D_MODEL)),
        "w_in": nrm((DEPTH, D_MODEL, N_IN), D_MODEL ** -0.5),
        "gdn_conv": nrm((DEPTH, SHORT_CONV, 3 * GDN_WIDTH), SHORT_CONV ** -0.5),
        "gdn_a_log": jnp.log(jax.random.uniform(next(ks), (DEPTH, GDN_HEADS), f32, 1.0, 16.0)),
        "gdn_dt_bias": dt + jnp.log(-jnp.expm1(-dt)),
        "gdn_norm": gain((DEPTH, HEAD_DIM)),
        "w_out": nrm((DEPTH, D_MIX, D_MODEL), D_MIX ** -0.5),
        "xattn_norm": gain((DEPTH, D_MODEL)),
        "mem_norm": gain((DEPTH, D_MODEL)),
        "w_xq": nrm((DEPTH, D_MODEL, X_WIDTH), D_MODEL ** -0.5),
        "w_xkv": nrm((DEPTH, D_MODEL, 2 * X_WIDTH), D_MODEL ** -0.5),
        "w_xo": nrm((DEPTH, X_WIDTH, D_MODEL), X_WIDTH ** -0.5),
        "ffn_norm": gain((DEPTH, D_MODEL)),
        "w_up": nrm((DEPTH, D_MODEL, 2 * D_FF_2), D_MODEL ** -0.5),
        "ffn_conv": nrm((DEPTH, FFN_CONV, 2 * D_FF_2), FFN_CONV ** -0.5),
        "ffn_conv_bias": nrm((DEPTH, 2 * D_FF_2), 0.02),
        "w_down": nrm((DEPTH, D_FF_2, D_MODEL), D_FF_2 ** -0.5),
        "final_norm": gain((D_MODEL,)),
    }

def second_block(x, mem, mix_norm, w_in, gdn_conv, gdn_a_log, gdn_dt_bias, gdn_norm, w_out,
              xattn_norm, mem_norm, w_xq, w_xkv, w_xo, ffn_norm, w_up, ffn_conv,
              ffn_conv_bias, w_down, final_norm):
    bsz, s, _ = x.shape
    cuts = [SB_WIDTH, 2 * SB_WIDTH, 3 * SB_WIDTH,
            3 * SB_WIDTH + GDN_WIDTH, 3 * SB_WIDTH + 2 * GDN_WIDTH,
            3 * SB_WIDTH + 3 * GDN_WIDTH, 3 * SB_WIDTH + 4 * GDN_WIDTH,
            3 * SB_WIDTH + 4 * GDN_WIDTH + GDN_HEADS]
    sb_heads = lambda t: t.astype(jnp.float32).reshape(bsz, s, SB_HEADS, HEAD_DIM)
    for l in range(DEPTH):
        h = rmsnorm_2(x, mix_norm[l])
        proj = h @ w_in[l]
        sq, sk, sv, gq, gk, gv, gz, gb, ga = jnp.split(proj, cuts, axis=-1)
        sb_out = stick_breaking_attention(sb_heads(sq), sb_heads(sk), sb_heads(sv))
        sb_out = sb_out.reshape(bsz, s, SB_WIDTH)
        gdn_out = gated_deltanet(gq, gk, gv, gz, gb, ga, gdn_conv[l], gdn_a_log[l],
                                 gdn_dt_bias[l], gdn_norm[l])
        mixed = jnp.concatenate([sb_out, gdn_out], axis=-1).astype(x.dtype)
        x = x + mixed @ w_out[l]
        mem_n = rmsnorm_2(mem, mem_norm[l])
        x = x + memory_cross_attention(rmsnorm_2(x, xattn_norm[l]), mem_n, w_xq[l], w_xkv[l], w_xo[l])
        x = x + conv_ffn(rmsnorm_2(x, ffn_norm[l]), w_up[l], ffn_conv[l], ffn_conv_bias[l], w_down[l])
    return rmsnorm_2(x, final_norm)


def setup_inputs(seed=0):
    out = dict(first_inputs(seed))
    for name, value in second_inputs(seed + 1).items():
        if name != "x":
            out[name + "_2"] = value
    return out


def reference(
    x, norm_mix_g, w_in, sinks, rel_bias, w_gate_up, b_gate, gla_norm_g, w_proj_a, w_proj_b,
    w_out, norm_ffn_g, w_ffn_gate, w_ffn_up, w_ffn_down, norm_final_g, mem_2, mix_norm_2,
    w_in_2, gdn_conv_2, gdn_a_log_2, gdn_dt_bias_2, gdn_norm_2, w_out_2, xattn_norm_2,
    mem_norm_2, w_xq_2, w_xkv_2, w_xo_2, ffn_norm_2, w_up_2, ffn_conv_2, ffn_conv_bias_2,
    w_down_2, final_norm_2,
):
    x = first_block(
        x, norm_mix_g, w_in, sinks, rel_bias, w_gate_up, b_gate, gla_norm_g, w_proj_a, w_proj_b,
        w_out, norm_ffn_g, w_ffn_gate, w_ffn_up, w_ffn_down, norm_final_g,
    )
    return second_block(
        x, mem_2, mix_norm_2, w_in_2, gdn_conv_2, gdn_a_log_2, gdn_dt_bias_2, gdn_norm_2,
        w_out_2, xattn_norm_2, mem_norm_2, w_xq_2, w_xkv_2, w_xo_2, ffn_norm_2, w_up_2,
        ffn_conv_2, ffn_conv_bias_2, w_down_2, final_norm_2,
    )


_drawn_inputs = setup_inputs


def setup_inputs(seed=0):
    import zlib

    import numpy as np

    out = dict(_drawn_inputs(seed))
    spreads = {}
    factors = {'norm_mix_g': 2.898,
     'sinks': 5.18,
     'b_gate': 2.985,
     'gla_norm_g': 6.454,
     'norm_ffn_g': 3.243,
     'mix_norm_2': 3.342,
     'gdn_norm_2': 8.0,
     'xattn_norm_2': 8.0,
     'mem_norm_2': 8.0,
     'ffn_norm_2': 13.173,
     'ffn_conv_bias_2': 13.093,
     'final_norm_2': 7.894}
    for name, (base, spread) in spreads.items():
        noise = np.random.default_rng([zlib.crc32(name.encode()), seed]).standard_normal(out[name].shape)
        drawn = base * np.exp(spread * noise) if base else spread * noise
        out[name] = __import__('jax').numpy.asarray(drawn.astype(out[name].dtype))
    for name, factor in factors.items():
        out[name] = (out[name] * factor).astype(out[name].dtype)
    return out
```

```python
from contextlib import ExitStack

import concourse.bass as bass
from concourse import mybir

ALU = mybir.AluOpType
ACT = mybir.ActivationFunctionType
AX = mybir.AxisListType
F32 = mybir.dt.float32
F32R = mybir.dt.float32r

P = 128
T = 256
TT = T // P
D = 2048
DC = D // P
NT = 512
UC = 2
SLOTS = 4
LATE = 3
EPS = 1e-6
FF1, FF2 = 5632, 5632
HC = FF1 // P
NEG = -1e30
BIG = 3e38

QA, KA, VA, QB, KB, VB, GL, OG, GA, GB = 0, 1024, 1280, 1536, 2048, 2560, 3584, 3600, 4624, 6672
C_ID, C_CUM, C_AFT, C_AFTALL, C_BEFALL, C_ONES, C_HALF, C_LVL = 0, 1, 2, 3, 4, 5, 6, 8
LEVELS = 6
N_CONST = C_LVL + LEVELS
CH = 64

COLS = {}
_at = 0
for _name, _n in (("g_mix", DC), ("g_ffn", DC), ("g_mix2", DC), ("g_x2", DC), ("g_mem2", DC), ("g_ffn2", DC),
                  ("g_gla", 2), ("g_gdn", 1), ("conv", 96), ("fconv", 264), ("fbias", 88),
                  ("sinks", 16), ("alog", 8), ("dtb", 8)):
    COLS[_name] = (_at, _n)
    _at += _n
N_COLS = _at


def loop(eng, first, last, body):
    if last - first == 1:
        body(first)
    elif last > first:
        with eng.Fori(first, last) as i:
            body(i)


class Kernel:

    def __init__(self, nc, ctx):
        self.nc, self.ctx = nc, ctx
        self.unit = 0
        self.tile = 0
        self.steps = {"act": 0, "dve": 0, "pool": 0}
        self.t_done = 0
        self.n_sem = 0
        self.ring = self.sb("ring", [P, SLOTS, UC, NT], F32)
        self.w_hi = self.sb("w_hi", [P, SLOTS, UC, NT], F32R)
        self.w_lo = self.sb("w_lo", [P, SLOTS, UC, NT], F32R)
        self.h = self.sb("h", [P, TT, D], F32)
        self.ident = self.sb("ident", [P, P], F32)
        self.consts = None
        self.cols = self.sb("cols", [P, N_COLS], F32)
        self.small = self.sb("small", [P, 64], F32)
        self.ps = ctx.enter_context(nc.psum_tensor("ps", [P, 8, NT], F32))
        self.w_arrived = [self.sem(f"w_arrived{s}") for s in range(SLOTS)]
        self.hi_ready = self.sem("hi_ready")
        self.lo_ready = self.sem("lo_ready")
        self.unit_used = self.sem("unit_used")
        self.act_free = self.sem("act_free")
        self.dve_free = self.sem("dve_free")
        self.step = {e: self.sem(f"{e}_step") for e in self.steps}
        self.tp_done = self.sem("tp_done")
        self.tp_hi = self.sem("tp_hi")
        self.tp_lo = self.sem("tp_lo")
        self.narrow = self.sem("narrow")
        self.narrow_done = 0
        self.landed = self.sem("landed")

    def sb(self, name, shape, dt=F32, ctx=None):
        return (ctx or self.ctx).enter_context(self.nc.sbuf_tensor(name, shape, dt))

    def sem(self, name):
        self.n_sem += 1
        return self.ctx.enter_context(self.nc.semaphore(name))

    def const(self, c):
        return self.ident[:] if c == C_ID else self.consts[:, c, :]

    def col(self, name, i=0, n=1):
        at = COLS[name][0] + i
        return self.cols[:, at:at + n]

    def then(self, eng, key, ins):
        self.steps[key] += 1
        ins.then_inc(self.step[key], 1)
        eng.wait_ge(self.step[key], self.steps[key])


def weight_unit(w, row, col):
    return w[row:row + UC * P, bass.ds(col, NT)].rearrange("(c p) n -> p c n", p=P)


class Tile:

    def __init__(self, w, chunks, col, hi, lo, rows=0):
        self.w, self.chunks, self.col, self.hi, self.lo, self.rows = w, chunks, col, hi, lo, rows


def load_unit(k, sp, tiles, i, u, base):
    n = u
    for tile in tiles:
        if n < tile.chunks // UC:
            break
        n -= tile.chunks // UC
    sp.dma_start(k.ring[:, u % SLOTS], weight_unit(tile.w, tile.rows + n * UC * P, tile.col(i)))\
        .then_inc(k.w_arrived[u % SLOTS], 16)


def prefetch(k, sp, tiles, base):
    for u in range(SLOTS):
        if base:
            sp.wait_ge(k.lo_ready, base + u - SLOTS + 1)
        load_unit(k, sp, tiles, 0, u, base)


def product(k, name, tiles, passes, act_evac, dve_evac, hooks=(), after=None, sp_first=None, pe_last=None,
            act_last=None, dve_last=None):
    nc = k.nc
    sizes = [t.chunks // UC for t in tiles]
    units = sum(sizes)
    nt = len(tiles)
    base, tbase = k.unit, k.tile
    assert units % SLOTS == 0 and (nt % 2 == 0 or passes == 1) and base % SLOTS == 0
    k.unit += units * passes
    k.tile += nt * passes
    ends = [sum(sizes[:m + 1]) for m in range(nt)]
    evac_at = {}
    for m in range(nt):
        at = ends[m] - 1 + LATE
        evac_at.setdefault((at // units, at % units), []).append(m)

    def stream(eng, which, unit_step, evac):
        mine = [(u, fn) for e, u, fn in hooks if e == which]

        def body(i, first=False):
            for u in range(units):
                unit_step(i, u)
                if not first:
                    for m in evac_at.get((1, u), ()):
                        evac(m, i - 1)
                    for at, fn in mine:
                        if at == u:
                            fn(eng, i - 1)
                for m in evac_at.get((0, u), ()):
                    evac(m, i)

        body(0, True)
        loop(eng, 1, passes, body)
        for u in range(units):
            for m in evac_at.get((1, u), ()):
                evac(m, passes - 1)
            for at, fn in mine:
                if at == u:
                    fn(eng, passes - 1)

    with nc.Block() as block:
        @block.sync
        def _(sp):
            if sp_first:
                sp_first(sp)

            def body(i, more=True):
                for u in range(SLOTS, units + SLOTS * more):
                    paired = () if isinstance(i, int) else [e for e in ends[:-1] if e > SLOTS]
                    if u not in paired:
                        ahead = (u + 1) in paired
                        sp.wait_ge(k.lo_ready, base + u - SLOTS + 1 + ahead + i * units)
                    if u < units:
                        load_unit(k, sp, tiles, i, u, base)
                    else:
                        load_unit(k, sp, tiles, i + 1, u - units, base)
            loop(sp, 0, passes - 1, body)
            body(passes - 1, False)
            if after:
                prefetch(k, sp, after, k.unit)

        @block.scalar
        def _(act):
            def split_hi(i, u):
                s = u % SLOTS
                act.wait_ge(k.w_arrived[s], 16 * ((base + u) // SLOTS + 1) + i * (16 * units // SLOTS))
                act.wait_ge(k.unit_used, base + u + 1 + i * units)
                act.copy(k.w_hi[:, s], k.ring[:, s]).then_inc(k.hi_ready, 1)

            def evac(m, i):
                act.wait_ge(k.unit_used, SLOTS + base + ends[m] + i * units)
                last = act_evac(act, m, i, 2 * ((tbase + m) % 2))
                (last.then_inc if last is not None else lambda *a: act.sem_inc(*a))(k.act_free, 1)
            stream(act, "act", split_hi, evac)
            if act_last:
                act_last(act)

        @block.vector
        def _(dve):
            def split_lo(i, u):
                s = u % SLOTS
                dve.wait_ge(k.hi_ready, base + u + 1 + i * units)
                dve.tensor_tensor(k.w_lo[:, s], k.ring[:, s], k.w_hi[:, s].bitcast(F32), ALU.subtract)\
                    .then_inc(k.lo_ready, 1)

            def evac(m, i):
                dve.wait_ge(k.unit_used, SLOTS + base + ends[m] + i * units)
                last = dve_evac(dve, m, i, 2 * ((tbase + m) % 2))
                (last.then_inc if last is not None else lambda *a: dve.sem_inc(*a))(k.dve_free, 1)
            stream(dve, "dve", split_lo, evac)
            if dve_last:
                dve_last(dve)

        @block.tensor
        def _(pe):
            mine = [(u, fn) for e, u, fn in hooks if e == "pe"]

            def body(i, first=False):
                u = 0
                for m, tile in enumerate(tiles):
                    bank = 2 * ((tbase + m) % 2)
                    pe.wait_ge(k.act_free, tbase + m + 1 + i * nt)
                    pe.wait_ge(k.dve_free, tbase + m + 1 + i * nt)
                    for n in range(sizes[m]):
                        s = u % SLOTS
                        pe.wait_ge(k.lo_ready, base + u + 1 + i * units)
                        for c in range(UC):
                            kc = n * UC + c
                            for t in range(TT):
                                acc = k.ps[:, bank + t, :]
                                hi = tile.hi[:, kc, t * P:(t + 1) * P]
                                lo = tile.lo[:, kc, t * P:(t + 1) * P]
                                pe.matmul(acc, hi, k.w_hi[:, s, c, :], start=(kc == 0), stop=False)
                                pe.matmul(acc, hi, k.w_lo[:, s, c, :], start=False, stop=False)
                                last = pe.matmul(acc, lo, k.w_hi[:, s, c, :], start=False,
                                                 stop=(kc == tile.chunks - 1))
                        last.then_inc(k.unit_used, 1)
                        if not first:
                            for at, fn in mine:
                                if at == u:
                                    fn(pe, i - 1)
                        u += 1
            if mine:
                body(0, True)
                loop(pe, 1, passes, body)
                for _, fn in mine:
                    fn(pe, passes - 1)
            else:
                loop(pe, 0, passes, body)
            if pe_last:
                pe_last(pe)


def transpose_pe(k, pe, src, chunks, ready):
    for s in range(chunks // 2):
        bank = 4 + s % 4
        ready(pe, s)
        if s >= 4:
            pe.wait_ge(k.tp_lo, k.t_done + s - 3)
        for c in range(2):
            for t in range(TT):
                last = pe.transpose(k.ps[:, bank, c * T + t * P:c * T + (t + 1) * P],
                                    src[:, t, (2 * s + c) * P:(2 * s + c + 1) * P], k.const(C_ID))
        last.then_inc(k.tp_done, 1)


def transpose_act(k, act, chunks, gain, hi):
    for s in range(chunks // 2):
        act.wait_ge(k.tp_done, k.t_done + s + 1)
        bank = 4 + s % 4
        for c in range(2):
            at = 2 * s + c
            last = act.activation(hi[:, at, :], k.ps[:, bank, c * T:(c + 1) * T], ACT.Copy, scale=gain(at))
        last.then_inc(k.tp_hi, 1)


def transpose_dve(k, dve, chunks, gain, hi, lo):
    for s in range(chunks // 2):
        dve.wait_ge(k.tp_hi, k.t_done + s + 1)
        bank = 4 + s % 4
        for c in range(2):
            at = 2 * s + c
            last = dve.scalar_tensor_tensor(lo[:, at, :], k.ps[:, bank, c * T:(c + 1) * T], gain(at),
                                            hi[:, at, :].bitcast(F32), ALU.mult, ALU.subtract)
        last.then_inc(k.tp_lo, 1)


def norm_transposed(k, src, gain, hi, lo, sp_work=None, nrm=None):
    nc = k.nc
    with ExitStack() as ctx:
        if nrm is None:
            nrm = k.sb(f"nrm{k.t_done}", [P, TT, D], F32, ctx)
        sums = k.small[:, 0:2]
        dve0 = k.steps["dve"]
        act0 = k.steps["act"]
        with nc.Block() as block:
            @block.sync
            def _(sp):
                if sp_work:
                    sp_work(sp)

            @block.scalar
            def _(act):
                for t in range(TT):
                    act.activation(nrm[:, t, :], src[:, t, :], ACT.Square, accum_out=sums[:, t:t + 1])\
                        .then_inc(k.step["act"], 1)
                k.steps["act"] += TT
                act.wait_ge(k.step["act"], k.steps["act"])
                act.wait_ge(k.step["dve"], dve0 + 1)
                act.activation(k.small[:, 2:4], k.small[:, 2:4], ACT.Sqrt).then_inc(k.step["act"], 1)
                k.steps["act"] += 1
                transpose_act(k, act, DC, gain, hi)

            @block.vector
            def _(dve):
                dve.wait_ge(k.step["act"], act0 + 2)
                k.then(dve, "dve", dve.tensor_scalar(k.small[:, 2:4], sums, 1.0 / D, EPS, ALU.mult, ALU.add))
                dve.wait_ge(k.step["act"], act0 + 3)
                k.then(dve, "dve", dve.reciprocal(k.small[:, 4:6], k.small[:, 2:4]))
                for t in range(TT):
                    k.then(dve, "dve", dve.tensor_scalar(nrm[:, t, :], src[:, t, :], k.small[:, 4 + t:5 + t], None,
                                                         ALU.mult))
                transpose_dve(k, dve, DC, gain, hi, lo)

            @block.tensor
            def _(pe):
                def ready(pe, s):
                    if s == 0:
                        pe.wait_ge(k.step["dve"], dve0 + 4)
                transpose_pe(k, pe, nrm, DC, ready)
    k.t_done += DC // 2


def split_transposed(k, src, chunks, gain, hi, lo, sp_work=None):
    with k.nc.Block() as block:
        @block.sync
        def _(sp):
            if sp_work:
                sp_work(sp)

        @block.scalar
        def _(act):
            transpose_act(k, act, chunks, gain, hi)

        @block.vector
        def _(dve):
            transpose_dve(k, dve, chunks, gain, hi, lo)

        @block.tensor
        def _(pe):
            transpose_pe(k, pe, src, chunks, lambda pe, s: None)
    k.t_done += chunks // 2


def narrow_split(k, act, dve, raw, hi, lo, landed):
    if act is not None:
        act.wait_ge(*landed)
        act.copy(hi[:], raw[:]).then_inc(k.narrow, 1)
    else:
        dve.wait_ge(k.narrow, k.narrow_done + 1)
        dve.tensor_tensor(lo[:], raw[:], hi[:].bitcast(F32), ALU.subtract).then_inc(k.narrow, 1)


def narrow_product(k, pe, hi, lo, w_hi, w_lo):
    pe.wait_ge(k.narrow, k.narrow_done + 2)
    for t in range(TT):
        acc = k.ps[:, 7, 16 * t:16 * t + 16]
        for c in range(DC):
            a, b = hi[:, c, t * P:(t + 1) * P], lo[:, c, t * P:(t + 1) * P]
            pe.matmul(acc, a, w_hi[:, c, :], start=(c == 0), stop=False)
            pe.matmul(acc, a, w_lo[:, c, :], start=False, stop=False)
            last = pe.matmul(acc, b, w_hi[:, c, :], start=False, stop=(c == DC - 1))
    last.then_inc(k.narrow, 1)


def sliding_window(k, proj, bias_rows, oa_hi, oa_lo):
    nc = k.nc
    G, HD, NG = 4, 64, 4
    scale = HD ** -0.5
    with ExitStack() as ctx:
        qT = k.sb("swa_qT", [HD, G, T], F32, ctx)
        kT = k.sb("swa_kT", [HD, T], F32, ctx)
        S = k.sb("swa_S", [P, G, 3 * P], F32, ctx)
        PT = k.sb("swa_PT", [P, 3 * G, P], F32, ctx)
        bias = k.sb("swa_bias", [P, 2, G, T], F32, ctx)
        bias_landed = [k.sem(f"swa_bias_landed{n}") for n in range(2)]
        st = k.sb("swa_st", [P, 6, 2 * G], F32, ctx)
        mx, neg, den, esk, rec, dif = (st[:, n, :] for n in range(6))
        qk_t, qk_c, sc_d, sb_d, ngm, ex_d, nm_d, pt_t, pt_c, ov_d, oh_d, ol_d = (
            k.sem(f"swa_{n}") for n in ("qk_transposed", "qk_copied", "scored", "biased", "neg_max", "exped",
                                        "normed", "p_transposed", "p_copied", "summed", "o_hi", "o_lo"))
        with nc.Block() as block:
            @block.sync
            def _(sp):
                for g in range(NG):
                    if g >= 2:
                        sp.wait_ge(nm_d, g - 1)
                    sp.dma_start(bias[:, g % 2], bass.AP(tensor=bias_rows, offset=G * g * 3 * P + P - 1,
                                                         ap=[[16 * 3 * P - 1, P], [3 * P, G], [1, T]]))\
                        .then_inc(bias_landed[g % 2], 16)

            @block.tensor
            def _(pe):
                ident = k.const(C_ID)
                for g in range(NG):
                    if g:
                        pe.wait_ge(pt_c, 2 * g)
                    for j in range(G):
                        for t in range(TT):
                            pe.transpose(k.ps[0:HD, j // 2, (j % 2) * T + t * P:(j % 2) * T + (t + 1) * P],
                                         proj[:, t, QA + (G * g + j) * HD:QA + (G * g + j + 1) * HD], ident)
                    for t in range(TT):
                        last = pe.transpose(k.ps[0:HD, 2, t * P:(t + 1) * P],
                                            proj[:, t, KA + g * HD:KA + (g + 1) * HD], ident)
                    last.then_inc(qk_t, 1)
                    pe.wait_ge(qk_c, 2 * (g + 1))
                    for j in range(G):
                        pe.matmul(k.ps[:, 3, j * P:(j + 1) * P], qT[:, j, 0:P], kT[:, 0:P], start=True, stop=True)
                    for j in range(G):
                        last = pe.matmul(k.ps[:, 4 + j // 2, (j % 2) * T:(j % 2 + 1) * T], qT[:, j, P:T], kT[:],
                                         start=True, stop=True)
                    last.then_inc(sc_d, 1)
                    pe.wait_ge(nm_d, g + 1)
                    for b in range(3):
                        for j in range(G):
                            last = pe.transpose(k.ps[:, b, j * P:(j + 1) * P], S[:, j, b * P:(b + 1) * P], ident)
                    last.then_inc(pt_t, 1)
                    pe.wait_ge(pt_c, 2 * (g + 1))
                    if g:
                        pe.wait_ge(ol_d, g)
                    for j in range(G):
                        at = HD * (j % 2)
                        for n, (b, kb) in enumerate(((0, 0), (1, 0), (2, 1))):
                            q = 0 if b == 0 else P
                            last = pe.matmul(k.ps[at:at + HD, 6, (j // 2) * T + q:(j // 2) * T + q + P],
                                             proj[:, kb, VA + g * HD:VA + (g + 1) * HD], PT[:, b * G + j, :],
                                             start=(b < 2), stop=(b != 1))
                    last.then_inc(ov_d, 1)

            @block.scalar
            def _(act):
                for g in range(NG):
                    act.wait_ge(qk_t, g + 1)
                    act.activation(qT[:], k.ps[0:HD, 0:2, :].rearrange("p b (j n) -> p (b j) n", j=2), ACT.Copy,
                                   scale=scale).then_inc(qk_c, 1)
                    act.copy(kT[:], k.ps[0:HD, 2, 0:T]).then_inc(qk_c, 1)
                    act.wait_ge(ngm, g + 1)
                    for b, (lo, hi) in enumerate(((0, P), (P, 3 * P))):
                        for j in range(G):
                            at = b * G + j
                            act.activation(S[:, j, lo:hi], S[:, j, lo:hi], ACT.Exp, bias=neg[:, at:at + 1],
                                           accum_out=den[:, at:at + 1])
                    act.activation(esk, dif, ACT.Exp).then_inc(ex_d, 1)
                    act.wait_ge(pt_t, g + 1)
                    act.copy(PT[:, 0:2 * G, :], k.ps[:, 0:2, :].rearrange("p b (j n) -> p (b j) n", j=G))\
                        .then_inc(pt_c, 1)
                    act.wait_ge(ov_d, g + 1)
                    act.copy(oa_hi[:, 2 * g:2 * g + 2, :], k.ps[:, 6, :].rearrange("p (c n) -> p c n", c=2))\
                        .then_inc(oh_d, 1)

            @block.vector
            def _(dve):
                for g in range(NG):
                    dve.wait_ge(bias_landed[g % 2], 16 * (g // 2 + 1))
                    dve.wait_ge(sc_d, g + 1)
                    if g:
                        dve.wait_ge(pt_t, g)
                    dve.tensor_tensor(S[:, :, 0:P], k.ps[:, 3, :].rearrange("p (j n) -> p j n", j=G),
                                      bias[:, g % 2, :, P:T], ALU.add)
                    k.then(dve, "dve", dve.tensor_tensor(
                        S[:, :, P:3 * P], k.ps[:, 4:6, :].rearrange("p b (j n) -> p (b j) n", j=2),
                        bias[:, g % 2], ALU.add))
                    dve.tensor_reduce(mx[:, 0:G], S[:, :, 0:P], AX.X, ALU.max)
                    k.then(dve, "dve", dve.tensor_reduce(mx[:, G:2 * G], S[:, :, P:3 * P], AX.X, ALU.max))
                    sink = k.col("sinks", G * g, G)
                    dve.tensor_tensor(mx[:, 0:G], mx[:, 0:G], sink, ALU.max)
                    k.then(dve, "dve", dve.tensor_tensor(mx[:, G:2 * G], mx[:, G:2 * G], sink, ALU.max))
                    dve.tensor_tensor(dif[:, 0:G], sink, mx[:, 0:G], ALU.subtract)
                    dve.tensor_tensor(dif[:, G:2 * G], sink, mx[:, G:2 * G], ALU.subtract)
                    dve.tensor_scalar(neg, mx, -1.0, None, ALU.mult).then_inc(ngm, 1)
                    dve.wait_ge(ex_d, g + 1)
                    k.then(dve, "dve", dve.tensor_tensor(den, den, esk, ALU.add))
                    k.then(dve, "dve", dve.reciprocal(rec, den))
                    for b, (lo, hi) in enumerate(((0, P), (P, 3 * P))):
                        for j in range(G):
                            at = b * G + j
                            last = dve.tensor_scalar(S[:, j, lo:hi], S[:, j, lo:hi], rec[:, at:at + 1], None,
                                                     ALU.mult)
                    last.then_inc(nm_d, 1)
                    dve.wait_ge(pt_t, g + 1)
                    dve.tensor_copy(PT[:, 2 * G:3 * G, :], k.ps[:, 2, :].rearrange("p (j n) -> p j n", j=G))\
                        .then_inc(pt_c, 1)
                    dve.wait_ge(oh_d, g + 1)
                    dve.tensor_tensor(oa_lo[:, 2 * g:2 * g + 2, :], k.ps[:, 6, :].rearrange("p (c n) -> p c n", c=2),
                                      oa_hi[:, 2 * g:2 * g + 2, :].bitcast(F32), ALU.subtract).then_inc(ol_d, 1)


def gated_linear(k, proj, og, gate_w, ob_hi, ob_lo, sp_work):
    nc = k.nc
    H, DV = 4, 256
    inv_tau = 1.0 / 16.0
    scale = float(P) ** -0.5
    with ExitStack() as ctx:
        gl = k.sb("gla_gl", [P, TT, 16], F32, ctx)
        glT = k.sb("gla_glT", [16, T], F32, ctx)
        la = at = proj[:, :, 0:H * P]
        ex = proj[:, :, H * P:2 * H * P]
        ks = proj[:, :, 2 * H * P:3 * H * P]
        y = proj[:, :, QB:VB]
        up = k.sb("gla_up", [P, H, T], F32, ctx)
        dn = k.sb("gla_dn", [P, H, T], F32, ctx)
        qd = k.sb("gla_qd", [P, H, T], F32, ctx)
        kd = dn
        state = k.sb("gla_state", [P, 3, H, DV], F32, ctx)
        st = k.sb("gla_st", [P, 3, TT * H], F32, ctx)
        names = ("gl_out", "gl_t", "gl_in", "z", "abs_done", "la", "b", "sfx", "exps", "qk", "decayed", "scored",
                 "masked", "grown", "state", "out", "squares", "root", "y")
        s = {n: k.sem(f"gla_{n}") for n in names}
        with nc.Block() as block:
            @block.sync
            def _(sp):
                sp_work(sp)

            @block.tensor
            def _(pe):
                pe.wait_ge(s["gl_out"], 1)
                for t in range(TT):
                    last = pe.transpose(k.ps[0:16, 6, t * P:(t + 1) * P], gl[:, t, :], k.const(C_ID))
                last.then_inc(s["gl_t"], 1)
                pe.wait_ge(s["gl_in"], 1)
                for t in range(TT):
                    pe.matmul(k.ps[:, t, :], glT[:, t * P:(t + 1) * P], gate_w[0:16, 0, :], start=True, stop=False)
                    last = pe.matmul(k.ps[:, t, :], k.consts[0:1, C_ONES, :], gate_w[0:1, 1, :], start=False, stop=True)
                last.then_inc(s["z"], 1)
                for base, bank in ((QB, 4), (KB, 6)):
                    for h in range(H):
                        for t in range(TT):
                            last = pe.transpose(k.ps[:, bank + h // 2, (h % 2) * T + t * P:(h % 2) * T + (t + 1) * P],
                                                proj[:, t, base + h * P:base + (h + 1) * P], k.const(C_ID))
                last.then_inc(s["qk"], 1)
                pe.wait_ge(s["la"], 1)
                for h in range(H):
                    for t in range(TT):
                        last = pe.matmul(k.ps[:, 2 + h // 2, (h % 2) * T + t * P:(h % 2) * T + (t + 1) * P],
                                         la[:, t, h * P:(h + 1) * P], k.const(C_CUM), start=True, stop=True)
                last.then_inc(s["b"], 1)
                for t in range(TT):
                    last = pe.matmul(k.ps[:, t, :], k.const(C_AFT), la[:, t, :], start=True, stop=True)
                last.then_inc(s["sfx"], 1)
                pe.wait_ge(s["decayed"], 1)
                for t in range(TT):
                    for h in range(H):
                        last = pe.matmul(k.ps[:, 2 + t, h * P:(h + 1) * P], kd[:, h, t * P:(t + 1) * P],
                                         qd[:, h, t * P:(t + 1) * P], start=True, stop=True)
                last.then_inc(s["scored"], 1)
                pe.wait_ge(s["decayed"], 2)
                for c in range(3):
                    t, p = c // 2, CH * (c % 2)
                    for h in range(H):
                        last = pe.matmul(k.ps[:, (4 + 2 * c) % 8 + h // 2, (h % 2) * DV:(h % 2 + 1) * DV],
                                         ks[p:p + CH, t, h * P:(h + 1) * P],
                                         proj[p:p + CH, t, VB + h * DV:VB + (h + 1) * DV], start=True, stop=True)
                    last.then_inc(s["grown"], 1)
                pe.wait_ge(s["masked"], 1)
                pe.wait_ge(s["state"], 3)
                for t in range(TT):
                    for h in range(H):
                        bank, lo = 2 + 2 * t + h // 2, (h % 2) * DV
                        for c in range(2 * t, 2 * t + 2):
                            p = CH * (c % 2)
                            last = pe.matmul(k.ps[p:p + CH, bank, lo:lo + DV], at[:, t, h * P + p:h * P + p + CH],
                                             proj[:, t, VB + h * DV:VB + (h + 1) * DV], start=True, stop=(c == 0))
                            if c:
                                last = pe.matmul(k.ps[p:p + CH, bank, lo:lo + DV], qd[:, h, c * CH:(c + 1) * CH],
                                                 state[:, c - 1, h, :], start=False, stop=True)
                last.then_inc(s["out"], 1)

            @block.scalar
            def _(act):
                act.wait_ge(k.narrow, k.narrow_done + 3)
                act.copy(gl[:], k.ps[:, 7, 0:32].rearrange("p (t n) -> p t n", t=TT)).then_inc(s["gl_out"], 1)
                act.wait_ge(s["gl_t"], 1)
                act.copy(glT[:], k.ps[0:16, 6, 0:T]).then_inc(s["gl_in"], 1)
                act.wait_ge(s["z"], 1)
                k.then(act, "act", act.activation(ex, k.ps[:, 0:2, :], ACT.Abs))
                k.then(act, "act", act.activation(ex, ex, ACT.Exp, scale=-1.0))
                act.activation(ex, ex, ACT.Ln, bias=1.0).then_inc(s["abs_done"], 1)
                act.wait_ge(s["b"], 1)
                b = k.ps[:, 2:4, :].rearrange("p b (j n) -> p (b j) n", j=2)
                act.activation(up[:], b, ACT.Exp, scale=inv_tau)
                act.activation(dn[:], b, ACT.Exp, scale=-inv_tau).then_inc(s["exps"], 1)
                act.wait_ge(s["sfx"], 1)
                act.wait_ge(s["la"], 1)
                act.activation(ex, k.ps[:, 0:2, :], ACT.Exp, scale=inv_tau).then_inc(s["exps"], 1)
                act.wait_ge(s["out"], 1)
                for t in range(TT):
                    for h in range(H):
                        last = act.activation(y[:, t, h * DV:(h + 1) * DV],
                                              k.ps[:, 2 + 2 * t + h // 2, (h % 2) * DV:(h % 2 + 1) * DV], ACT.Square,
                                              accum_out=st[:, 0, t * H + h:t * H + h + 1])
                last.then_inc(s["squares"], 1)
                act.wait_ge(s["root"], 1)
                act.activation(st[:, 1, :], st[:, 1, :], ACT.Sqrt).then_inc(s["root"], 1)

            @block.vector
            def _(dve):
                dve.wait_ge(s["abs_done"], 1)
                for t in range(TT):
                    last = dve.scalar_tensor_tensor(la[:, t, :], k.ps[:, t, :], 0.0, ex[:, t, :], ALU.min, ALU.subtract)
                last.then_inc(s["la"], 1)
                dve.wait_ge(s["qk"], 1)
                dve.wait_ge(s["exps"], 1)
                for b in range(2):
                    for j in range(2):
                        dve.scalar_tensor_tensor(qd[:, 2 * b + j, :], k.ps[:, 4 + b, j * T:(j + 1) * T], scale,
                                                 up[:, 2 * b + j, :], ALU.mult, ALU.mult)
                last = dve.tensor_tensor(kd[:], k.ps[:, 6:8, :].rearrange("p b (j n) -> p (b j) n", j=2), dn[:],
                                         ALU.mult)
                last.then_inc(s["decayed"], 1)
                dve.wait_ge(s["exps"], 2)
                dve.tensor_tensor(ks, proj[:, :, KB:KB + H * P], ex, ALU.mult).then_inc(s["decayed"], 1)
                dve.wait_ge(s["scored"], 1)
                k.then(dve, "dve", dve.tensor_scalar(at, k.ps[:, 2:4, :],
                                                     BIG, -BIG, ALU.min, ALU.max))
                for t in range(TT):
                    for h in range(H):
                        one = at[:, t, h * P:(h + 1) * P]
                        last = dve.tensor_tensor(one, one, k.const(C_CUM), ALU.mult)
                last.then_inc(s["masked"], 1)
                for c in range(3):
                    dve.wait_ge(s["grown"], c + 1)
                    grown = k.ps[:, (4 + 2 * c) % 8:(4 + 2 * c) % 8 + 2, :].rearrange("p b (j n) -> p (b j) n", j=2)
                    if c == 0:
                        dve.tensor_copy(state[:, 0, :, :], grown).then_inc(s["state"], 1)
                    else:
                        dve.wait_ge(s["state"], c)
                        for h in range(H):
                            last = dve.scalar_tensor_tensor(
                                state[:, c, h, :], state[:, c - 1, h, :], up[:, h, CH * (c + 1) - 1:CH * (c + 1)],
                                grown[:, h, :], ALU.mult, ALU.add)
                        last.then_inc(s["state"], 1)
                dve.wait_ge(s["squares"], 1)
                dve.tensor_scalar(st[:, 1, :], st[:, 0, :], 1.0 / DV, EPS, ALU.mult, ALU.add).then_inc(s["root"], 1)
                dve.wait_ge(s["root"], 2)
                k.then(dve, "dve", dve.reciprocal(st[:, 2, :], st[:, 1, :]))
                for t in range(TT):
                    for h in range(H):
                        last = dve.scalar_tensor_tensor(
                            y[:, t, h * DV:(h + 1) * DV],
                            k.ps[:, 2 + 2 * t + h // 2, (h % 2) * DV:(h % 2 + 1) * DV],
                            st[:, 2, t * H + h:t * H + h + 1], og[:, t, h * DV:(h + 1) * DV], ALU.mult, ALU.mult)
                k.then(dve, "dve", last)
        k.narrow_done += 3
        split_transposed(k, y, H * DV // P, lambda c: k.col("g_gla", c % 2), ob_hi, ob_lo)


def norm_rows(k, name, gain, landed, dst):
    nc = k.nc
    with ExitStack() as ctx:
        junk = k.sb(f"{name}_sq", [P, TT, D], F32, ctx)
        act0, dve0 = k.steps["act"], k.steps["dve"]
        with nc.Block() as block:
            @block.scalar
            def _(act):
                for t in range(TT):
                    last = act.activation(junk[:, t, :], k.h[:, t, :], ACT.Square, accum_out=k.small[:, t:t + 1])
                k.steps["act"] += 1
                last.then_inc(k.step["act"], 1)
                act.wait_ge(k.step["dve"], dve0 + 1)
                act.activation(k.small[:, 2:4], k.small[:, 2:4], ACT.Sqrt).then_inc(k.step["act"], 1)
                k.steps["act"] += 1

            @block.vector
            def _(dve):
                dve.wait_ge(k.step["act"], act0 + 1)
                k.then(dve, "dve", dve.tensor_scalar(k.small[:, 2:4], k.small[:, 0:2], 1.0 / D, EPS, ALU.mult, ALU.add))
                dve.wait_ge(k.step["act"], act0 + 2)
                k.then(dve, "dve", dve.reciprocal(k.small[:, 4:6], k.small[:, 2:4]))
                dve.wait_ge(*landed)
                for t in range(TT):
                    k.then(dve, "dve", dve.scalar_tensor_tensor(dst[:, t, :], k.h[:, t, :], k.small[:, 4 + t:5 + t],
                                                                gain[:], ALU.mult, ALU.mult))


def start(k, ctx, x, consts, cols, rel, onehot, rows, bias_rows, first_tiles, w_low, low_raw,
          low_landed):
    nc = k.nc
    s_rel = k.sem("rel_landed")
    s_neg = k.sem("rel_masked")
    s_tab = k.sem("bias_table")
    s_row = k.sem("bias_rows_stored")
    H, N = 16, 3 * P
    bias_row = nc.dram_tensor("bias_row", [H, N], F32, kind="Internal")
    with ExitStack() as tmp:
        relx = k.sb("relx", [33, H], F32, tmp)
        oh = k.sb("onehot_sb", [33, N], F32, tmp)
        table = k.sb("bias_table_sb", [H, N], F32, tmp)
        with nc.Block() as block:
            @block.sync
            def _(sp):
                sp.dma_start(k.h[:], x.rearrange("b (t p) d -> p (b t) d", p=P)).then_inc(k.landed, 16)
                sp.dma_start(k.ident[:], consts[:, C_ID, :]).then_inc(k.landed, 16)
                sp.dma_start(k.consts[:], consts).then_inc(k.landed, 16)
                sp.dma_start(k.cols[:], cols).then_inc(k.landed, 16)
                prefetch(k, sp, first_tiles, 0)
                sp.dma_start(relx[0:32, :], rel).then_inc(s_rel, 16)
                sp.dma_start(oh[:], onehot).then_inc(s_rel, 16)
                sp.dma_start(low_raw[:], w_low.rearrange("(c p) n -> p c n", p=P)).then_inc(low_landed, 16)
                for dst, src in rows:
                    sp.dma_start(dst, src).then_inc(k.landed, 16)
                sp.wait_ge(s_tab, 2)
                sp.dma_start(bias_row.ap(), table[:]).then_inc(s_row, 16)
                sp.wait_ge(s_row, 16)
                sp.dma_start(bias_rows.ap(), bass.AP(tensor=bias_row, offset=0, ap=[[0, P], [1, H * N]]))\
                    .then_inc(s_row, 16)
                sp.wait_ge(s_row, 32)
                sp.wait_ge(k.landed, 16 * (4 + len(rows)))

            @block.vector
            def _(dve):
                dve.memset(k.small[:, 0:1], 0.0).then_inc(k.unit_used, SLOTS)
                dve.memset(k.small[:, 1:2], 0.0).then_inc(k.act_free, 2)
                dve.memset(k.small[:, 2:3], 0.0).then_inc(k.dve_free, 2)
                dve.memset(relx[32:33, :], NEG).then_inc(s_neg, 1)

            @block.tensor
            def _(pe):
                pe.wait_ge(s_rel, 32)
                pe.wait_ge(s_neg, 1)
                pe.matmul(k.ps[0:H, 7, 0:N], relx[:], oh[:], start=True, stop=True).then_inc(s_tab, 1)

            @block.scalar
            def _(act):
                act.wait_ge(s_tab, 1)
                act.copy(table[:], k.ps[0:H, 7, 0:N]).then_inc(s_tab, 1)


def add_to_stream(k):
    def dve_evac_at(col):
        def dve_evac(dve, m, i, bank):
            for t in range(TT):
                at = k.h[:, t, bass.ds(col(m, i), NT)]
                last = dve.tensor_tensor(at, at, k.ps[:, bank + t, :], ALU.add)
            return last
        return dve_evac
    return dve_evac_at


def no_evac(eng, m, i, bank):
    return None


def copy_evacs(dst, col):
    def act_evac(act, m, i, bank, ps):
        return act.copy(dst[:, 0, bass.ds(col(m, i), NT)], ps[:, bank, :])

    def dve_evac(dve, m, i, bank, ps):
        return dve.tensor_copy(dst[:, 1, bass.ds(col(m, i), NT)], ps[:, bank + 1, :])
    return act_evac, dve_evac


def ffn1_tiles(w_gate, w_up, hi, lo):
    return [Tile(w_gate, DC, lambda i: i * NT, hi, lo), Tile(w_up, DC, lambda i: i * NT, hi, lo)]


def down_tiles(w_down, hi, lo):
    return [Tile(w_down, HC, lambda i, m=m: i * (2 * NT) + m * NT, hi, lo) for m in range(2)]


def square_tiles(w, chunks, hi, lo):
    return [Tile(w, chunks, lambda i, m=m: i * (2 * NT) + m * NT, hi, lo) for m in range(2)]


def stream_col(m, i):
    return i * (2 * NT) + m * NT


def hidden_transposed(k, hid, hT_hi, hT_lo, t0, hid_ready):
    def pe_hook(pe, i):
        hid_ready(pe, i)
        pe.wait_ge(k.tp_lo, t0 + 2 * i)
        for s in range(2):
            for c in range(2):
                for t in range(TT):
                    at = (2 * s + c) * P
                    last = pe.transpose(k.ps[:, 4 + s, c * T + t * P:c * T + (t + 1) * P], hid[:, t, at:at + P],
                                        k.const(C_ID))
            last.then_inc(k.tp_done, 1)

    def at(i, s):
        return bass.ds(i * (4 * T) + s * 2 * T, 2 * T)

    def act_hook(act, i):
        for s in range(2):
            act.wait_ge(k.tp_done, t0 + 1 + s + 2 * i)
            act.copy(hT_hi.rearrange("p c n -> p (c n)")[:, at(i, s)], k.ps[:, 4 + s, :]).then_inc(k.tp_hi, 1)

    def dve_hook(dve, i):
        for s in range(2):
            dve.wait_ge(k.tp_hi, t0 + 1 + s + 2 * i)
            dve.tensor_tensor(hT_lo.rearrange("p c n -> p (c n)")[:, at(i, s)], k.ps[:, 4 + s, :],
                              hT_hi.rearrange("p c n -> p (c n)")[:, at(i, s)].bitcast(F32), ALU.subtract)\
                .then_inc(k.tp_lo, 1)
    return pe_hook, act_hook, dve_hook


def first_block(k, a, hi, lo, next_tiles, next_loads, stop=None):
    nc = k.nc
    w_in = a["w_in"]
    head = [Tile(w_in, DC, lambda i: QA, hi, lo), Tile(w_in, DC, lambda i: OG, hi, lo),
            Tile(w_in, DC, lambda i: OG + NT, hi, lo)]
    body = [Tile(w_in, DC, lambda i, m=m: NT + i * (2 * NT) + m * NT, hi, lo) for m in range(2)]
    with ExitStack() as life:
        og = k.sb("og", [P, TT, 1024], F32, life)
        oa = [k.sb(f"oa_{n}", [P, 8, T], F32R, life) for n in ("hi", "lo")]
        ob = [k.sb(f"ob_{n}", [P, 8, T], F32R, life) for n in ("hi", "lo")]
        merge = [Tile(w_in, DC, lambda i: GA + i * NT, hi, lo), Tile(w_in, DC, lambda i: GB + i * NT, hi, lo),
                 Tile(a["w_proj_a"], 8, lambda i: i * NT, *oa), Tile(a["w_proj_b"], 8, lambda i: i * NT, *ob)]
        out_tiles = square_tiles(a["w_out"], DC, hi, lo)
        ffn_tiles = ffn1_tiles(a["w_ffn_gate"], a["w_ffn_up"], hi, lo)
        with ExitStack() as mid:
            proj = k.sb("proj", [P, TT, GL], F32, mid)
            gate_w = k.sb("gate_w", [16, 2, 512], F32, mid)
            low = [k.sb(f"low_{n}", [P, DC, 16], d, mid) for n, d in (("raw", F32), ("hi", F32R), ("lo", F32R))]
            low_landed = k.sem("low_landed")
            with ExitStack() as swa:
                bias_rows = nc.dram_tensor("bias_rows", [P, 16 * 3 * P], F32, kind="Internal")
                start(k, swa, a["x"], a["consts"], a["cols"], a["rel_bias"], a["onehot"],
                      [(gate_w[:, 0, :], a["w_gate_up"]), (gate_w[0:1, 1, :], a["b_gate"])],
                      bias_rows, head, w_in[:, GL:OG], low[0], low_landed)
                norm_transposed(k, k.h, lambda c: k.col("g_mix", c), hi, lo,
                                nrm=proj[:, :, 0:D])

                def act_evac(act, m, i, bank):
                    if m == 0:
                        return act.copy(proj[:, 0, 0:NT], k.ps[:, bank, :])
                    for t in range(TT):
                        last = act.activation(og[:, t, (m - 1) * NT:m * NT], k.ps[:, bank + t, :], ACT.Silu)
                    return last

                def dve_evac(dve, m, i, bank):
                    return dve.tensor_copy(proj[:, 1, 0:NT], k.ps[:, bank + 1, :]) if m == 0 else None
                product(k, "head", head, 1, act_evac, dve_evac, after=body)

                ae, de = copy_evacs(proj, lambda m, i: NT + i * (2 * NT) + m * NT)
                product(k, "qkv", body, 3, lambda e, m, i, b: ae(e, m, i, b, k.ps),
                        lambda e, m, i, b: de(e, m, i, b, k.ps),
                        act_last=lambda act: narrow_split(k, act, None, *low, (low_landed, 16)),
                        dve_last=lambda dve: narrow_split(k, None, dve, *low, None),
                        pe_last=lambda pe: narrow_product(k, pe, hi, lo, low[1], low[2]))
                sliding_window(k, proj, bias_rows, *oa)
            if stop == "swa":
                return
            gated_linear(k, proj, og, gate_w, *ob, lambda sp: prefetch(k, sp, merge, k.unit))
        if stop == "gla":
            return
        with ExitStack() as mid:
            merged = k.sb("merged", [P, TT, D], F32, mid)
            sg = k.sb("gates", [P, 2, TT, NT], F32, mid)
            term = k.sb("term", [P, TT, NT], F32, mid)
            term_done = k.sem("merge_term")
            tb = k.tile

            def act_evac(act, m, i, bank):
                if m > 1:
                    return None
                act.wait_ge(k.dve_free, tb + m + 1 + 4 * i)
                return act.activation(sg[:, m, :, :], k.ps[:, bank:bank + 2, :], ACT.Sigmoid)

            def dve_evac(dve, m, i, bank):
                if m < 2:
                    return None
                dve.wait_ge(k.act_free, 2 + tb + m - 1 + 4 * i)
                acc = k.ps[:, bank:bank + 2, :]
                at = merged[:, :, bass.ds(i * NT, NT)]
                if m == 2:
                    return dve.tensor_tensor(at, acc, sg[:, 0, :, :], ALU.mult)
                dve.tensor_tensor(term[:], acc, sg[:, 1, :, :], ALU.mult).then_inc(term_done, 1)
                dve.wait_ge(term_done, 1 + i)
                dve.wait_ge(k.dve_free, 2 + tb + 3 + 4 * i)
                return dve.tensor_tensor(at, at, term[:], ALU.add)
            product(k, "merge", merge, 4, act_evac, dve_evac, after=out_tiles)
            split_transposed(k, merged, DC, lambda c: 1.0, hi, lo)
    add = add_to_stream(k)
    product(k, "out", out_tiles, 2, no_evac, add(stream_col), after=ffn_tiles)
    if stop == "mix":
        return
    norm_transposed(k, k.h, lambda c: k.col("g_ffn", c), hi, lo)
    with ExitStack() as life:
        hT = [k.sb(f"hT_{n}", [P, HC, T], F32R, life) for n in ("hi", "lo")]
        down = down_tiles(a["w_ffn_down"], *hT)
        with ExitStack() as mid:
            hid = k.sb("hid", [P, TT, NT], F32, mid)
            sg = k.sb("ffn_silu", [P, TT, NT], F32, mid)
            tb, t0 = k.tile, k.t_done

            def act_evac(act, m, i, bank):
                if m:
                    return None
                act.wait_ge(k.dve_free, tb + 2 + 2 * i)
                return act.activation(sg[:], k.ps[:, bank:bank + 2, :], ACT.Silu)

            def dve_evac(dve, m, i, bank):
                if m == 0:
                    return None
                dve.wait_ge(k.act_free, 2 + tb + 1 + 2 * i)
                dve.wait_ge(k.tp_done, t0 + 2 * i)
                return dve.tensor_tensor(hid[:], k.ps[:, bank:bank + 2, :], sg[:], ALU.mult)
            pe_hook, act_hook, dve_hook = hidden_transposed(
                k, hid, *hT, t0, lambda pe, i: pe.wait_ge(k.dve_free, 2 + tb + 2 + 2 * i))
            product(k, "ffn", ffn_tiles, FF1 // NT, act_evac, dve_evac, after=down,
                    hooks=[("pe", 5, pe_hook), ("act", 7, act_hook), ("dve", 8, dve_hook)])
            k.t_done += 2 * (FF1 // NT)
        product(k, "down", down, 2, no_evac, add(stream_col), after=next_tiles)
    with ExitStack() as mid:
        gain = k.sb("gain_final1", [P, D], F32, mid)
        s_gain = k.sem("gain_final1_landed")
        with nc.Block() as block:
            @block.sync
            def _(sp):
                sp.dma_start(gain[:], a["g_final1"]).then_inc(s_gain, 16)
        norm_rows(k, "final1", gain, (s_gain, 16), k.h)


SQ, SK, SV, GQ, GK, GV, GZ, GBA = (1024 * n for n in range(8))
HEADS2 = 8


def stick_breaking(k, proj, hi, lo, sp_work):
    nc = k.nc
    G, W = 4, T + P
    scale = float(P) ** -0.5
    names = ("qk", "qT", "kT", "z", "log", "stay", "later", "exponent", "exp", "weights", "out", "hi", "lo")
    s = {n: k.sem(f"stick_{n}") for n in names}
    with ExitStack() as ctx:
        qT = k.sb("stick_qT", [P, G, T], F32, ctx)
        kT = k.sb("stick_kT", [P, G, T], F32, ctx)
        ln = k.sb("stick_ln", [P, G, W], F32, ctx)
        lb = k.sb("stick_lb", [P, G, W], F32, ctx)
        st = k.sb("stick_st", [P, G, W], F32, ctx)
        z0 = k.ps[:, 4:6, :].rearrange("p b (j n) -> p (b j) n", j=2)
        z1 = k.ps[:, 6, :].rearrange("p (j n) -> p j n", j=G)
        before = k.const(C_BEFALL)
        with nc.Block() as block:
            @block.sync
            def _(sp):
                sp_work(sp)

            @block.tensor
            def _(pe):
                for g in range(HEADS2 // G):
                    if g:
                        pe.wait_ge(s["lo"], g)
                    for bank, base in ((0, SQ), (2, SK)):
                        for j in range(G):
                            for t in range(TT):
                                last = pe.transpose(
                                    k.ps[:, bank + j // 2, (j % 2) * T + t * P:(j % 2) * T + (t + 1) * P],
                                    proj[:, t, base + (G * g + j) * P:base + (G * g + j + 1) * P], k.const(C_ID))
                    last.then_inc(s["qk"], 1)
                    pe.wait_ge(s["qT"], g + 1)
                    pe.wait_ge(s["kT"], g + 1)
                    for j in range(G):
                        pe.matmul(z0[:, j, :], kT[:, j, 0:P], qT[:, j, :], start=True, stop=True)
                    for j in range(G):
                        last = pe.matmul(z1[:, j, :], kT[:, j, P:T], qT[:, j, P:T], start=True, stop=True)
                    last.then_inc(s["z"], 1)
                    pe.wait_ge(s["stay"], g + 1)
                    for j in range(G):
                        pe.matmul(z0[:, j, 0:P], k.const(C_AFTALL), st[:, j, 0:P], start=True, stop=True)
                        pe.matmul(z0[:, j, P:T], k.const(C_AFTALL), st[:, j, P:T], start=True, stop=False)
                        pe.matmul(z0[:, j, P:T], k.const(C_ONES), st[:, j, T:W], start=False, stop=True)
                    for j in range(G):
                        last = pe.matmul(z1[:, j, :], k.const(C_AFTALL), st[:, j, T:W], start=True, stop=True)
                    last.then_inc(s["later"], 1)
                    pe.wait_ge(s["weights"], g + 1)
                    for j in range(G):
                        v = [proj[:, t, SV + (G * g + j) * P:SV + (G * g + j + 1) * P] for t in range(TT)]
                        bank, at = j // 2, (j % 2) * T
                        pe.matmul(k.ps[:, bank, at:at + P], v[0], lb[:, j, 0:P], start=True, stop=True)
                        pe.matmul(k.ps[:, bank, at + P:at + T], v[0], lb[:, j, P:T], start=True, stop=False)
                        last = pe.matmul(k.ps[:, bank, at + P:at + T], v[1], lb[:, j, T:W], start=False, stop=True)
                    last.then_inc(s["out"], 1)

            @block.scalar
            def _(act):
                for g in range(HEADS2 // G):
                    act.wait_ge(s["qk"], g + 1)
                    act.activation(qT[:], k.ps[:, 0:2, :].rearrange("p b (j n) -> p (b j) n", j=2), ACT.Copy,
                                   scale=scale).then_inc(s["qT"], 1)
                    act.wait_ge(s["z"], g + 1)
                    if g:
                        act.wait_ge(s["stay"], g)
                    act.activation(ln[:, :, 0:T], z0, ACT.Abs)
                    k.then(act, "act", act.activation(ln[:, :, T:W], z1, ACT.Abs))
                    k.then(act, "act", act.activation(ln[:], ln[:], ACT.Exp, scale=-1.0))
                    act.activation(ln[:], ln[:], ACT.Ln, bias=1.0).then_inc(s["log"], 1)
                    act.wait_ge(s["exponent"], g + 1)
                    act.activation(lb[:], lb[:], ACT.Exp).then_inc(s["exp"], 1)
                    act.wait_ge(s["out"], g + 1)
                    act.copy(hi[:, G * g:G * (g + 1), :], k.ps[:, 0:2, :].rearrange("p b (j n) -> p (b j) n", j=2))\
                        .then_inc(s["hi"], 1)

            @block.vector
            def _(dve):
                for g in range(HEADS2 // G):
                    dve.wait_ge(s["qk"], g + 1)
                    dve.tensor_copy(kT[:], k.ps[:, 2:4, :].rearrange("p b (j n) -> p (b j) n", j=2))\
                        .then_inc(s["kT"], 1)
                    dve.wait_ge(s["log"], g + 1)
                    if g:
                        dve.wait_ge(s["out"], g)
                    for z, a, b in ((z0, 0, T), (z1, T, W)):
                        dve.scalar_tensor_tensor(st[:, :, a:b], z, 0.0, ln[:, :, a:b], ALU.max, ALU.add)
                        last = dve.scalar_tensor_tensor(lb[:, :, a:b], z, 0.0, ln[:, :, a:b], ALU.min, ALU.subtract)
                    k.then(dve, "dve", last)
                    for j in range(G):
                        for a in (0, T):
                            last = dve.tensor_tensor(st[:, j, a:a + P], st[:, j, a:a + P], before, ALU.mult)
                    last.then_inc(s["stay"], 1)
                    dve.wait_ge(s["later"], g + 1)
                    dve.tensor_tensor(lb[:, :, 0:T], lb[:, :, 0:T], z0, ALU.subtract)
                    dve.tensor_tensor(lb[:, :, T:W], lb[:, :, T:W], z1, ALU.subtract).then_inc(s["exponent"], 1)
                    dve.wait_ge(s["exp"], g + 1)
                    for j in range(G):
                        for a in (0, T):
                            last = dve.tensor_tensor(lb[:, j, a:a + P], lb[:, j, a:a + P], before, ALU.mult)
                    last.then_inc(s["weights"], 1)
                    dve.wait_ge(s["hi"], g + 1)
                    dve.tensor_tensor(lo[:, G * g:G * (g + 1), :],
                                      k.ps[:, 0:2, :].rearrange("p b (j n) -> p (b j) n", j=2),
                                      hi[:, G * g:G * (g + 1), :].bitcast(F32), ALU.subtract).then_inc(s["lo"], 1)


def delta_inputs(k, proj, slab, sc, s):
    nc = k.nc
    H = HEADS2
    S0, S1, S2, S3, S4, S5 = (proj[:, :, 1024 * n:1024 * (n + 1)] for n in range(6))
    khat, vbeta, khatT, kbe, A = slab

    def head(x, h, a=0, b=T):
        return x[:, h // 4, (h % 4) * T + a:(h % 4) * T + b]

    with nc.Block() as block:
        @block.tensor
        def _(pe):
            for c in range(12):
                if c >= 4:
                    pe.wait_ge(s["taps"], c - 3)
                for j in range(2):
                    for t in range(TT):
                        last = pe.transpose(k.ps[:, c % 4, j * T + t * P:j * T + (t + 1) * P],
                                            proj[:, t, GQ + (2 * c + j) * P:GQ + (2 * c + j + 1) * P], k.const(C_ID))
                last.then_inc(s["channels"], 1)
            pe.wait_ge(s["squares"], 1)
            for n, x in enumerate((S3, S4)):
                for h in range(H):
                    for t in range(TT):
                        at = n * 16 + t * H + h
                        last = pe.matmul(k.ps[:, 4, at:at + 1], head(x, h, t * P, (t + 1) * P),
                                         k.consts[:, C_ONES, 0:1], start=True, stop=True)
            last.then_inc(s["sums"], 1)
            pe.wait_ge(s["silu"], 2)
            for x, banks in ((S1, (0, 1, 2, 3)), (S2, (5, 6, 7, 0))):
                for n, bank in enumerate(banks):
                    if x is S2 and bank == 0:
                        pe.wait_ge(s["khat"], 1)
                    t, q = n // 2, n % 2
                    for j in range(4):
                        last = pe.transpose(k.ps[:, bank, j * P:(j + 1) * P], head(x, 4 * q + j, t * P, (t + 1) * P),
                                            k.const(C_ID))
                    last.then_inc(s["rows"], 1)
            pe.wait_ge(s["g"], 1)
            pe.wait_ge(s["sums2"], 1)
            for t in range(TT):
                pe.matmul(k.ps[:, 4, 64 + 8 * t:72 + 8 * t], k.const(C_CUM), sc["g"][:, t, :], start=True, stop=True)
                pe.matmul(k.ps[:, 4, 80 + 8 * t:88 + 8 * t], k.const(C_AFT), sc["g"][:, t, :], start=True, stop=True)
            for c in range(4):
                last = pe.matmul(k.ps[:, 4, 96 + 8 * c:104 + 8 * c], k.const(C_HALF + c % 2), sc["g"][:, c // 2, :],
                                 start=True, stop=True)
            last.then_inc(s["gsums"], 1)
            pe.wait_ge(s["khat"], 4)
            for n in range(4):
                if n == 0:
                    pe.wait_ge(s["vbeta"], 4)
                for j in range(2):
                    for t in range(TT):
                        h = 2 * n + j
                        last = pe.transpose(k.ps[:, n, j * T + t * P:j * T + (t + 1) * P],
                                            khat[:, t, h * P:(h + 1) * P], k.const(C_ID))
            last.then_inc(s["khatT"], 1)

        @block.scalar
        def _(act):
            act.wait_ge(k.narrow, k.narrow_done + 3)
            ba = k.ps[:, 7, 0:32].rearrange("p (t n) -> p t n", t=TT)
            act.activation(sc["beta"], ba[:, :, 0:8], ACT.Sigmoid).then_inc(s["beta"], 1)
            act.wait_ge(s["x"], 1)
            k.then(act, "act", act.activation(sc["ln"], sc["x"], ACT.Abs))
            k.then(act, "act", act.activation(sc["ln"], sc["ln"], ACT.Exp, scale=-1.0))
            act.activation(sc["ln"], sc["ln"], ACT.Ln, bias=1.0)
            act.activation(sc["ea"], k.col("alog", 0, 8), ACT.Exp).then_inc(s["x"], 1)
            for c in range(12):
                act.wait_ge(s["channels"], c + 1)
                for j in range(2):
                    n = 2 * c + j
                    last = act.activation(head((S0, S1, S2)[n // 8], n % 8), k.ps[:, c % 4, j * T:(j + 1) * T],
                                          ACT.Copy, scale=k.col("conv", 4 * n + 3))
                last.then_inc(s["tap0"], 1)
            act.wait_ge(s["taps"], 12)
            act.activation(S0, S0, ACT.Silu)
            act.activation(S1, S1, ACT.Silu).then_inc(s["silu"], 1)
            act.activation(S2, S2, ACT.Silu).then_inc(s["silu"], 1)
            act.activation(proj[:, :, GZ:GZ + 1024], proj[:, :, GZ:GZ + 1024], ACT.Silu)
            act.wait_ge(s["silu"], 1)
            act.activation(S3, S0, ACT.Square)
            act.activation(S4, S1, ACT.Square).then_inc(s["squares"], 1)
            act.wait_ge(s["sums2"], 1)
            act.activation(sc["norms"], sc["norms"], ACT.Sqrt).then_inc(s["sums2"], 1)
            act.wait_ge(s["gsums"], 1)
            act.activation(sc["exps"], k.ps[:, 4, 64:128], ACT.Exp).then_inc(s["exps"], 1)
            for n in range(4):
                act.wait_ge(s["rows"], 5 + n)
                t, q = n // 2, n % 2
                for j in range(4):
                    h = 4 * q + j
                    last = act.activation(vbeta[:, t, h * P:(h + 1) * P],
                                          k.ps[:, (5, 6, 7, 0)[n], j * P:(j + 1) * P], ACT.Copy,
                                          scale=sc["beta"][:, t, h:h + 1])
                last.then_inc(s["vbeta"], 1)
            act.wait_ge(s["khatT"], 1)
            for n in range(4):
                last = act.copy(khatT[:, n // 2, (n % 2) * 2 * T:(n % 2 + 1) * 2 * T], k.ps[:, n, :])
            last.then_inc(s["ready"], 1)

        @block.vector
        def _(dve):
            dve.wait_ge(k.narrow, k.narrow_done + 3)
            dve.wait_ge(s["beta"], 1)
            ba = k.ps[:, 7, 0:32].rearrange("p (t n) -> p t n", t=TT)
            for t in range(TT):
                last = dve.tensor_tensor(sc["x"][:, t, :], ba[:, t, 8:16], k.col("dtb", 0, 8), ALU.add)
            last.then_inc(s["x"], 1)
            dve.wait_ge(s["x"], 2)
            k.then(dve, "dve", dve.scalar_tensor_tensor(sc["x"], sc["x"], 0.0, sc["ln"], ALU.max, ALU.add))
            for t in range(TT):
                last = dve.scalar_tensor_tensor(sc["g"][:, t, :], sc["x"][:, t, :], -1.0, sc["ea"], ALU.mult, ALU.mult)
            last.then_inc(s["g"], 1)
            for c in range(12):
                dve.wait_ge(s["tap0"], c + 1)
                for tap in range(1, 4):
                    for j in range(2):
                        n = 2 * c + j
                        y = head((S0, S1, S2)[n // 8], n % 8, tap, T)
                        last = dve.scalar_tensor_tensor(y, k.ps[:, c % 4, j * T:(j + 1) * T - tap],
                                                        k.col("conv", 4 * n + 3 - tap), y, ALU.mult, ALU.add)
                    if tap < 3:
                        k.then(dve, "dve", last)
                last.then_inc(s["taps"], 1)
            dve.wait_ge(s["sums"], 1)
            dve.tensor_scalar(sc["norms"], k.ps[:, 4, 0:32], EPS, None, ALU.add).then_inc(s["sums2"], 1)
            dve.wait_ge(s["sums2"], 2)
            k.then(dve, "dve", dve.reciprocal(sc["rnorms"], sc["norms"]))
            for n in range(4):
                dve.wait_ge(s["rows"], n + 1)
                t, q = n // 2, n % 2
                for j in range(4):
                    h = 4 * q + j
                    last = dve.tensor_scalar(khat[:, t, h * P:(h + 1) * P], k.ps[:, n, j * P:(j + 1) * P],
                                             sc["rnorms"][:, 16 + t * H + h:17 + t * H + h], None, ALU.mult)
                last.then_inc(s["khat"], 1)
            dve.wait_ge(s["exps"], 1)
            dve.wait_ge(s["beta"], 1)
            dve.wait_ge(s["khat"], 4)
            k.then(dve, "dve", dve.tensor_tensor(sc["be"], sc["beta"],
                                                 sc["exps"][:, 0:16].rearrange("p (t n) -> p t n", t=TT), ALU.mult))
            dve.tensor_scalar(sc["rnorms"][:, 0:16], sc["rnorms"][:, 0:16], float(P) ** -0.5, None, ALU.mult)
            for t in range(TT):
                for h in range(H):
                    at = slice(h * P, (h + 1) * P)
                    dve.tensor_scalar(kbe[:, t, at], khat[:, t, at], sc["be"][:, t, h:h + 1], None, ALU.mult)
                    dve.tensor_scalar(A[:, t, at], k.const(C_AFT), sc["g"][:, t, h:h + 1], None, ALU.mult)
            dve.wait_ge(s["khatT"], 1)
            for t in range(TT):
                for h in range(H):
                    at = slice(h * P, (h + 1) * P)
                    last = dve.tensor_scalar(khat[:, t, at], khat[:, t, at],
                                             sc["exps"][:, 16 + t * H + h:17 + t * H + h], None, ALU.mult)
            last.then_inc(s["ready"], 1)


def delta_matrices(k, proj, slab, sc, s):
    nc = k.nc
    H, NG = HEADS2, 4
    S0, S1, S2, S3, S4, S5 = (proj[:, :, 1024 * n:1024 * (n + 1)] for n in range(6))
    khat, vbeta, khatT, kbe, A = slab
    decT, dec, L, LT, Tm, TmT, Cm, Y, G, ecs = S3, S4, S5, S2, S4, S1, A, khatT, S1, A

    def head(x, h, a=0, b=T):
        return x[:, h // 4, (h % 4) * T + a:(h % 4) * T + b]

    def group(x, g):
        return x[:, g // 2, (g % 2) * 512:(g % 2 + 1) * 512]

    def one(x, g, j):
        return x[:, g // 2, (g % 2) * 512 + j * P:(g % 2) * 512 + (j + 1) * P]

    def each(c):
        return k.const(c).unsqueeze(1).broadcast_to([P, 4, P])

    def four(x):
        return x.rearrange("p (j n) -> p j n", j=4)

    with nc.Block() as block:
        @block.tensor
        def _(pe):
            pe.wait_ge(s["ready"], 2)
            cum = k.const(C_CUM)
            for g in range(NG):
                for j in range(4):
                    last = pe.matmul(k.ps[:, g, j * P:(j + 1) * P], one(A, g, j), cum, start=True, stop=True)
                last.then_inc(s["logT"], 1)
                pe.matmul(k.ps[:, 4 + g, :], cum, group(A, g), start=True, stop=True).then_inc(s["log"], 1)
            for g in range(NG):
                t = g // 2
                pe.wait_ge(s["decT"], g + 1)
                for j in range(4):
                    h = 4 * (g % 2) + j
                    last = pe.matmul(k.ps[:, g, j * P:(j + 1) * P], head(khatT, h, t * P, (t + 1) * P),
                                     head(S0, h, t * P, (t + 1) * P), start=True, stop=True)
                last.then_inc(s["qk"], 1)
            for g in range(NG):
                t = g // 2
                pe.wait_ge(s["dec"], g + 1)
                for j in range(4):
                    h = 4 * (g % 2) + j
                    kk = head(khatT, h, t * P, (t + 1) * P)
                    last = pe.matmul(k.ps[:, 4 + g, j * P:(j + 1) * P], kk, kk, start=True, stop=True)
                last.then_inc(s["kk"], 1)
            for g in range(NG):
                pe.wait_ge(s["attn"], g + 1)
                pe.wait_ge(s["G"], 1)
                for j in range(4):
                    last = pe.matmul(k.ps[:, g, j * P:(j + 1) * P], one(G, g, j), cum, start=True, stop=True)
                last.then_inc(s["cs"], 1)
            for g in range(NG):
                pe.wait_ge(s["L"], g + 1)
                for j in range(4):
                    last = pe.transpose(k.ps[:, 4 + g, j * P:(j + 1) * P], one(L, g, j), k.const(C_ID))
                last.then_inc(s["LT"], 1)
            for g in range(NG):
                pe.wait_ge(s["TT"], g + 1)
                for j in range(4):
                    last = pe.transpose(k.ps[:, g, j * P:(j + 1) * P], one(TmT, g, j), k.const(C_ID))
                last.then_inc(s["T0"], 1)
            for lv in range(1, LEVELS):
                done = (lv - 1) * NG
                for g in range(NG):
                    pe.wait_ge(s["C"], done + g + 1)
                    pe.wait_ge(s["T"], done + g + 1)
                    for j in range(4):
                        last = pe.matmul(k.ps[:, g, j * P:(j + 1) * P], one(Cm, g, j), one(Tm, g, j), start=True,
                                         stop=True)
                    last.then_inc(s["Y"], 1)
                for g in range(NG):
                    pe.wait_ge(s["Ys"], done + g + 1)
                    for j in range(4):
                        last = pe.matmul(k.ps[:, 4 + g, j * P:(j + 1) * P], one(Y, g, j), one(TmT, g, j), start=True,
                                         stop=True)
                    last.then_inc(s["ZT"], 1)
                    if lv < LEVELS - 1:
                        for j in range(4):
                            last = pe.matmul(k.ps[:, g, j * P:(j + 1) * P], one(TmT, g, j), one(Y, g, j), start=True,
                                             stop=True)
                        last.then_inc(s["Z"], 1)
            for g in range(NG):
                t = g // 2
                pe.wait_ge(s["TT"], LEVELS * NG - NG + g + 1)
                for j in range(4):
                    last = pe.matmul(k.ps[:, g, j * P:(j + 1) * P], one(TmT, g, j), one(vbeta, g, j), start=True,
                                     stop=True)
                last.then_inc(s["u"], 1)
                for j in range(4):
                    last = pe.matmul(k.ps[:, 4 + g, j * P:(j + 1) * P], one(kbe, g, j), one(TmT, g, j), start=True,
                                     stop=True)
                last.then_inc(s["w"], 1)

        @block.scalar
        def _(act):
            for g in range(NG):
                act.wait_ge(s["logT"], g + 1)
                act.activation(group(decT, g), k.ps[:, g, :], ACT.Exp).then_inc(s["decT"], 1)
                act.wait_ge(s["log"], g + 1)
                act.activation(group(dec, g), k.ps[:, 4 + g, :], ACT.Exp).then_inc(s["dec"], 1)
            for g in range(NG):
                act.wait_ge(s["cs"], g + 1)
                act.activation(group(ecs, g), k.ps[:, g, :], ACT.Exp).then_inc(s["ecs"], 1)
            for g in range(NG):
                act.wait_ge(s["LT"], g + 1)
                act.copy(group(LT, g), k.ps[:, 4 + g, :]).then_inc(s["LTs"], 1)
            for g in range(NG):
                act.wait_ge(s["T0"], g + 1)
                act.copy(group(Tm, g), k.ps[:, g, :]).then_inc(s["T"], 1)
            for lv in range(1, LEVELS):
                for g in range(NG):
                    act.wait_ge(s["Y"], (lv - 1) * NG + g + 1)
                    act.copy(group(Y, g), k.ps[:, g, :]).then_inc(s["Ys"], 1)
            for g in range(NG):
                act.wait_ge(s["w"], g + 1)
                act.copy(group(S4, g), k.ps[:, 4 + g, :]).then_inc(s["ws"], 1)

        @block.vector
        def _(dve):
            for t in range(TT):
                for h in range(H):
                    last = dve.tensor_scalar(G[:, t, h * P:(h + 1) * P], k.const(C_ONES), sc["g"][:, t, h:h + 1],
                                             None, ALU.mult)
            last.then_inc(s["G"], 1)
            for g in range(NG):
                dve.wait_ge(s["decT"], g + 1)
                last = dve.tensor_tensor(four(group(decT, g)), four(group(decT, g)), each(C_CUM), ALU.mult)
                dve.wait_ge(s["dec"], g + 1)
                last = dve.tensor_tensor(four(group(dec, g)), four(group(dec, g)), each(C_AFT), ALU.mult)
            k.then(dve, "dve", last)
            for g in range(NG):
                dve.wait_ge(s["qk"], g + 1)
                dve.tensor_tensor(group(decT, g), k.ps[:, g, :], group(decT, g), ALU.mult).then_inc(s["attn"], 1)
            for g in range(NG):
                dve.wait_ge(s["kk"], g + 1)
                for j in range(4):
                    h = 4 * (g % 2) + j
                    last = dve.scalar_tensor_tensor(one(L, g, j), k.ps[:, 4 + g, j * P:(j + 1) * P],
                                                    sc["beta"][:, g // 2, h:h + 1], one(dec, g, j), ALU.mult,
                                                    ALU.mult)
                last.then_inc(s["L"], 1)
            for g in range(NG):
                dve.wait_ge(s["ecs"], g + 1)
                t, q = g // 2, g % 2
                qT = S0[:, q, :].rearrange("p (j n) -> p j n", j=4)[:, :, t * P:(t + 1) * P]
                last = dve.tensor_tensor(qT, qT, four(group(ecs, g)), ALU.mult)
            k.then(dve, "dve", last)
            for g in range(NG):
                dve.wait_ge(s["LTs"], g + 1)
                k.then(dve, "dve", dve.tensor_tensor(four(group(TmT, g)), four(group(LT, g)), each(C_LVL), ALU.mult))
                dve.tensor_tensor(four(group(TmT, g)), each(C_ID), four(group(TmT, g)), ALU.subtract)\
                    .then_inc(s["TT"], 1)
            for g in range(NG):
                dve.tensor_tensor(four(group(Cm, g)), four(group(LT, g)), each(C_LVL + 1), ALU.mult)\
                    .then_inc(s["C"], 1)
            for lv in range(1, LEVELS):
                done = (lv - 1) * NG
                if lv > 1:
                    pass
                for g in range(NG):
                    dve.wait_ge(s["ZT"], done + g + 1)
                    if lv < LEVELS - 1:
                        dve.wait_ge(s["Z"], done + g + 1)
                    dve.wait_ge(s["TT"], done + g + 1)
                    dve.tensor_tensor(group(TmT, g), group(TmT, g), k.ps[:, 4 + g, :], ALU.subtract)\
                        .then_inc(s["TT"], 1)
                    if lv < LEVELS - 1:
                        dve.wait_ge(s["T"], done + g + 1)
                        dve.tensor_tensor(group(Tm, g), group(Tm, g), k.ps[:, g, :], ALU.subtract)\
                            .then_inc(s["T"], 1)
                        dve.tensor_tensor(four(group(Cm, g)), four(group(LT, g)), each(C_LVL + lv + 1), ALU.mult)\
                            .then_inc(s["C"], 1)
            for g in range(NG):
                dve.wait_ge(s["u"], g + 1)
                dve.tensor_copy(group(S5, g), k.ps[:, g, :]).then_inc(s["us"], 1)


def delta_recurrence(k, proj, slab, sc, s, hi, lo, sp_work):
    nc = k.nc
    H = HEADS2
    S0, S1, S2, S3, S4, S5 = (proj[:, :, 1024 * n:1024 * (n + 1)] for n in range(6))
    ktail, vbeta, khatT, kbe, A = slab
    attn, wT, u, vn, o = S3, S4, S5, S2, A
    state = khatT[:, 0, :]

    with nc.Block() as block:
        @block.sync
        def _(sp):
            sp_work(sp)

        @block.tensor
        def _(pe):
            for c in range(4):
                t, p = c // 2, CH * (c % 2)
                rows = slice(p, p + CH)
                if c:
                    pe.wait_ge(s["S"], c)
                    for h in range(H):
                        last = pe.matmul(k.ps[rows, h // 4, (h % 4) * P:(h % 4 + 1) * P],
                                         wT[:, t, h * P + p:h * P + p + CH], state[:, h * P:(h + 1) * P],
                                         start=True, stop=True)
                    last.then_inc(s["wS"], 1)
                    pe.wait_ge(s["o"], c)
                    for h in range(H):
                        q = S0[:, h // 4, (h % 4) * T + c * CH:(h % 4) * T + (c + 1) * CH]
                        last = pe.matmul(k.ps[rows, 6 + h // 4, (h % 4) * P:(h % 4 + 1) * P], q,
                                         state[:, h * P:(h + 1) * P], start=True, stop=True)
                    last.then_inc(s["qS"], 1)
                pe.wait_ge(s["vn"], c + 1)
                if c < 3:
                    for h in range(H):
                        last = pe.matmul(k.ps[:, 4 + h // 4, (h % 4) * P:(h % 4 + 1) * P],
                                         ktail[rows, t, h * P:(h + 1) * P], vn[rows, t, h * P:(h + 1) * P],
                                         start=True, stop=True)
                    last.then_inc(s["kv"], 1)
                for h in range(H):
                    last = pe.matmul(k.ps[rows, 2 + h // 4, (h % 4) * P:(h % 4 + 1) * P],
                                     attn[rows, t, h * P + p:h * P + p + CH], vn[rows, t, h * P:(h + 1) * P],
                                     start=True, stop=True)
                last.then_inc(s["av"], 1)

        @block.scalar
        def _(act):
            for c in range(4):
                t, p = c // 2, CH * (c % 2)
                act.wait_ge(s["av"], c + 1)
                act.copy(o[p:p + CH, t, :], k.ps[p:p + CH, 2:4, :].rearrange("p b n -> p (b n)"))\
                    .then_inc(s["o"], 1)
            act.wait_ge(s["scaled"], 1)
            for t in range(TT):
                for h in range(H):
                    at = slice(h * P, (h + 1) * P)
                    last = act.activation(S1[:, t, at], o[:, t, at], ACT.Square,
                                          accum_out=sc["oss"][:, t * H + h:t * H + h + 1])
            last.then_inc(s["oss"], 1)
            act.wait_ge(s["oss"], 2)
            act.activation(sc["oss"], sc["oss"], ACT.Sqrt).then_inc(s["oss"], 1)

        @block.vector
        def _(dve):
            for c in range(4):
                t, p = c // 2, CH * (c % 2)
                rows = slice(p, p + CH)
                if c == 0:
                    dve.tensor_copy(vn[rows, t, :], u[rows, t, :]).then_inc(s["vn"], 1)
                else:
                    dve.wait_ge(s["wS"], c)
                    dve.tensor_tensor(vn[rows, t, :], u[rows, t, :],
                                      k.ps[rows, 0:2, :].rearrange("p b n -> p (b n)"), ALU.subtract)\
                        .then_inc(s["vn"], 1)
                if c < 3:
                    dve.wait_ge(s["kv"], c + 1)
                    kv = k.ps[:, 4:6, :].rearrange("p b n -> p (b n)")
                    if c == 0:
                        dve.tensor_copy(state, kv).then_inc(s["S"], 1)
                    else:
                        dve.wait_ge(s["qS"], c)
                        dve.wait_ge(s["S"], c)
                        for h in range(H):
                            at = slice(h * P, (h + 1) * P)
                            last = dve.scalar_tensor_tensor(state[:, at], state[:, at],
                                                            sc["exps"][:, 32 + 8 * c + h:33 + 8 * c + h], kv[:, at],
                                                            ALU.mult, ALU.add)
                        last.then_inc(s["S"], 1)
                if c:
                    dve.wait_ge(s["o"], c + 1)
                    dve.wait_ge(s["qS"], c)
                    last = dve.tensor_tensor(o[rows, t, :], o[rows, t, :],
                                             k.ps[rows, 6:8, :].rearrange("p b n -> p (b n)"), ALU.add)
                    last.then_inc(s["oS"], 1)
            dve.wait_ge(s["oS"], 3)
            for t in range(TT):
                for h in range(H):
                    at = slice(h * P, (h + 1) * P)
                    last = dve.tensor_scalar(o[:, t, at], o[:, t, at], sc["rnorms"][:, t * H + h:t * H + h + 1], None,
                                             ALU.mult)
            last.then_inc(s["scaled"], 1)
            dve.wait_ge(s["oss"], 1)
            dve.tensor_scalar(sc["oss"], sc["oss"], 1.0 / P, EPS, ALU.mult, ALU.add).then_inc(s["oss"], 1)
            dve.wait_ge(s["oss"], 3)
            k.then(dve, "dve", dve.reciprocal(sc["orn"], sc["oss"]))
            for t in range(TT):
                for h in range(H):
                    at = slice(h * P, (h + 1) * P)
                    last = dve.scalar_tensor_tensor(o[:, t, at], o[:, t, at], sc["orn"][:, t * H + h:t * H + h + 1],
                                                    proj[:, t, GZ + h * P:GZ + (h + 1) * P], ALU.mult, ALU.mult)
            k.then(dve, "dve", last)
    split_transposed(k, o, H, lambda c: k.col("g_gdn"), hi[:, 8:16, :], lo[:, 8:16, :])


def gated_delta(k, proj, hi, lo, sp_work):
    names = ("taps", "channels", "squares", "sums", "silu", "khat", "vbeta", "rows", "g", "gsums", "khatT", "beta",
             "x", "tap0", "sums2", "exps", "ready", "logT", "log", "decT", "dec", "qk", "kk", "attn", "G", "cs",
             "L", "LT", "TT", "T0", "C", "T", "Y", "Ys", "ZT", "Z", "u", "w", "ecs", "LTs", "us", "ws", "S", "wS",
             "o", "qS", "vn", "kv", "av", "scaled", "oss", "oS")
    s = {n: k.sem(f"delta_{n}") for n in names}
    with ExitStack() as ctx:
        slab = [k.sb(f"delta_{n}", [P, TT, 1024], F32, ctx) for n in ("khat", "vbeta", "khatT", "kbe", "A")]
        sc = {}
        for n, shape in (("beta", [TT, 8]), ("x", [TT, 8]), ("ln", [TT, 8]), ("g", [TT, 8]), ("be", [TT, 8]),
                         ("ea", [8]), ("norms", [32]), ("rnorms", [32]), ("exps", [64]), ("oss", [16]), ("orn", [16])):
            sc[n] = k.sb(f"delta_s_{n}", [P, *shape], F32, ctx)[:]
        delta_inputs(k, proj, slab, sc, s)
        delta_matrices(k, proj, slab, sc, s)
        k.narrow_done += 3
        delta_recurrence(k, proj, slab, sc, s, hi, lo, sp_work)


def memory_attention(k, q, kv, xa_hi, xa_lo, sp_work):
    nc = k.nc
    H = 4
    scale = float(P) ** -0.5
    s = {n: k.sem(f"mem_{n}") for n in ("qk", "qT", "kT", "scored", "neg", "exp", "normed", "pt", "ptc", "out", "hi",
                                        "lo")}
    with ExitStack() as ctx:
        qT = k.sb("mem_qT", [P, H, T], F32, ctx)
        kT = k.sb("mem_kT", [P, H, T], F32, ctx)
        pr = k.sb("mem_p", [P, 2 * H, T], F32, ctx)
        pt = k.sb("mem_pT", [P, 2 * H, T], F32, ctx)
        st = k.sb("mem_st", [P, 4, 2 * H], F32, ctx)
        with nc.Block() as block:
            @block.sync
            def _(sp):
                sp_work(sp)

            @block.tensor
            def _(pe):
                for bank, x in ((0, q), (2, kv)):
                    for h in range(H):
                        for t in range(TT):
                            last = pe.transpose(
                                k.ps[:, bank + h // 2, (h % 2) * T + t * P:(h % 2) * T + (t + 1) * P],
                                x[:, t, h * P:(h + 1) * P], k.const(C_ID))
                last.then_inc(s["qk"], 1)
                pe.wait_ge(s["qT"], 1)
                pe.wait_ge(s["kT"], 1)
                for h in range(H):
                    for t in range(TT):
                        last = pe.matmul(k.ps[:, 4 + h, t * T:(t + 1) * T], qT[:, h, t * P:(t + 1) * P], kT[:, h, :],
                                         start=True, stop=True)
                last.then_inc(s["scored"], 1)
                pe.wait_ge(s["normed"], 1)
                for h in range(H):
                    for m in range(TT):
                        for t in range(TT):
                            last = pe.transpose(k.ps[:, h, m * T + t * P:m * T + (t + 1) * P],
                                                pr[:, TT * h + t, m * P:(m + 1) * P], k.const(C_ID))
                last.then_inc(s["pt"], 1)
                pe.wait_ge(s["ptc"], 2)
                for h in range(H):
                    for m in range(TT):
                        last = pe.matmul(k.ps[:, 4 + h // 2, (h % 2) * T:(h % 2 + 1) * T],
                                         kv[:, m, 512 + h * P:512 + (h + 1) * P], pt[:, TT * h + m, :],
                                         start=(m == 0), stop=(m == 1))
                last.then_inc(s["out"], 1)

            @block.scalar
            def _(act):
                act.wait_ge(s["qk"], 1)
                act.activation(qT[:], k.ps[:, 0:2, :].rearrange("p b (j n) -> p (b j) n", j=2), ACT.Copy,
                               scale=scale).then_inc(s["qT"], 1)
                act.wait_ge(s["neg"], 1)
                for n in range(2 * H):
                    last = act.activation(pr[:, n, :], k.ps[:, 4 + n // 2, (n % 2) * T:(n % 2 + 1) * T], ACT.Exp,
                                          bias=st[:, 1, n:n + 1], accum_out=st[:, 2, n:n + 1])
                last.then_inc(s["exp"], 1)
                act.wait_ge(s["pt"], 1)
                act.copy(pt[:, 0:4, :], k.ps[:, 0:2, :].rearrange("p b (j n) -> p (b j) n", j=2))\
                    .then_inc(s["ptc"], 1)
                act.wait_ge(s["out"], 1)
                act.copy(xa_hi[:], k.ps[:, 4:6, :].rearrange("p b (j n) -> p (b j) n", j=2)).then_inc(s["hi"], 1)

            @block.vector
            def _(dve):
                dve.wait_ge(s["qk"], 1)
                dve.tensor_copy(kT[:], k.ps[:, 2:4, :].rearrange("p b (j n) -> p (b j) n", j=2)).then_inc(s["kT"], 1)
                dve.wait_ge(s["scored"], 1)
                k.then(dve, "dve", dve.tensor_reduce(st[:, 0, :],
                                                     k.ps[:, 4:8, :].rearrange("p b (j n) -> p (b j) n", j=2), AX.X,
                                                     ALU.max))
                dve.tensor_scalar(st[:, 1, :], st[:, 0, :], -1.0, None, ALU.mult).then_inc(s["neg"], 1)
                dve.wait_ge(s["exp"], 1)
                k.then(dve, "dve", dve.reciprocal(st[:, 3, :], st[:, 2, :]))
                for n in range(2 * H):
                    last = dve.tensor_scalar(pr[:, n, :], pr[:, n, :], st[:, 3, n:n + 1], None, ALU.mult)
                last.then_inc(s["normed"], 1)
                dve.wait_ge(s["pt"], 1)
                dve.tensor_copy(pt[:, 4:8, :], k.ps[:, 2:4, :].rearrange("p b (j n) -> p (b j) n", j=2))\
                    .then_inc(s["ptc"], 1)
                dve.wait_ge(s["hi"], 1)
                dve.tensor_tensor(xa_lo[:], k.ps[:, 4:6, :].rearrange("p b (j n) -> p (b j) n", j=2),
                                  xa_hi[:].bitcast(F32), ALU.subtract).then_inc(s["lo"], 1)


def conv_hidden(k, stage, cv, hT_hi, hT_lo, tb):
    s = {n: k.sem(f"ffn2_{n}") for n in ("turned", "tap0", "tap1", "taps", "silu", "hid", "hi", "lo")}
    flat_hi, flat_lo = (x.rearrange("p c n -> p (c n)") for x in (hT_hi, hT_lo))
    at0 = COLS["fconv"][0]

    def weight(i, n, tap):
        return k.cols[:, bass.ds(at0 + 3 * ((n // 4) * HC + n % 4) + tap + i * 12, 1)]

    def bias(i, n):
        return k.cols[:, bass.ds(COLS["fbias"][0] + (n // 4) * HC + n % 4 + i * 4, 1)]

    def pe_hook(pe, i):
        pe.wait_ge(k.act_free, 2 + tb + 1 + 2 * i)
        pe.wait_ge(k.dve_free, 2 + tb + 2 + 2 * i)
        pe.wait_ge(s["taps"], i)
        for b in range(4):
            for j in range(2):
                c = 2 * (b % 2) + j
                for t in range(TT):
                    last = pe.transpose(k.ps[:, 4 + b, j * T + t * P:j * T + (t + 1) * P],
                                        stage[:, b // 2, t, c * P:(c + 1) * P], k.ident[:])
        last.then_inc(s["turned"], 1)

    def tap0(act, i):
        act.wait_ge(s["turned"], 1 + i)
        act.wait_ge(s["lo"], i)
        for n in range(8):
            last = act.activation(cv[:, n, :], k.ps[:, 4 + n // 2, (n % 2) * T:(n % 2 + 1) * T], ACT.Identity,
                                  scale=weight(i, n, 2), bias=bias(i, n))
        last.then_inc(s["tap0"], 1)

    def taps(dve, i):
        dve.wait_ge(s["tap0"], 1 + i)
        for tap, sem in ((1, "tap1"), (2, "taps")):
            for n in range(8):
                y = cv[:, n, tap:T]
                last = dve.scalar_tensor_tensor(y, k.ps[:, 4 + n // 2, (n % 2) * T:(n % 2 + 1) * T - tap],
                                                weight(i, n, 2 - tap), y, ALU.mult, ALU.add)
            last.then_inc(s[sem], 1)
            if tap == 1:
                dve.wait_ge(s["tap1"], 1 + i)

    def silu(act, i):
        act.wait_ge(s["taps"], 1 + i)
        act.activation(cv[:, 0:4, :], cv[:, 0:4, :], ACT.Silu).then_inc(s["silu"], 1)

    def mult(dve, i):
        dve.wait_ge(s["silu"], 1 + i)
        dve.tensor_tensor(cv[:, 0:4, :], cv[:, 0:4, :], cv[:, 4:8, :], ALU.mult).then_inc(s["hid"], 1)

    def part(x, i):
        return x[:, bass.ds(i * (4 * T), 4 * T)]

    def high(act, i):
        act.wait_ge(s["hid"], 1 + i)
        act.copy(part(flat_hi, i), cv[:, 0:4, :].rearrange("p c n -> p (c n)")).then_inc(s["hi"], 1)

    def low(dve, i):
        dve.wait_ge(s["hi"], 1 + i)
        dve.tensor_tensor(part(flat_lo, i), cv[:, 0:4, :].rearrange("p c n -> p (c n)"),
                          part(flat_hi, i).bitcast(F32), ALU.subtract).then_inc(s["lo"], 1)
    return s, [("pe", 5, pe_hook), ("act", 6, tap0), ("dve", 8, taps), ("act", 10, silu), ("dve", 11, mult),
               ("act", 12, high), ("dve", 13, low)]


def in2_tiles(w, hi, lo):
    return [Tile(w, DC, lambda i, m=m: i * (2 * NT) + m * NT, hi, lo) for m in range(2)]


def second_block_mix(k, a, hi, lo, xq_tiles_of):
    nc = k.nc
    tiles = in2_tiles(a["w_in_2"], hi, lo)
    out_tiles = square_tiles(a["w_out_2"], DC, hi, lo)
    with ExitStack() as life:
        proj = k.sb("proj2", [P, TT, 7 * 1024], F32, life)
        low_landed = k.sem("low2_landed")
        with ExitStack() as mid:
            low = [k.sb(f"low2_{n}", [P, DC, 16], d, mid) for n, d in (("raw", F32), ("hi", F32R), ("lo", F32R))]
            norm_transposed(k, k.h, lambda c: k.col("g_mix2", c), hi, lo, nrm=proj[:, :, 0:D],
                            sp_work=lambda sp: sp.dma_start(
                                low[0][:], a["w_in_2"][:, GBA:GBA + 16].rearrange("(c p) n -> p c n", p=P))
                            .then_inc(low_landed, 16))
            ae, de = copy_evacs(proj, stream_col)
            product(k, "in2", tiles, 7, lambda e, m, i, b: ae(e, m, i, b, k.ps), lambda e, m, i, b: de(e, m, i, b, k.ps),
                    act_last=lambda act: narrow_split(k, act, None, *low, (low_landed, 16)),
                    dve_last=lambda dve: narrow_split(k, None, dve, *low, None),
                    pe_last=lambda pe: narrow_product(k, pe, hi, lo, low[1], low[2]))
        stick_breaking(k, proj, hi, lo, lambda sp: prefetch(k, sp, out_tiles, k.unit))
        gated_delta(k, proj, hi, lo, lambda sp: None)
    product(k, "out2", out_tiles, 2, no_evac, add_to_stream(k)(stream_col), after=xq_tiles_of)


def second_block_memory(k, a, hi, lo, mem_parts, xq_tiles, next_tiles):
    nc = k.nc
    m_hi, m_lo = mem_parts
    with ExitStack() as life:
        q = k.sb("mem_q", [P, TT, 512], F32, life)
        kv = k.sb("mem_kv", [P, TT, 1024], F32, life)
        xa = [k.sb(f"xa_{n}", [P, 4, T], F32R, life) for n in ("hi", "lo")]
        xo_tiles = [Tile(a["w_xo_2"], 4, lambda i, m=m: m * NT, *xa) for m in range(4)]
        mem_landed = k.sem("mem_landed")
        with ExitStack() as mid:
            mem = k.sb("mem_rows", [P, TT, D], F32, mid)
            with nc.Block() as block:
                @block.sync
                def _(sp):
                    sp.dma_start(mem[:], a["mem_2"].rearrange("b (t p) d -> p (b t) d", p=P)).then_inc(mem_landed, 16)
                    sp.wait_ge(mem_landed, 16)
            norm_transposed(k, mem, lambda c: k.col("g_mem2", c), m_hi, m_lo)
        norm_transposed(k, k.h, lambda c: k.col("g_x2", c), hi, lo)

        def act_evac(act, m, i, bank):
            dst = q[:, 0, :] if m == 0 else kv[:, 0, (m - 1) * NT:m * NT]
            return act.copy(dst, k.ps[:, bank, :])

        def dve_evac(dve, m, i, bank):
            dst = q[:, 1, :] if m == 0 else kv[:, 1, (m - 1) * NT:m * NT]
            return dve.tensor_copy(dst, k.ps[:, bank + 1, :])
        product(k, "xqkv", xq_tiles, 1, act_evac, dve_evac)
        memory_attention(k, q, kv, *xa, lambda sp: prefetch(k, sp, xo_tiles, k.unit))
        product(k, "xo", xo_tiles, 1, no_evac, add_to_stream(k)(lambda m, i: m * NT), after=next_tiles)


def second_block_ffn(k, a, hi, lo, tiles):
    norm_transposed(k, k.h, lambda c: k.col("g_ffn2", c), hi, lo)
    with ExitStack() as life:
        hT = [k.sb(f"hT2_{n}", [P, HC, T], F32R, life) for n in ("hi", "lo")]
        down = down_tiles(a["w_down_2"], *hT)
        with ExitStack() as mid:
            stage = k.sb("ffn2_rows", [P, 2, TT, NT], F32, mid)
            cv = k.sb("ffn2_conv", [P, 8, T], F32, mid)
            tb = k.tile
            s, hooks = conv_hidden(k, stage, cv, *hT, tb)

            def act_evac(act, m, i, bank):
                if m:
                    return None
                act.wait_ge(s["turned"], i)
                return act.copy(stage[:, 0], k.ps[:, bank:bank + 2, :])

            def dve_evac(dve, m, i, bank):
                if m == 0:
                    return None
                dve.wait_ge(s["turned"], i)
                return dve.tensor_copy(stage[:, 1], k.ps[:, bank:bank + 2, :])
            product(k, "ffn2", tiles, FF2 // NT, act_evac, dve_evac, after=down, hooks=hooks)
        product(k, "down2", down, 2, no_evac, add_to_stream(k)(stream_col))


def build_program(nc, a, out):
    with ExitStack() as ctx:
        k = Kernel(nc, ctx)
        hi = k.sb("act_hi", [P, DC, T], F32R)
        lo = k.sb("act_lo", [P, DC, T], F32R)
        tiles2 = in2_tiles(a["w_in_2"], hi, lo)
        up_tiles = [Tile(a["w_up_2"], DC, lambda i, m=m: i * NT + m * FF2, hi, lo) for m in range(2)]
        with ExitStack() as masks:
            k.consts = k.sb("masks", [P, N_CONST, P], F32, masks)
            first_block(k, a, hi, lo, tiles2, None)
            with ExitStack() as late:
                q_tiles = [Tile(a["w_xq_2"], DC, lambda i: 0, hi, lo)]
                m_parts = [None, None]

                class Later(Tile):
                    pass
                kv_tiles = [Later(a["w_xkv_2"], DC, lambda i, m=m: m * NT, None, None) for m in range(2)]
                second_block_mix(k, a, hi, lo, q_tiles + kv_tiles)
                m_parts = [k.sb(f"memT_{n}", [P, DC, T], F32R, late) for n in ("hi", "lo")]
                for t in kv_tiles:
                    t.hi, t.lo = m_parts
                second_block_memory(k, a, hi, lo, m_parts, q_tiles + kv_tiles, up_tiles)
        second_block_ffn(k, a, hi, lo, up_tiles)
        gain = k.sb("gain_final2", [P, D], F32)
        s_gain, s_out = k.sem("gain_final2_landed"), k.sem("stored")
        res = k.sb("result", [P, TT, D], F32)
        with nc.Block() as block:
            @block.sync
            def _(sp):
                sp.dma_start(gain[:], a["g_final2"]).then_inc(s_gain, 16)
        norm_rows(k, "final2", gain, (s_gain, 16), res)
        with nc.Block() as block:
            @block.sync
            def _(sp):
                sp.dma_start(out.rearrange("b (t p) d -> p (b t) d", p=P), res[:]).then_inc(s_out, 16)
                sp.wait_ge(s_out, 16)




def _masks():
    import numpy as np
    c = np.zeros((P, N_CONST, P), np.float32)
    r, q = np.arange(P)[:, None], np.arange(P)[None, :]
    same = r // CH == q // CH
    c[:, C_ID] = r == q
    c[:, C_CUM] = (r <= q) & same
    c[:, C_AFT] = (r > q) & same
    c[:, C_AFTALL] = r > q
    c[:, C_BEFALL] = r < q
    c[:, C_ONES] = 1
    c[:CH, C_HALF] = 1
    c[CH:, C_HALF + 1] = 1
    for level in range(LEVELS):
        s = 1 << level
        c[:, C_LVL + level] = (r // (2 * s) == q // (2 * s)) & (r // s % 2 == 0) & (q // s % 2 == 1)
    return c


def _buckets():
    import math

    import numpy as np
    o = np.zeros((33, 3 * P), np.float32)
    for n in range(3 * P):
        d = 2 * P - 1 - n
        if d < 0 or d >= P:
            o[32, n] = 1
        elif d < 16:
            o[d, n] = 1
        else:
            o[min(31, 16 + int(math.log(d / 16) / math.log(8) * 16)), n] = 1
    return o


def kernel(**inputs):
    import numpy as np
    import concourse.bacc as bacc
    from concourse.bass_utils import run_bass_kernel_spmd

    v = {n: np.asarray(x) for n, x in inputs.items()}

    def chunks(x):
        return x.reshape(-1, P).T

    def every(x):
        return np.broadcast_to(x.reshape(1, -1), (P, x.size))
    parts = {
        "g_mix": chunks(v["norm_mix_g"]), "g_ffn": chunks(v["norm_ffn_g"]), "g_mix2": chunks(v["mix_norm_2"]),
        "g_x2": chunks(v["xattn_norm_2"]), "g_mem2": chunks(v["mem_norm_2"]), "g_ffn2": chunks(v["ffn_norm_2"]),
        "g_gla": chunks(v["gla_norm_g"]), "g_gdn": chunks(v["gdn_norm_2"]),
        "conv": v["gdn_conv_2"].reshape(4, 24, P).transpose(2, 1, 0).reshape(P, 96),
        "fconv": v["ffn_conv_2"].reshape(3, 88, P).transpose(2, 1, 0).reshape(P, 264),
        "fbias": chunks(v["ffn_conv_bias_2"]),
        "sinks": every(v["sinks"]), "alog": every(v["gdn_a_log_2"]), "dtb": every(v["gdn_dt_bias_2"]),
    }
    given = {"consts": _masks(), "onehot": _buckets(),
             "cols": np.ascontiguousarray(np.concatenate([parts[n] for n in COLS], 1)),
             "g_final1": np.ascontiguousarray(every(v["norm_final_g"])),
             "g_final2": np.ascontiguousarray(every(v["final_norm_2"])),
             "x": v["x"], "mem_2": v["mem_2"], "rel_bias": v["rel_bias"], "b_gate": v["b_gate"]}
    for n in ("w_in", "w_gate_up", "w_proj_a", "w_proj_b", "w_out", "w_ffn_gate", "w_ffn_up", "w_ffn_down",
              "w_in_2", "w_out_2", "w_xq_2", "w_xkv_2", "w_xo_2", "w_up_2", "w_down_2"):
        given[n] = v[n][0]
    nc = bacc.Bacc("TRN2", target_bir_lowering=False, num_devices=1)
    arrays, a = {}, {}
    for n, x in given.items():
        arrays[f"in_{n}"] = np.ascontiguousarray(x)
        a[n] = nc.dram_tensor(f"in_{n}", x.shape, mybir.dt.from_np(x.dtype), kind="ExternalInput").ap()
    out = nc.dram_tensor("out_0", (1, T, D), F32, kind="ExternalOutput").ap()
    build_program(nc, a, out)
    r = run_bass_kernel_spmd(nc, [arrays], core_ids=[0])
    return r.results[0]["out_0"]
```

```python
from contextlib import ExitStack

import concourse.bass as bass
from concourse import mybir

ALU = mybir.AluOpType
ACT = mybir.ActivationFunctionType
AX = mybir.AxisListType
F32 = mybir.dt.float32
F32R = mybir.dt.float32r

P = 128
T = 256
TT = T // P
D = 2048
DC = D // P
NT = 512
UC = 2
SLOTS = 4
LATE = 3
EPS = 1e-6
FF1, FF2 = 5632, 5632
HC = FF1 // P
NEG = -1e30
BIG = 3e38

QA, KA, VA, QB, KB, VB, GL, OG, GA, GB = 0, 1024, 1280, 1536, 2048, 2560, 3584, 3600, 4624, 6672
C_ID, C_CUM, C_AFT, C_AFTALL, C_BEFALL, C_ONES, C_HALF, C_LVL = 0, 1, 2, 3, 4, 5, 6, 8
LEVELS = 6
N_CONST = C_LVL + LEVELS
CH = 64

COLS = {}
_at = 0
for _name, _n in (("g_mix", DC), ("g_ffn", DC), ("g_mix2", DC), ("g_x2", DC), ("g_mem2", DC), ("g_ffn2", DC),
                  ("g_gla", 2), ("g_gdn", 1), ("conv", 96), ("fconv", 264), ("fbias", 88),
                  ("sinks", 16), ("alog", 8), ("dtb", 8)):
    COLS[_name] = (_at, _n)
    _at += _n
N_COLS = _at


def loop(eng, first, last, body):
    if last - first == 1:
        body(first)
    elif last > first:
        with eng.Fori(first, last) as i:
            body(i)


class Kernel:

    def __init__(self, nc, ctx):
        self.nc, self.ctx = nc, ctx
        self.unit = 0
        self.tile = 0
        self.steps = {"act": 0, "dve": 0, "pool": 0}
        self.t_done = 0
        self.n_sem = 0
        self.ring = self.sb("ring", [P, SLOTS, UC, NT], F32)
        self.w_hi = self.sb("w_hi", [P, SLOTS, UC, NT], F32R)
        self.w_lo = self.sb("w_lo", [P, SLOTS, UC, NT], F32R)
        self.h = self.sb("h", [P, TT, D], F32)
        self.ident = self.sb("ident", [P, P], F32)
        self.consts = None
        self.cols = self.sb("cols", [P, N_COLS], F32)
        self.small = self.sb("small", [P, 64], F32)
        self.ps = ctx.enter_context(nc.psum_tensor("ps", [P, 8, NT], F32))
        self.w_arrived = [self.sem(f"w_arrived{s}") for s in range(SLOTS)]
        self.hi_ready = self.sem("hi_ready")
        self.lo_ready = self.sem("lo_ready")
        self.unit_used = self.sem("unit_used")
        self.act_free = self.sem("act_free")
        self.dve_free = self.sem("dve_free")
        self.step = {e: self.sem(f"{e}_step") for e in self.steps}
        self.tp_done = self.sem("tp_done")
        self.tp_hi = self.sem("tp_hi")
        self.tp_lo = self.sem("tp_lo")
        self.narrow = self.sem("narrow")
        self.narrow_done = 0
        self.rms = self.sem("rms")
        self.rms_done = 0
        self.sums = self.sb("sums", [P, 2, TT, 4], F32)
        self.ahead = 0
        self.landed = self.sem("landed")

    def sb(self, name, shape, dt=F32, ctx=None):
        return (ctx or self.ctx).enter_context(self.nc.sbuf_tensor(name, shape, dt))

    def sem(self, name):
        self.n_sem += 1
        return self.ctx.enter_context(self.nc.semaphore(name))

    def const(self, c):
        return self.ident[:] if c == C_ID else self.consts[:, c, :]

    def col(self, name, i=0, n=1):
        at = COLS[name][0] + i
        return self.cols[:, at:at + n]

    def then(self, eng, key, ins):
        self.steps[key] += 1
        ins.then_inc(self.step[key], 1)
        eng.wait_ge(self.step[key], self.steps[key])


def weight_unit(w, row, col):
    return w[row:row + UC * P, bass.ds(col, NT)].rearrange("(c p) n -> p c n", p=P)


class Tile:

    def __init__(self, w, chunks, col, hi, lo, rows=0):
        self.w, self.chunks, self.col, self.hi, self.lo, self.rows = w, chunks, col, hi, lo, rows


def load_unit(k, sp, tiles, i, u, base):
    n = u
    for tile in tiles:
        if n < tile.chunks // UC:
            break
        n -= tile.chunks // UC
    sp.dma_start(k.ring[:, u % SLOTS], weight_unit(tile.w, tile.rows + n * UC * P, tile.col(i)))\
        .then_inc(k.w_arrived[u % SLOTS], 16)


def prefetch(k, sp, tiles, base):
    for u in range(SLOTS):
        if base:
            sp.wait_ge(k.lo_ready, base + u - SLOTS + 1)
        load_unit(k, sp, tiles, 0, u, base)


class Rows:

    def __init__(self, k, ctx, src, chunks, gain, hi, lo, normed=False, landed=None, summed=False,
                 which=0):
        self.k, self.src, self.pairs, self.gain, self.hi, self.lo, self.normed = k, src, chunks // 2, gain, hi, lo, normed
        self.summed, self.sums = summed, k.sums[:, which]
        self.landed = landed
        k.t_done += self.pairs
        if normed:
            self.rms0 = k.rms_done
            k.rms_done += 5
            self.stat = k.sb(f"rms_stat{self.rms0}", [P, 3, TT], F32, ctx)
            self.diag = k.sb(f"rms_diag{self.rms0}", [P, TT, P], F32, ctx)

    def stats_act(self, act):
        k = self.k
        if self.landed:
            act.wait_ge(self.landed, 16)
        if not self.summed:
            for t in range(TT):
                last = act.activation(self.hi[:, t * 8:(t + 1) * 8, :].rearrange("p c n -> p (c n)"),
                                      self.src[:, t, :], ACT.Square, accum_out=self.sums[:, t, 0:1])
            last.then_inc(k.rms, 1)
        act.wait_ge(k.rms, self.rms0 + 2)
        act.activation(self.stat[:, 1, :], self.stat[:, 1, :], ACT.Sqrt).then_inc(k.rms, 1)

    def stats_dve(self, dve):
        k = self.k
        if self.summed:
            dve.tensor_reduce(self.stat[:, 0, :], self.sums, AX.X, ALU.add).then_inc(k.rms, 1)
        dve.wait_ge(k.rms, self.rms0 + 1)
        sums = self.stat[:, 0, :] if self.summed else self.sums[:, :, 0]
        dve.tensor_scalar(self.stat[:, 1, :], sums, 1.0 / D, EPS, ALU.mult, ALU.add).then_inc(k.rms, 1)
        dve.wait_ge(k.rms, self.rms0 + 3)
        dve.reciprocal(self.stat[:, 2, :], self.stat[:, 1, :]).then_inc(k.rms, 1)
        dve.wait_ge(k.rms, self.rms0 + 4)
        for t in range(TT):
            last = dve.tensor_scalar(self.diag[:, t, :], k.ident[:], self.stat[:, 2, t:t + 1], None, ALU.mult)
        last.then_inc(k.rms, 1)

    def pair_pe(self, pe, s, bank):
        k = self.k
        if self.normed and s == 0:
            pe.wait_ge(k.rms, self.rms0 + 5)
        for c in range(2):
            for t in range(TT):
                out = k.ps[:, bank, c * T + t * P:c * T + (t + 1) * P]
                one = self.src[:, t, (2 * s + c) * P:(2 * s + c + 1) * P]
                if self.normed:
                    last = pe.matmul(out, one, self.diag[:, t, :], start=True, stop=True)
                else:
                    last = pe.transpose(out, one, k.ident[:])
        last.then_inc(k.tp_done, 1)

    def pair_act(self, act, s, bank):
        for c in range(2):
            at = 2 * s + c
            last = act.activation(self.hi[:, at, :], self.k.ps[:, bank, c * T:(c + 1) * T], ACT.Copy,
                                  scale=self.gain(at))
        last.then_inc(self.k.tp_hi, 1)

    def pair_dve(self, dve, s, bank):
        for c in range(2):
            at = 2 * s + c
            last = dve.scalar_tensor_tensor(self.lo[:, at, :], self.k.ps[:, bank, c * T:(c + 1) * T], self.gain(at),
                                            self.hi[:, at, :].bitcast(F32), ALU.mult, ALU.subtract)
        last.then_inc(self.k.tp_lo, 1)


def split_hi(k, act, s, count, more=0):
    act.wait_ge(k.w_arrived[s], 16 * (count // SLOTS + 1) + more * 16 // SLOTS)
    act.wait_ge(k.unit_used, count + 1 + more)
    act.copy(k.w_hi[:, s], k.ring[:, s]).then_inc(k.hi_ready, 1)


def split_lo(k, dve, s, count, more=0):
    dve.wait_ge(k.hi_ready, count + 1 + more)
    dve.tensor_tensor(k.w_lo[:, s], k.ring[:, s], k.w_hi[:, s].bitcast(F32), ALU.subtract).then_inc(k.lo_ready, 1)


def product(k, name, tiles, passes, act_evac, dve_evac, hooks=(), after=None, sp_first=None, pe_last=None,
            pool_work=None, once=(), rows=(), rows_at=0, rows_need=0,
            hooks_in_next=False):
    nc = k.nc
    sizes = [t.chunks // UC for t in tiles]
    units = sum(sizes)
    nt = len(tiles)
    base, tbase = k.unit, k.tile
    done, k.ahead = k.ahead, (SLOTS if after else 0)
    assert units % SLOTS == 0 and (nt % 2 == 0 or passes == 1) and base % SLOTS == 0
    k.unit += units * passes
    k.tile += nt * passes
    ends = [sum(sizes[:m + 1]) for m in range(nt)]
    pairs = [(r, n) for r in rows for n in range(r.pairs)]
    starts = {0: rows[0]} if rows else {}
    if len(rows) > 1:
        starts[rows[0].pairs - 2] = rows[1]
    t0 = k.t_done - len(pairs)
    assert not rows or rows_at + len(pairs) + 2 <= units
    evac_at = {}
    for m in range(nt):
        at = ends[m] - 1 + LATE
        evac_at.setdefault((at // units, at % units), []).append(m)

    def stream(eng, which, unit_step, evac, stats, pair):
        mine = [(u, fn) for e, u, fn in hooks if e == which]
        mine_once = [(u, fn) for e, u, fn in once if e == which]

        def pair_step(j):
            if j in starts and starts[j].normed:
                stats(starts[j])
            pair(j)

        def body(i, first=False):
            for u in range(units):
                if first and 0 <= u - rows_at - 2 < len(pairs):
                    pair_step(u - rows_at - 2)
                if not (first and u < done):
                    unit_step(i, u)
                if first:
                    for at, fn in mine_once:
                        if at == u:
                            fn(eng)
                else:
                    for m in evac_at.get((1, u), ()):
                        evac(m, i - 1)
                    for at, fn in mine:
                        if at == u:
                            fn(eng, i - 1)
                for m in evac_at.get((0, u), ()):
                    evac(m, i)

        if rows_at == 0 and rows and rows[0].normed:
            stats(rows[0])
            del starts[0]
        body(0, True)
        if rows_at == 0 and rows and rows[0].normed:
            starts[0] = rows[0]
        loop(eng, 1, passes, body)
        for u in range(units):
            if u < k.ahead:
                unit_step(passes, u)
            for m in evac_at.get((1, u), ()):
                evac(m, passes - 1)
            for at, fn in mine:
                if at == u and not hooks_in_next:
                    fn(eng, passes - 1)

    with nc.Block() as block:
        @block.sync
        def _(sp):
            if sp_first:
                sp_first(sp)

            def body(i, more=True):
                for u in range(SLOTS, units + SLOTS * more):
                    paired = () if isinstance(i, int) else [e for e in ends[:-1] if e > SLOTS]
                    if u not in paired:
                        ahead = (u + 1) in paired
                        sp.wait_ge(k.lo_ready, base + u - SLOTS + 1 + ahead + i * units)
                    if u < units:
                        load_unit(k, sp, tiles, i, u, base)
                    else:
                        load_unit(k, sp, tiles, i + 1, u - units, base)
            loop(sp, 0, passes - 1, body)
            body(passes - 1, False)
            if after:
                prefetch(k, sp, after, k.unit)

        if pool_work:
            @block.gpsimd
            def _(pool):
                pool_work(pool)

        @block.scalar
        def _(act):
            def evac(m, i):
                act.wait_ge(k.unit_used, SLOTS + base + ends[m] + i * units)
                last = act_evac(act, m, i, 2 * ((tbase + m) % 2))
                (last.then_inc if last is not None else lambda *a: act.sem_inc(*a))(k.act_free, 1)

            def pair(j):
                act.wait_ge(k.tp_done, t0 + j + 1)
                pairs[j][0].pair_act(act, pairs[j][1], 4 + j % 4)
            stream(act, "act", lambda i, u: split_hi(k, act, u % SLOTS, base + u, i * units), evac, lambda r: r.stats_act(act), pair)

        @block.vector
        def _(dve):
            def evac(m, i):
                dve.wait_ge(k.unit_used, SLOTS + base + ends[m] + i * units)
                last = dve_evac(dve, m, i, 2 * ((tbase + m) % 2))
                (last.then_inc if last is not None else lambda *a: dve.sem_inc(*a))(k.dve_free, 1)

            def pair(j):
                dve.wait_ge(k.tp_hi, t0 + j + 1)
                pairs[j][0].pair_dve(dve, pairs[j][1], 4 + j % 4)
            stream(dve, "dve", lambda i, u: split_lo(k, dve, u % SLOTS, base + u, i * units), evac, lambda r: r.stats_dve(dve), pair)

        @block.tensor
        def _(pe):
            mine = [(u, fn) for e, u, fn in hooks if e == "pe"]

            def pair(j):
                if j < len(pairs):
                    if j >= 4:
                        pe.wait_ge(k.tp_lo, t0 + j - 3)
                    pairs[j][0].pair_pe(pe, pairs[j][1], 4 + j % 4)

            def body(i, first=False):
                u = 0
                for m, tile in enumerate(tiles):
                    bank = 2 * ((tbase + m) % 2)
                    pe.wait_ge(k.act_free, tbase + m + 1 + i * nt)
                    pe.wait_ge(k.dve_free, tbase + m + 1 + i * nt)
                    for n in range(sizes[m]):
                        s = u % SLOTS
                        if first:
                            for e, at, fn in once:
                                if e == "pe_first" and at == u:
                                    fn(pe)
                        if first and u == rows_at:
                            for j in range(4):
                                pair(j)
                        if first and 0 <= u - rows_need < len(pairs):
                            pe.wait_ge(k.tp_lo, t0 + u - rows_need + 1)
                        pe.wait_ge(k.lo_ready, base + u + 1 + i * units)
                        for c in range(UC):
                            kc = n * UC + c
                            for t in range(TT):
                                acc = k.ps[:, bank + t, :]
                                hi = tile.hi[:, kc, t * P:(t + 1) * P]
                                lo = tile.lo[:, kc, t * P:(t + 1) * P]
                                pe.matmul(acc, hi, k.w_hi[:, s, c, :], start=(kc == 0), stop=False)
                                pe.matmul(acc, hi, k.w_lo[:, s, c, :], start=False, stop=False)
                                last = pe.matmul(acc, lo, k.w_hi[:, s, c, :], start=False,
                                                 stop=(kc == tile.chunks - 1))
                        last.then_inc(k.unit_used, 1)
                        if first and u >= rows_at:
                            pair(u - rows_at + 4)
                        if not first:
                            for at, fn in mine:
                                if at == u:
                                    fn(pe, i - 1)
                        u += 1
            if mine or rows or once:
                body(0, True)
                loop(pe, 1, passes, body)
                for _, fn in mine:
                    fn(pe, passes - 1)
            else:
                loop(pe, 0, passes, body)
            if pe_last:
                pe_last(pe)


class Narrow:
    STEPS = 5

    def __init__(self, k, name, ctx):
        self.k = k
        self.raw = k.sb(f"{name}_raw", [P, DC, 16], F32, ctx)
        self.hi = k.sb(f"{name}_hi", [P, DC, P], F32R, ctx)
        self.lo = k.sb(f"{name}_lo", [P, DC, P], F32R, ctx)
        self.landed = k.sem(f"{name}_landed")

    def load(self, sp, w):
        sp.dma_start(self.raw[:], w.rearrange("(c p) n -> p c n", p=P)).then_inc(self.landed, 16)

    def pad(self, pool):
        pool.memset(self.hi[:].bitcast(F32), 0.0).then_inc(self.k.narrow, 1)
        pool.memset(self.lo[:].bitcast(F32), 0.0).then_inc(self.k.narrow, 1)

    def split_hi(self, act):
        act.wait_ge(self.landed, 16)
        act.wait_ge(self.k.narrow, self.k.narrow_done + 2)
        act.copy(self.hi[:, :, 0:16], self.raw[:]).then_inc(self.k.narrow, 1)

    def split_lo(self, dve):
        dve.wait_ge(self.k.narrow, self.k.narrow_done + 3)
        dve.tensor_tensor(self.lo[:, :, 0:16], self.raw[:], self.hi[:, :, 0:16].bitcast(F32), ALU.subtract)\
            .then_inc(self.k.narrow, 1)

    def product(self, pe, hi, lo):
        k = self.k
        pe.wait_ge(k.narrow, k.narrow_done + 4)
        acc = k.ps[:, 7, 0:T]
        for c in range(DC):
            pe.matmul(acc, self.hi[:, c, :], hi[:, c, :], start=(c == 0), stop=False)
            pe.matmul(acc, self.hi[:, c, :], lo[:, c, :], start=False, stop=False)
            last = pe.matmul(acc, self.lo[:, c, :], hi[:, c, :], start=False, stop=(c == DC - 1))
        last.then_inc(k.narrow, 1)


def sliding_window(k, proj, bias_rows, oa_hi, oa_lo):
    nc = k.nc
    G, HD, NG = 4, 64, 4
    scale = HD ** -0.5
    with ExitStack() as ctx:
        qT = k.sb("swa_qT", [HD, G, T], F32, ctx)
        kT = k.sb("swa_kT", [HD, T], F32, ctx)
        S2 = k.sb("swa_S", [P, 2, G, 3 * P], F32, ctx)
        PT = k.sb("swa_PT", [P, 3 * G, P], F32, ctx)
        bias = k.sb("swa_bias", [P, 2, G, T], F32, ctx)
        bias_landed = [k.sem(f"swa_bias_landed{n}") for n in range(2)]
        st = k.sb("swa_st", [P, 2, 6, 2 * G], F32, ctx)
        qk_t, qk_c, sc_d, sb_d, ngm, ex_d, nm_d, pt_t, pt_c, ov_d, oh_d, ol_d = (
            k.sem(f"swa_{n}") for n in ("qk_transposed", "qk_copied", "scored", "biased", "neg_max", "exped",
                                        "normed", "p_transposed", "p_copied", "summed", "o_hi", "o_lo"))
        with nc.Block() as block:
            @block.sync
            def _(sp):
                for g in range(NG):
                    if g >= 2:
                        sp.wait_ge(nm_d, g - 1)
                    sp.dma_start(bias[:, g % 2], bass.AP(tensor=bias_rows, offset=G * g * 3 * P + P - 1,
                                                         ap=[[16 * 3 * P - 1, P], [3 * P, G], [1, T]]))\
                        .then_inc(bias_landed[g % 2], 16)

            @block.tensor
            def _(pe):
                ident = k.const(C_ID)

                def queries_keys(g):
                    if g >= NG:
                        return
                    if g >= 2:
                        pe.wait_ge(pt_c, 2 * (g - 1))
                    if g == 1:
                        pe.wait_ge(qk_c, 2)
                    for j in range(G):
                        for t in range(TT):
                            pe.transpose(k.ps[0:HD, j // 2, (j % 2) * T + t * P:(j % 2) * T + (t + 1) * P],
                                         proj[:, t, QA + (G * g + j) * HD:QA + (G * g + j + 1) * HD], ident)
                    for t in range(TT):
                        last = pe.transpose(k.ps[0:HD, 2, t * P:(t + 1) * P],
                                            proj[:, t, KA + g * HD:KA + (g + 1) * HD], ident)
                    last.then_inc(qk_t, 1)

                def scores(g):
                    if g >= NG:
                        return
                    pe.wait_ge(qk_c, 2 * (g + 1))
                    if g:
                        pe.wait_ge(sb_d, g)
                    for j in range(G):
                        pe.matmul(k.ps[:, 3, j * P:(j + 1) * P], qT[:, j, 0:P], kT[:, 0:P], start=True, stop=True)
                    for j in range(G):
                        last = pe.matmul(k.ps[:, 4 + j // 2, (j % 2) * T:(j % 2 + 1) * T], qT[:, j, P:T], kT[:],
                                         start=True, stop=True)
                    last.then_inc(sc_d, 1)

                queries_keys(0)
                scores(0)
                queries_keys(1)
                for g in range(NG):
                    S = S2[:, g % 2]
                    scores(g + 1)
                    pe.wait_ge(nm_d, g + 1)
                    if g + 1 < NG:
                        pe.wait_ge(qk_c, 2 * (g + 2))
                    for b in range(3):
                        for j in range(G):
                            last = pe.transpose(k.ps[:, b, j * P:(j + 1) * P], S[:, j, b * P:(b + 1) * P], ident)
                    last.then_inc(pt_t, 1)
                    pe.wait_ge(pt_c, 2 * (g + 1))
                    if g:
                        pe.wait_ge(ol_d, g)
                    for j in range(G):
                        at = HD * (j % 2)
                        for b, kb in enumerate((0, 0, 1)):
                            q = 0 if b == 0 else P
                            last = pe.matmul(k.ps[at:at + HD, 6, (j // 2) * T + q:(j // 2) * T + q + P],
                                             proj[:, kb, VA + g * HD:VA + (g + 1) * HD], PT[:, b * G + j, :],
                                             start=(b < 2), stop=(b != 1))
                    last.then_inc(ov_d, 1)
                    queries_keys(g + 2)

            @block.scalar
            def _(act):
                def queries_keys(g):
                    if g >= NG:
                        return
                    act.wait_ge(qk_t, g + 1)
                    if g:
                        act.wait_ge(sc_d, g)
                    act.activation(qT[:], k.ps[0:HD, 0:2, :].rearrange("p b (j n) -> p (b j) n", j=2), ACT.Copy,
                                   scale=scale).then_inc(qk_c, 1)
                    act.copy(kT[:], k.ps[0:HD, 2, 0:T]).then_inc(qk_c, 1)

                def exponentials(g):
                    if g >= NG:
                        return
                    S, (mx, neg, den, esk, rec, dif) = S2[:, g % 2], (st[:, g % 2, n, :] for n in range(6))
                    act.wait_ge(ngm, g + 1)
                    for b, (lo, hi) in enumerate(((0, P), (P, 3 * P))):
                        for j in range(G):
                            at = b * G + j
                            act.activation(S[:, j, lo:hi], S[:, j, lo:hi], ACT.Exp, bias=neg[:, at:at + 1],
                                           accum_out=den[:, at:at + 1])
                    act.activation(esk, dif, ACT.Exp).then_inc(ex_d, 1)

                queries_keys(0)
                exponentials(0)
                queries_keys(1)
                for g in range(NG):
                    exponentials(g + 1)
                    act.wait_ge(pt_t, g + 1)
                    act.copy(PT[:, 0:2 * G, :], k.ps[:, 0:2, :].rearrange("p b (j n) -> p (b j) n", j=G))\
                        .then_inc(pt_c, 1)
                    act.wait_ge(ov_d, g + 1)
                    act.copy(oa_hi[:, 2 * g:2 * g + 2, :], k.ps[:, 6, :].rearrange("p (c n) -> p c n", c=2))\
                        .then_inc(oh_d, 1)
                    queries_keys(g + 2)

            @block.vector
            def _(dve):
                def maxima(g):
                    if g >= NG:
                        return
                    S, (mx, neg, den, esk, rec, dif) = S2[:, g % 2], (st[:, g % 2, n, :] for n in range(6))
                    dve.wait_ge(bias_landed[g % 2], 16 * (g // 2 + 1))
                    dve.wait_ge(sc_d, g + 1)
                    if g >= 2:
                        dve.wait_ge(pt_t, g - 1)
                    dve.tensor_tensor(S[:, :, 0:P], k.ps[:, 3, :].rearrange("p (j n) -> p j n", j=G),
                                      bias[:, g % 2, :, P:T], ALU.add)
                    dve.tensor_tensor(
                        S[:, :, P:3 * P], k.ps[:, 4:6, :].rearrange("p b (j n) -> p (b j) n", j=2),
                        bias[:, g % 2], ALU.add).then_inc(sb_d, 1)
                    dve.wait_ge(sb_d, g + 1)
                    dve.tensor_reduce(mx[:, 0:G], S[:, :, 0:P], AX.X, ALU.max)
                    k.then(dve, "dve", dve.tensor_reduce(mx[:, G:2 * G], S[:, :, P:3 * P], AX.X, ALU.max))
                    sink = k.col("sinks", G * g, G)
                    dve.tensor_tensor(mx[:, 0:G], mx[:, 0:G], sink, ALU.max)
                    k.then(dve, "dve", dve.tensor_tensor(mx[:, G:2 * G], mx[:, G:2 * G], sink, ALU.max))
                    dve.tensor_tensor(dif[:, 0:G], sink, mx[:, 0:G], ALU.subtract)
                    dve.tensor_tensor(dif[:, G:2 * G], sink, mx[:, G:2 * G], ALU.subtract)
                    dve.tensor_scalar(neg, mx, -1.0, None, ALU.mult).then_inc(ngm, 1)

                maxima(0)
                for g in range(NG):
                    maxima(g + 1)
                    S, (mx, neg, den, esk, rec, dif) = S2[:, g % 2], (st[:, g % 2, n, :] for n in range(6))
                    dve.wait_ge(ex_d, g + 1)
                    k.then(dve, "dve", dve.tensor_tensor(den, den, esk, ALU.add))
                    k.then(dve, "dve", dve.reciprocal(rec, den))
                    for b, (lo, hi) in enumerate(((0, P), (P, 3 * P))):
                        for j in range(G):
                            at = b * G + j
                            last = dve.tensor_scalar(S[:, j, lo:hi], S[:, j, lo:hi], rec[:, at:at + 1], None,
                                                     ALU.mult)
                    last.then_inc(nm_d, 1)
                    dve.wait_ge(pt_t, g + 1)
                    dve.tensor_copy(PT[:, 2 * G:3 * G, :], k.ps[:, 2, :].rearrange("p (j n) -> p j n", j=G))\
                        .then_inc(pt_c, 1)
                    dve.wait_ge(oh_d, g + 1)
                    dve.tensor_tensor(oa_lo[:, 2 * g:2 * g + 2, :], k.ps[:, 6, :].rearrange("p (c n) -> p c n", c=2),
                                      oa_hi[:, 2 * g:2 * g + 2, :].bitcast(F32), ALU.subtract).then_inc(ol_d, 1)


def gated_linear(k, proj, og, w_up, b_up, sp_work):
    nc = k.nc
    H, DV = 4, 256
    inv_tau = 1.0 / 16.0
    scale = float(P) ** -0.5
    with ExitStack() as ctx:
        gate_w = k.sb("gla_gate_w", [16, 2, 512], F32, ctx)
        gate_landed = k.sem("gla_gate_landed")
        glT = k.sb("gla_glT", [16, T], F32, ctx)
        la = at = proj[:, :, 0:H * P]
        ex = proj[:, :, H * P:2 * H * P]
        ks = proj[:, :, 2 * H * P:3 * H * P]
        y = proj[:, :, QB:VB]
        up = k.sb("gla_up", [P, H, T], F32, ctx)
        dn = k.sb("gla_dn", [P, H, T], F32, ctx)
        qd = k.sb("gla_qd", [P, H, T], F32, ctx)
        kd = dn
        state = k.sb("gla_state", [P, 3, H, DV], F32, ctx)
        st = k.sb("gla_st", [P, 3, TT * H], F32, ctx)
        names = ("gl_in", "z", "abs_done", "la", "b", "sfx", "exps", "qk", "decayed", "scored",
                 "masked", "grown", "state", "out", "squares", "root", "y")
        s = {n: k.sem(f"gla_{n}") for n in names}
        with nc.Block() as block:
            @block.sync
            def _(sp):
                sp.dma_start(gate_w[:, 0, :], w_up).then_inc(gate_landed, 16)
                sp.dma_start(gate_w[0:1, 1, :], b_up).then_inc(gate_landed, 16)
                sp_work(sp)

            @block.tensor
            def _(pe):
                pe.wait_ge(s["gl_in"], 1)
                pe.wait_ge(gate_landed, 32)
                for t in range(TT):
                    pe.matmul(k.ps[:, t, :], glT[:, t * P:(t + 1) * P], gate_w[0:16, 0, :], start=True, stop=False)
                    last = pe.matmul(k.ps[:, t, :], k.consts[0:1, C_ONES, :], gate_w[0:1, 1, :], start=False, stop=True)
                last.then_inc(s["z"], 1)
                for base, bank in ((QB, 4), (KB, 6)):
                    for h in range(H):
                        for t in range(TT):
                            last = pe.transpose(k.ps[:, bank + h // 2, (h % 2) * T + t * P:(h % 2) * T + (t + 1) * P],
                                                proj[:, t, base + h * P:base + (h + 1) * P], k.const(C_ID))
                last.then_inc(s["qk"], 1)
                pe.wait_ge(s["la"], 1)
                for h in range(H):
                    for t in range(TT):
                        last = pe.matmul(k.ps[:, 2 + h // 2, (h % 2) * T + t * P:(h % 2) * T + (t + 1) * P],
                                         la[:, t, h * P:(h + 1) * P], k.const(C_CUM), start=True, stop=True)
                last.then_inc(s["b"], 1)
                for t in range(TT):
                    last = pe.matmul(k.ps[:, t, :], k.const(C_AFT), la[:, t, :], start=True, stop=True)
                last.then_inc(s["sfx"], 1)
                pe.wait_ge(s["decayed"], 1)
                for t in range(TT):
                    for h in range(H):
                        last = pe.matmul(k.ps[:, 2 + t, h * P:(h + 1) * P], kd[:, h, t * P:(t + 1) * P],
                                         qd[:, h, t * P:(t + 1) * P], start=True, stop=True)
                last.then_inc(s["scored"], 1)
                pe.wait_ge(s["decayed"], 2)
                for c in range(3):
                    t, p = c // 2, CH * (c % 2)
                    for h in range(H):
                        last = pe.matmul(k.ps[:, (4 + 2 * c) % 8 + h // 2, (h % 2) * DV:(h % 2 + 1) * DV],
                                         ks[p:p + CH, t, h * P:(h + 1) * P],
                                         proj[p:p + CH, t, VB + h * DV:VB + (h + 1) * DV], start=True, stop=True)
                    last.then_inc(s["grown"], 1)
                pe.wait_ge(s["masked"], 1)
                pe.wait_ge(s["state"], 3)
                for t in range(TT):
                    for h in range(H):
                        bank, lo = 2 + 2 * t + h // 2, (h % 2) * DV
                        for c in range(2 * t, 2 * t + 2):
                            p = CH * (c % 2)
                            last = pe.matmul(k.ps[p:p + CH, bank, lo:lo + DV], at[:, t, h * P + p:h * P + p + CH],
                                             proj[:, t, VB + h * DV:VB + (h + 1) * DV], start=True, stop=(c == 0))
                            if c:
                                last = pe.matmul(k.ps[p:p + CH, bank, lo:lo + DV], qd[:, h, c * CH:(c + 1) * CH],
                                                 state[:, c - 1, h, :], start=False, stop=True)
                last.then_inc(s["out"], 1)

            @block.scalar
            def _(act):
                act.wait_ge(k.narrow, k.narrow_done + Narrow.STEPS)
                act.copy(glT[:], k.ps[0:16, 7, 0:T]).then_inc(s["gl_in"], 1)
                act.wait_ge(s["z"], 1)
                k.then(act, "act", act.activation(ex, k.ps[:, 0:2, :], ACT.Abs))
                k.then(act, "act", act.activation(ex, ex, ACT.Exp, scale=-1.0))
                act.activation(ex, ex, ACT.Ln, bias=1.0).then_inc(s["abs_done"], 1)
                act.wait_ge(s["b"], 1)
                b = k.ps[:, 2:4, :].rearrange("p b (j n) -> p (b j) n", j=2)
                act.activation(up[:], b, ACT.Exp, scale=inv_tau)
                act.activation(dn[:], b, ACT.Exp, scale=-inv_tau).then_inc(s["exps"], 1)
                act.wait_ge(s["sfx"], 1)
                act.wait_ge(s["la"], 1)
                act.activation(ex, k.ps[:, 0:2, :], ACT.Exp, scale=inv_tau).then_inc(s["exps"], 1)
                act.wait_ge(s["out"], 1)
                for t in range(TT):
                    for h in range(H):
                        last = act.activation(y[:, t, h * DV:(h + 1) * DV],
                                              k.ps[:, 2 + 2 * t + h // 2, (h % 2) * DV:(h % 2 + 1) * DV], ACT.Square,
                                              accum_out=st[:, 0, t * H + h:t * H + h + 1])
                last.then_inc(s["squares"], 1)
                act.wait_ge(s["root"], 1)
                act.activation(st[:, 1, :], st[:, 1, :], ACT.Sqrt).then_inc(s["root"], 1)

            @block.vector
            def _(dve):
                dve.wait_ge(s["abs_done"], 1)
                for t in range(TT):
                    last = dve.scalar_tensor_tensor(la[:, t, :], k.ps[:, t, :], 0.0, ex[:, t, :], ALU.min, ALU.subtract)
                last.then_inc(s["la"], 1)
                dve.wait_ge(s["qk"], 1)
                dve.wait_ge(s["exps"], 1)
                for b in range(2):
                    for j in range(2):
                        dve.scalar_tensor_tensor(qd[:, 2 * b + j, :], k.ps[:, 4 + b, j * T:(j + 1) * T], scale,
                                                 up[:, 2 * b + j, :], ALU.mult, ALU.mult)
                last = dve.tensor_tensor(kd[:], k.ps[:, 6:8, :].rearrange("p b (j n) -> p (b j) n", j=2), dn[:],
                                         ALU.mult)
                last.then_inc(s["decayed"], 1)
                dve.wait_ge(s["exps"], 2)
                dve.tensor_tensor(ks, proj[:, :, KB:KB + H * P], ex, ALU.mult).then_inc(s["decayed"], 1)
                dve.wait_ge(s["scored"], 1)
                k.then(dve, "dve", dve.tensor_scalar(at, k.ps[:, 2:4, :],
                                                     BIG, -BIG, ALU.min, ALU.max))
                for t in range(TT):
                    for h in range(H):
                        one = at[:, t, h * P:(h + 1) * P]
                        last = dve.tensor_tensor(one, one, k.const(C_CUM), ALU.mult)
                last.then_inc(s["masked"], 1)
                for c in range(3):
                    dve.wait_ge(s["grown"], c + 1)
                    grown = k.ps[:, (4 + 2 * c) % 8:(4 + 2 * c) % 8 + 2, :].rearrange("p b (j n) -> p (b j) n", j=2)
                    if c == 0:
                        dve.tensor_copy(state[:, 0, :, :], grown).then_inc(s["state"], 1)
                    else:
                        dve.wait_ge(s["state"], c)
                        for h in range(H):
                            last = dve.scalar_tensor_tensor(
                                state[:, c, h, :], state[:, c - 1, h, :], up[:, h, CH * (c + 1) - 1:CH * (c + 1)],
                                grown[:, h, :], ALU.mult, ALU.add)
                        last.then_inc(s["state"], 1)
                dve.wait_ge(s["squares"], 1)
                dve.tensor_scalar(st[:, 1, :], st[:, 0, :], 1.0 / DV, EPS, ALU.mult, ALU.add).then_inc(s["root"], 1)
                dve.wait_ge(s["root"], 2)
                k.then(dve, "dve", dve.reciprocal(st[:, 2, :], st[:, 1, :]))
                for t in range(TT):
                    for h in range(H):
                        last = dve.scalar_tensor_tensor(
                            y[:, t, h * DV:(h + 1) * DV],
                            k.ps[:, 2 + 2 * t + h // 2, (h % 2) * DV:(h % 2 + 1) * DV],
                            st[:, 2, t * H + h:t * H + h + 1], og[:, t, h * DV:(h + 1) * DV], ALU.mult, ALU.mult)
                k.then(dve, "dve", last)
        k.narrow_done += Narrow.STEPS
    return y


def norm_rows(k, gain, landed, room, again):
    nc = k.nc
    act0, dve0 = k.steps["act"], k.steps["dve"]
    with nc.Block() as block:
        @block.scalar
        def _(act):
            act.wait_ge(k.step["dve"], dve0 + 2)
            act.activation(k.small[:, 2:4], k.small[:, 2:4], ACT.Sqrt).then_inc(k.step["act"], 1)
            k.steps["act"] += 1
            if again:
                for t in range(TT):
                    act.wait_ge(k.step["dve"], dve0 + 4 + t)
                    act.activation(room[:, 8 * t:8 * (t + 1), :].rearrange("p c n -> p (c n)"), k.h[:, t, :],
                                   ACT.Square, accum_out=k.sums[:, 0, t, 0:1])

        @block.vector
        def _(dve):
            k.then(dve, "dve", dve.tensor_reduce(k.small[:, 0:2], k.sums[:, 0], AX.X, ALU.add))
            k.then(dve, "dve", dve.tensor_scalar(k.small[:, 2:4], k.small[:, 0:2], 1.0 / D, EPS, ALU.mult, ALU.add))
            dve.wait_ge(k.step["act"], act0 + 1)
            k.then(dve, "dve", dve.reciprocal(k.small[:, 4:6], k.small[:, 2:4]))
            if again:
                dve.memset(k.sums[:, 0, :, 1:4], 0.0)
            dve.wait_ge(*landed)
            for t in range(TT):
                k.then(dve, "dve", dve.scalar_tensor_tensor(k.h[:, t, :], k.h[:, t, :], k.small[:, 4 + t:5 + t],
                                                            gain[:], ALU.mult, ALU.mult))


def start(k, x, consts, cols, rel, onehot, bias_rows, first_tiles, w_low, low):
    nc = k.nc
    s_rel = k.sem("rel_landed")
    s_neg = k.sem("rel_masked")
    s_tab = k.sem("bias_table")
    s_row = k.sem("bias_rows_stored")
    H, N = 16, 3 * P
    bias_row = nc.dram_tensor("bias_row", [H, N], F32, kind="Internal")
    with ExitStack() as tmp:
        relx = k.sb("relx", [33, H], F32, tmp)
        oh = k.sb("onehot_sb", [33, N], F32, tmp)
        table = k.sb("bias_table_sb", [H, N], F32, tmp)
        with nc.Block() as block:
            @block.sync
            def _(sp):
                sp.dma_start(k.h[:], x.rearrange("b (t p) d -> p (b t) d", p=P)).then_inc(k.landed, 16)
                sp.dma_start(k.ident[:], consts[:, C_ID, :]).then_inc(k.landed, 16)
                sp.dma_start(k.consts[:], consts).then_inc(k.landed, 16)
                sp.dma_start(k.cols[:], cols).then_inc(k.landed, 16)
                prefetch(k, sp, first_tiles, 0)
                sp.dma_start(relx[0:32, :], rel).then_inc(s_rel, 16)
                sp.dma_start(oh[:], onehot).then_inc(s_rel, 16)
                low.load(sp, w_low)
                sp.wait_ge(s_tab, 2)
                sp.dma_start(bias_row.ap(), table[:]).then_inc(s_row, 16)
                sp.wait_ge(s_row, 16)
                sp.dma_start(bias_rows.ap(), bass.AP(tensor=bias_row, offset=0, ap=[[0, P], [1, H * N]]))\
                    .then_inc(s_row, 16)
                sp.wait_ge(s_row, 32)
                sp.wait_ge(k.landed, 16 * 4)

            @block.vector
            def _(dve):
                dve.memset(k.small[:, 0:1], 0.0).then_inc(k.unit_used, SLOTS)
                dve.memset(k.small[:, 1:2], 0.0).then_inc(k.act_free, 2)
                dve.memset(k.small[:, 2:3], 0.0).then_inc(k.dve_free, 2)
                dve.memset(relx[32:33, :], NEG).then_inc(s_neg, 1)

            @block.tensor
            def _(pe):
                pe.wait_ge(s_rel, 32)
                pe.wait_ge(s_neg, 1)
                pe.matmul(k.ps[0:H, 7, 0:N], relx[:], oh[:], start=True, stop=True).then_inc(s_tab, 1)

            @block.scalar
            def _(act):
                act.wait_ge(s_tab, 1)
                act.copy(table[:], k.ps[0:H, 7, 0:N]).then_inc(s_tab, 1)


def add_to_stream(k, per_pass=2):
    tb = k.tile

    def columns(m, i):
        return slice((i * per_pass + m) * NT, (i * per_pass + m + 1) * NT)

    def act_evac(act, m, i, bank):
        act.wait_ge(k.dve_free, 2 + tb + m + 1 + i * per_pass)
        for t in range(TT):
            last = act.activation(k.ps[:, 4 + t, :], k.h[:, t, columns(m, i)], ACT.Square,
                                  accum_out=k.sums[:, 0, t, i * per_pass + m:i * per_pass + m + 1])
        return last

    def dve_evac(dve, m, i, bank):
        for t in range(TT):
            at = k.h[:, t, columns(m, i)]
            last = dve.tensor_tensor(at, at, k.ps[:, bank + t, :], ALU.add)
        return last
    return act_evac, dve_evac


def copy_evacs(dst, col):
    def act_evac(act, m, i, bank, ps):
        return act.copy(dst[:, 0, bass.ds(col(m, i), NT)], ps[:, bank, :])

    def dve_evac(dve, m, i, bank, ps):
        return dve.tensor_copy(dst[:, 1, bass.ds(col(m, i), NT)], ps[:, bank + 1, :])
    return act_evac, dve_evac


def ffn1_tiles(w_gate, w_up, hi, lo):
    return [Tile(w_gate, DC, lambda i: i * NT, hi, lo), Tile(w_up, DC, lambda i: i * NT, hi, lo)]


def down_tiles(w_down, hi, lo):
    return [Tile(w_down, HC, lambda i, m=m: i * (2 * NT) + m * NT, hi, lo) for m in range(2)]


def square_tiles(w, chunks, hi, lo):
    return [Tile(w, chunks, lambda i, m=m: i * (2 * NT) + m * NT, hi, lo) for m in range(2)]


def stream_col(m, i):
    return i * (2 * NT) + m * NT


def hidden_transposed(k, hid, hT_hi, hT_lo, t0, hid_ready):
    def pe_hook(pe, i):
        hid_ready(pe, i)
        pe.wait_ge(k.tp_lo, t0 + 2 * i)
        for s in range(2):
            for c in range(2):
                for t in range(TT):
                    at = (2 * s + c) * P
                    last = pe.transpose(k.ps[:, 4 + s, c * T + t * P:c * T + (t + 1) * P], hid[:, t, at:at + P],
                                        k.const(C_ID))
            last.then_inc(k.tp_done, 1)

    def at(i, s):
        return bass.ds(i * (4 * T) + s * 2 * T, 2 * T)

    def act_hook(act, i):
        for s in range(2):
            act.wait_ge(k.tp_done, t0 + 1 + s + 2 * i)
            act.copy(hT_hi.rearrange("p c n -> p (c n)")[:, at(i, s)], k.ps[:, 4 + s, :]).then_inc(k.tp_hi, 1)

    def dve_hook(dve, i):
        for s in range(2):
            dve.wait_ge(k.tp_hi, t0 + 1 + s + 2 * i)
            dve.tensor_tensor(hT_lo.rearrange("p c n -> p (c n)")[:, at(i, s)], k.ps[:, 4 + s, :],
                              hT_hi.rearrange("p c n -> p (c n)")[:, at(i, s)].bitcast(F32), ALU.subtract)\
                .then_inc(k.tp_lo, 1)
    return pe_hook, act_hook, dve_hook


def first_block(k, a, hi, lo, next_tiles):
    nc = k.nc
    w_in = a["w_in"]
    head = [Tile(w_in, DC, lambda i: QA, hi, lo), Tile(w_in, DC, lambda i: OG, hi, lo),
            Tile(w_in, DC, lambda i: OG + NT, hi, lo)]
    body = [Tile(w_in, DC, lambda i, m=m: NT + i * (2 * NT) + m * NT, hi, lo) for m in range(2)]
    with ExitStack() as life:
        og = k.sb("og", [P, TT, 1024], F32, life)
        oa = [k.sb(f"oa_{n}", [P, 8, T], F32R, life) for n in ("hi", "lo")]
        ob = [k.sb(f"ob_{n}", [P, 8, T], F32R, life) for n in ("hi", "lo")]
        merge = [Tile(w_in, DC, lambda i: GA + i * NT, hi, lo), Tile(w_in, DC, lambda i: GB + i * NT, hi, lo),
                 Tile(a["w_proj_a"], 8, lambda i: i * NT, *oa), Tile(a["w_proj_b"], 8, lambda i: i * NT, *ob)]
        out_tiles = square_tiles(a["w_out"], DC, hi, lo)
        ffn_tiles = ffn1_tiles(a["w_ffn_gate"], a["w_ffn_up"], hi, lo)
        with ExitStack() as mid:
            proj = k.sb("proj", [P, TT, GL], F32, mid)
            bias_rows = nc.dram_tensor("bias_rows", [P, 16 * 3 * P], F32, kind="Internal")
            with ExitStack() as early:
                low = Narrow(k, "low", early)
                start(k, a["x"], a["consts"], a["cols"], a["rel_bias"], a["onehot"], bias_rows, head,
                      w_in[:, GL:OG], low)
                mix = Rows(k, early, k.h, DC, lambda c: k.col("g_mix", c), hi, lo, normed=True)

                def act_evac(act, m, i, bank):
                    if m == 0:
                        return act.copy(proj[:, 0, 0:NT], k.ps[:, bank, :])
                    for t in range(TT):
                        last = act.activation(og[:, t, (m - 1) * NT:m * NT], k.ps[:, bank + t, :], ACT.Silu)
                    return last

                def dve_evac(dve, m, i, bank):
                    return dve.tensor_copy(proj[:, 1, 0:NT], k.ps[:, bank + 1, :]) if m == 0 else None
                product(k, "head", head, 1, act_evac, dve_evac, after=body, pool_work=low.pad, rows=[mix],
                        once=[("act", 12, low.split_hi), ("dve", 13, low.split_lo)],
                        pe_last=lambda pe: low.product(pe, hi, lo))

                ae, de = copy_evacs(proj, lambda m, i: NT + i * (2 * NT) + m * NT)
                product(k, "qkv", body, 3, lambda e, m, i, b: ae(e, m, i, b, k.ps),
                        lambda e, m, i, b: de(e, m, i, b, k.ps))
            sliding_window(k, proj, bias_rows, *oa)
            y = gated_linear(k, proj, og, a["w_gate_up"], a["b_gate"], lambda sp: prefetch(k, sp, merge, k.unit))
            linear = Rows(k, mid, y, 8, lambda c: k.col("g_gla", c % 2), *ob)
            merged = k.sb("merged", [P, TT, D], F32, mid)
            sg = k.sb("gates", [P, 2, TT, NT], F32, mid)
            term = k.sb("term", [P, TT, NT], F32, mid)
            term_done = k.sem("merge_term")
            tb = k.tile

            def act_evac(act, m, i, bank):
                if m > 1:
                    return None
                act.wait_ge(k.dve_free, tb + m + 1 + 4 * i)
                return act.activation(sg[:, m, :, :], k.ps[:, bank:bank + 2, :], ACT.Sigmoid)

            def dve_evac(dve, m, i, bank):
                if m < 2:
                    return None
                dve.wait_ge(k.act_free, 2 + tb + m - 1 + 4 * i)
                acc = k.ps[:, bank:bank + 2, :]
                at = merged[:, :, bass.ds(i * NT, NT)]
                if m == 2:
                    return dve.tensor_tensor(at, acc, sg[:, 0, :, :], ALU.mult)
                dve.tensor_tensor(term[:], acc, sg[:, 1, :, :], ALU.mult).then_inc(term_done, 1)
                dve.wait_ge(term_done, 1 + i)
                dve.wait_ge(k.dve_free, 2 + tb + 3 + 4 * i)
                return dve.tensor_tensor(at, at, term[:], ALU.add)
            product(k, "merge", merge, 4, act_evac, dve_evac, after=out_tiles, rows=[linear], rows_at=8,
                    rows_need=(2 * DC + 8) // UC)
            product(k, "out", out_tiles, 2, *add_to_stream(k), after=ffn_tiles,
                    rows=[Rows(k, mid, merged, DC, lambda c: 1.0, hi, lo)])
    with ExitStack() as life:
        hT = [k.sb(f"hT_{n}", [P, HC, T], F32R, life) for n in ("hi", "lo")]
        down = down_tiles(a["w_ffn_down"], *hT)
        with ExitStack() as mid:
            hid = k.sb("hid", [P, TT, NT], F32, mid)
            sg = k.sb("ffn_silu", [P, TT, NT], F32, mid)
            ffn = Rows(k, mid, k.h, DC, lambda c: k.col("g_ffn", c), hi, lo, normed=True, summed=True)
            tb, t0 = k.tile, k.t_done

            def act_evac(act, m, i, bank):
                if m:
                    return None
                act.wait_ge(k.dve_free, tb + 2 + 2 * i)
                return act.activation(sg[:], k.ps[:, bank:bank + 2, :], ACT.Silu)

            def dve_evac(dve, m, i, bank):
                if m == 0:
                    return None
                dve.wait_ge(k.act_free, 2 + tb + 1 + 2 * i)
                dve.wait_ge(k.tp_done, t0 + 2 * i)
                return dve.tensor_tensor(hid[:], k.ps[:, bank:bank + 2, :], sg[:], ALU.mult)
            pe_hook, act_hook, dve_hook = hidden_transposed(
                k, hid, *hT, t0, lambda pe, i: pe.wait_ge(k.dve_free, 2 + tb + 2 + 2 * i))
            product(k, "ffn", ffn_tiles, FF1 // NT, act_evac, dve_evac, after=down, rows=[ffn],
                    hooks=[("pe", 5, pe_hook), ("act", 7, act_hook), ("dve", 8, dve_hook)], hooks_in_next=True)
            k.t_done += 2 * (FF1 // NT)
        gain = k.sb("gain_final1", [P, D], F32, life)
        s_gain = k.sem("gain_final1_landed")
        last = FF1 // NT - 1
        late = [("act", 0, lambda act: act_hook(act, last)), ("dve", 1, lambda dve: dve_hook(dve, last)),
                ("pe_first", 4 * last // UC, lambda pe: pe.wait_ge(k.tp_lo, t0 + 2 * (last + 1)))]
        product(k, "down", down, 2, *add_to_stream(k), after=next_tiles, once=late,
                sp_first=lambda sp: sp.dma_start(gain[:], a["g_final1"]).then_inc(s_gain, 16))
        norm_rows(k, gain, (s_gain, 16), hT[0], True)


SQ, SK, SV, GQ, GK, GV, GZ, GBA = (1024 * n for n in range(8))
HEADS2 = 8


def stick_breaking(k, proj, hi, lo, sp_work):
    nc = k.nc
    G, W = 4, T + P
    scale = float(P) ** -0.5
    names = ("qk", "qT", "kT", "z", "log", "stay", "later", "exponent", "exp", "weights", "out", "hi", "lo")
    s = {n: k.sem(f"stick_{n}") for n in names}
    with ExitStack() as ctx:
        qT = k.sb("stick_qT", [P, G, T], F32, ctx)
        kT = k.sb("stick_kT", [P, G, T], F32, ctx)
        ln = k.sb("stick_ln", [P, G, W], F32, ctx)
        lb = k.sb("stick_lb", [P, G, W], F32, ctx)
        st = k.sb("stick_st", [P, G, W], F32, ctx)
        z0 = k.ps[:, 4:6, :].rearrange("p b (j n) -> p (b j) n", j=2)
        z1 = k.ps[:, 6, :].rearrange("p (j n) -> p j n", j=G)
        before = k.const(C_BEFALL)
        with nc.Block() as block:
            @block.sync
            def _(sp):
                sp_work(sp)

            @block.tensor
            def _(pe):
                for g in range(HEADS2 // G):
                    if g:
                        pe.wait_ge(s["lo"], g)
                    for bank, base in ((0, SQ), (2, SK)):
                        for j in range(G):
                            for t in range(TT):
                                last = pe.transpose(
                                    k.ps[:, bank + j // 2, (j % 2) * T + t * P:(j % 2) * T + (t + 1) * P],
                                    proj[:, t, base + (G * g + j) * P:base + (G * g + j + 1) * P], k.const(C_ID))
                    last.then_inc(s["qk"], 1)
                    pe.wait_ge(s["qT"], g + 1)
                    pe.wait_ge(s["kT"], g + 1)
                    for j in range(G):
                        pe.matmul(z0[:, j, :], kT[:, j, 0:P], qT[:, j, :], start=True, stop=True)
                    for j in range(G):
                        last = pe.matmul(z1[:, j, :], kT[:, j, P:T], qT[:, j, P:T], start=True, stop=True)
                    last.then_inc(s["z"], 1)
                    pe.wait_ge(s["stay"], g + 1)
                    for j in range(G):
                        pe.matmul(z0[:, j, 0:P], k.const(C_AFTALL), st[:, j, 0:P], start=True, stop=True)
                        pe.matmul(z0[:, j, P:T], k.const(C_AFTALL), st[:, j, P:T], start=True, stop=False)
                        pe.matmul(z0[:, j, P:T], k.const(C_ONES), st[:, j, T:W], start=False, stop=True)
                    for j in range(G):
                        last = pe.matmul(z1[:, j, :], k.const(C_AFTALL), st[:, j, T:W], start=True, stop=True)
                    last.then_inc(s["later"], 1)
                    pe.wait_ge(s["weights"], g + 1)
                    for j in range(G):
                        v = [proj[:, t, SV + (G * g + j) * P:SV + (G * g + j + 1) * P] for t in range(TT)]
                        bank, at = j // 2, (j % 2) * T
                        pe.matmul(k.ps[:, bank, at:at + P], v[0], lb[:, j, 0:P], start=True, stop=True)
                        pe.matmul(k.ps[:, bank, at + P:at + T], v[0], lb[:, j, P:T], start=True, stop=False)
                        last = pe.matmul(k.ps[:, bank, at + P:at + T], v[1], lb[:, j, T:W], start=False, stop=True)
                    last.then_inc(s["out"], 1)

            @block.scalar
            def _(act):
                for g in range(HEADS2 // G):
                    act.wait_ge(s["qk"], g + 1)
                    act.activation(qT[:], k.ps[:, 0:2, :].rearrange("p b (j n) -> p (b j) n", j=2), ACT.Copy,
                                   scale=scale).then_inc(s["qT"], 1)
                    act.wait_ge(s["z"], g + 1)
                    if g:
                        act.wait_ge(s["stay"], g)
                    act.activation(ln[:, :, 0:T], z0, ACT.Abs)
                    k.then(act, "act", act.activation(ln[:, :, T:W], z1, ACT.Abs))
                    k.then(act, "act", act.activation(ln[:], ln[:], ACT.Exp, scale=-1.0))
                    act.activation(ln[:], ln[:], ACT.Ln, bias=1.0).then_inc(s["log"], 1)
                    act.wait_ge(s["exponent"], g + 1)
                    act.activation(lb[:], lb[:], ACT.Exp).then_inc(s["exp"], 1)
                    act.wait_ge(s["out"], g + 1)
                    act.copy(hi[:, G * g:G * (g + 1), :], k.ps[:, 0:2, :].rearrange("p b (j n) -> p (b j) n", j=2))\
                        .then_inc(s["hi"], 1)

            @block.vector
            def _(dve):
                for g in range(HEADS2 // G):
                    dve.wait_ge(s["qk"], g + 1)
                    dve.tensor_copy(kT[:], k.ps[:, 2:4, :].rearrange("p b (j n) -> p (b j) n", j=2))\
                        .then_inc(s["kT"], 1)
                    dve.wait_ge(s["log"], g + 1)
                    if g:
                        dve.wait_ge(s["out"], g)
                    for z, a, b in ((z0, 0, T), (z1, T, W)):
                        dve.scalar_tensor_tensor(st[:, :, a:b], z, 0.0, ln[:, :, a:b], ALU.max, ALU.add)
                        last = dve.scalar_tensor_tensor(lb[:, :, a:b], z, 0.0, ln[:, :, a:b], ALU.min, ALU.subtract)
                    k.then(dve, "dve", last)
                    for j in range(G):
                        for a in (0, T):
                            last = dve.tensor_tensor(st[:, j, a:a + P], st[:, j, a:a + P], before, ALU.mult)
                    last.then_inc(s["stay"], 1)
                    dve.wait_ge(s["later"], g + 1)
                    dve.tensor_tensor(lb[:, :, 0:T], lb[:, :, 0:T], z0, ALU.subtract)
                    dve.tensor_tensor(lb[:, :, T:W], lb[:, :, T:W], z1, ALU.subtract).then_inc(s["exponent"], 1)
                    dve.wait_ge(s["exp"], g + 1)
                    for j in range(G):
                        for a in (0, T):
                            last = dve.tensor_tensor(lb[:, j, a:a + P], lb[:, j, a:a + P], before, ALU.mult)
                    last.then_inc(s["weights"], 1)
                    dve.wait_ge(s["hi"], g + 1)
                    dve.tensor_tensor(lo[:, G * g:G * (g + 1), :],
                                      k.ps[:, 0:2, :].rearrange("p b (j n) -> p (b j) n", j=2),
                                      hi[:, G * g:G * (g + 1), :].bitcast(F32), ALU.subtract).then_inc(s["lo"], 1)


def delta_inputs(k, proj, slab, sc, s):
    nc = k.nc
    H = HEADS2
    S0, S1, S2, S3, S4, S5 = (proj[:, :, 1024 * n:1024 * (n + 1)] for n in range(6))
    khat, vbeta, khatT, kbe, A = slab

    def head(x, h, a=0, b=T):
        return x[:, h // 4, (h % 4) * T + a:(h % 4) * T + b]

    with nc.Block() as block:
        @block.tensor
        def _(pe):
            pe.wait_ge(s["ba_in"], 1)
            for t in range(TT):
                last = pe.transpose(k.ps[:, 7, t * 16:(t + 1) * 16], sc["baT"][:, t * P:(t + 1) * P],
                                    k.ident[0:16, 0:16])
            last.then_inc(s["ba_rows"], 1)
            for c in range(12):
                if c >= 4:
                    pe.wait_ge(s["taps"], c - 3)
                for j in range(2):
                    for t in range(TT):
                        last = pe.transpose(k.ps[:, c % 4, j * T + t * P:j * T + (t + 1) * P],
                                            proj[:, t, GQ + (2 * c + j) * P:GQ + (2 * c + j + 1) * P], k.const(C_ID))
                last.then_inc(s["channels"], 1)
            pe.wait_ge(s["squares"], 1)
            for n, x in enumerate((S3, S4)):
                for h in range(H):
                    for t in range(TT):
                        at = n * 16 + t * H + h
                        last = pe.matmul(k.ps[:, 4, at:at + 1], head(x, h, t * P, (t + 1) * P),
                                         k.consts[:, C_ONES, 0:1], start=True, stop=True)
            last.then_inc(s["sums"], 1)
            pe.wait_ge(s["silu"], 2)
            for x, banks in ((S1, (0, 1, 2, 3)), (S2, (5, 6, 7, 0))):
                for n, bank in enumerate(banks):
                    if x is S2 and bank == 0:
                        pe.wait_ge(s["khat"], 1)
                    t, q = n // 2, n % 2
                    for j in range(4):
                        last = pe.transpose(k.ps[:, bank, j * P:(j + 1) * P], head(x, 4 * q + j, t * P, (t + 1) * P),
                                            k.const(C_ID))
                    last.then_inc(s["rows"], 1)
            pe.wait_ge(s["g"], 1)
            pe.wait_ge(s["sums2"], 1)
            for t in range(TT):
                pe.matmul(k.ps[:, 4, 64 + 8 * t:72 + 8 * t], k.const(C_CUM), sc["g"][:, t, :], start=True, stop=True)
                pe.matmul(k.ps[:, 4, 80 + 8 * t:88 + 8 * t], k.const(C_AFT), sc["g"][:, t, :], start=True, stop=True)
            for c in range(4):
                last = pe.matmul(k.ps[:, 4, 96 + 8 * c:104 + 8 * c], k.const(C_HALF + c % 2), sc["g"][:, c // 2, :],
                                 start=True, stop=True)
            last.then_inc(s["gsums"], 1)
            pe.wait_ge(s["khat"], 4)
            for n in range(4):
                if n == 0:
                    pe.wait_ge(s["vbeta"], 4)
                for j in range(2):
                    for t in range(TT):
                        h = 2 * n + j
                        last = pe.transpose(k.ps[:, n, j * T + t * P:j * T + (t + 1) * P],
                                            khat[:, t, h * P:(h + 1) * P], k.const(C_ID))
            last.then_inc(s["khatT"], 1)

        @block.scalar
        def _(act):
            act.wait_ge(k.narrow, k.narrow_done + Narrow.STEPS)
            act.copy(sc["baT"], k.ps[0:16, 7, 0:T]).then_inc(s["ba_in"], 1)
            act.wait_ge(s["ba_rows"], 1)
            ba = k.ps[:, 7, 0:32].rearrange("p (t n) -> p t n", t=TT)
            act.activation(sc["beta"], ba[:, :, 0:8], ACT.Sigmoid).then_inc(s["beta"], 1)
            act.wait_ge(s["x"], 1)
            k.then(act, "act", act.activation(sc["ln"], sc["x"], ACT.Abs))
            k.then(act, "act", act.activation(sc["ln"], sc["ln"], ACT.Exp, scale=-1.0))
            act.activation(sc["ln"], sc["ln"], ACT.Ln, bias=1.0)
            act.activation(sc["ea"], k.col("alog", 0, 8), ACT.Exp).then_inc(s["x"], 1)
            for c in range(12):
                act.wait_ge(s["channels"], c + 1)
                for j in range(2):
                    n = 2 * c + j
                    last = act.activation(head((S0, S1, S2)[n // 8], n % 8), k.ps[:, c % 4, j * T:(j + 1) * T],
                                          ACT.Copy, scale=k.col("conv", 4 * n + 3))
                last.then_inc(s["tap0"], 1)
            act.wait_ge(s["taps"], 12)
            act.activation(S0, S0, ACT.Silu)
            act.activation(S1, S1, ACT.Silu).then_inc(s["silu"], 1)
            act.activation(S2, S2, ACT.Silu).then_inc(s["silu"], 1)
            act.activation(proj[:, :, GZ:GZ + 1024], proj[:, :, GZ:GZ + 1024], ACT.Silu)
            act.wait_ge(s["silu"], 1)
            act.activation(S3, S0, ACT.Square)
            act.activation(S4, S1, ACT.Square).then_inc(s["squares"], 1)
            act.wait_ge(s["sums2"], 1)
            act.activation(sc["norms"], sc["norms"], ACT.Sqrt).then_inc(s["sums2"], 1)
            act.wait_ge(s["gsums"], 1)
            act.activation(sc["exps"], k.ps[:, 4, 64:128], ACT.Exp).then_inc(s["exps"], 1)
            for n in range(4):
                act.wait_ge(s["rows"], 5 + n)
                t, q = n // 2, n % 2
                for j in range(4):
                    h = 4 * q + j
                    last = act.activation(vbeta[:, t, h * P:(h + 1) * P],
                                          k.ps[:, (5, 6, 7, 0)[n], j * P:(j + 1) * P], ACT.Copy,
                                          scale=sc["beta"][:, t, h:h + 1])
                last.then_inc(s["vbeta"], 1)
            act.wait_ge(s["khatT"], 1)
            for n in range(4):
                last = act.copy(khatT[:, n // 2, (n % 2) * 2 * T:(n % 2 + 1) * 2 * T], k.ps[:, n, :])
            last.then_inc(s["ready"], 1)

        @block.vector
        def _(dve):
            dve.wait_ge(s["beta"], 1)
            ba = k.ps[:, 7, 0:32].rearrange("p (t n) -> p t n", t=TT)
            for t in range(TT):
                last = dve.tensor_tensor(sc["x"][:, t, :], ba[:, t, 8:16], k.col("dtb", 0, 8), ALU.add)
            last.then_inc(s["x"], 1)
            dve.wait_ge(s["x"], 2)
            k.then(dve, "dve", dve.scalar_tensor_tensor(sc["x"], sc["x"], 0.0, sc["ln"], ALU.max, ALU.add))
            for t in range(TT):
                last = dve.scalar_tensor_tensor(sc["g"][:, t, :], sc["x"][:, t, :], -1.0, sc["ea"], ALU.mult, ALU.mult)
            last.then_inc(s["g"], 1)
            for c in range(12):
                dve.wait_ge(s["tap0"], c + 1)
                for tap in range(1, 4):
                    for j in range(2):
                        n = 2 * c + j
                        y = head((S0, S1, S2)[n // 8], n % 8, tap, T)
                        last = dve.scalar_tensor_tensor(y, k.ps[:, c % 4, j * T:(j + 1) * T - tap],
                                                        k.col("conv", 4 * n + 3 - tap), y, ALU.mult, ALU.add)
                    if tap < 3:
                        k.then(dve, "dve", last)
                last.then_inc(s["taps"], 1)
            dve.wait_ge(s["sums"], 1)
            dve.tensor_scalar(sc["norms"], k.ps[:, 4, 0:32], EPS, None, ALU.add).then_inc(s["sums2"], 1)
            dve.wait_ge(s["sums2"], 2)
            k.then(dve, "dve", dve.reciprocal(sc["rnorms"], sc["norms"]))
            for n in range(4):
                dve.wait_ge(s["rows"], n + 1)
                t, q = n // 2, n % 2
                for j in range(4):
                    h = 4 * q + j
                    last = dve.tensor_scalar(khat[:, t, h * P:(h + 1) * P], k.ps[:, n, j * P:(j + 1) * P],
                                             sc["rnorms"][:, 16 + t * H + h:17 + t * H + h], None, ALU.mult)
                last.then_inc(s["khat"], 1)
            dve.wait_ge(s["exps"], 1)
            dve.wait_ge(s["beta"], 1)
            dve.wait_ge(s["khat"], 4)
            k.then(dve, "dve", dve.tensor_tensor(sc["be"], sc["beta"],
                                                 sc["exps"][:, 0:16].rearrange("p (t n) -> p t n", t=TT), ALU.mult))
            dve.tensor_scalar(sc["rnorms"][:, 0:16], sc["rnorms"][:, 0:16], float(P) ** -0.5, None, ALU.mult)
            for t in range(TT):
                for h in range(H):
                    at = slice(h * P, (h + 1) * P)
                    dve.tensor_scalar(kbe[:, t, at], khat[:, t, at], sc["be"][:, t, h:h + 1], None, ALU.mult)
                    dve.tensor_scalar(A[:, t, at], k.const(C_AFT), sc["g"][:, t, h:h + 1], None, ALU.mult)
            dve.wait_ge(s["khatT"], 1)
            for t in range(TT):
                for h in range(H):
                    at = slice(h * P, (h + 1) * P)
                    last = dve.tensor_scalar(khat[:, t, at], khat[:, t, at],
                                             sc["exps"][:, 16 + t * H + h:17 + t * H + h], None, ALU.mult)
            last.then_inc(s["ready"], 1)


def delta_matrices(k, proj, slab, sc, s):
    nc = k.nc
    H, NG = HEADS2, 4
    S0, S1, S2, S3, S4, S5 = (proj[:, :, 1024 * n:1024 * (n + 1)] for n in range(6))
    khat, vbeta, khatT, kbe, A = slab
    decT, dec, L, LT, Tm, TmT, Cm, Y, G, ecs = S3, S4, S5, S2, S4, S1, A, khatT, S1, A

    def head(x, h, a=0, b=T):
        return x[:, h // 4, (h % 4) * T + a:(h % 4) * T + b]

    def group(x, g):
        return x[:, g // 2, (g % 2) * 512:(g % 2 + 1) * 512]

    def one(x, g, j):
        return x[:, g // 2, (g % 2) * 512 + j * P:(g % 2) * 512 + (j + 1) * P]

    def each(c):
        return k.const(c).unsqueeze(1).broadcast_to([P, 4, P])

    def four(x):
        return x.rearrange("p (j n) -> p j n", j=4)

    with nc.Block() as block:
        @block.tensor
        def _(pe):
            pe.wait_ge(s["ready"], 2)
            cum = k.const(C_CUM)
            for g in range(NG):
                for j in range(4):
                    last = pe.matmul(k.ps[:, g, j * P:(j + 1) * P], one(A, g, j), cum, start=True, stop=True)
                last.then_inc(s["logT"], 1)
                pe.matmul(k.ps[:, 4 + g, :], cum, group(A, g), start=True, stop=True).then_inc(s["log"], 1)
            for g in range(NG):
                t = g // 2
                pe.wait_ge(s["decT"], g + 1)
                for j in range(4):
                    h = 4 * (g % 2) + j
                    last = pe.matmul(k.ps[:, g, j * P:(j + 1) * P], head(khatT, h, t * P, (t + 1) * P),
                                     head(S0, h, t * P, (t + 1) * P), start=True, stop=True)
                last.then_inc(s["qk"], 1)
            for g in range(NG):
                t = g // 2
                pe.wait_ge(s["dec"], g + 1)
                for j in range(4):
                    h = 4 * (g % 2) + j
                    kk = head(khatT, h, t * P, (t + 1) * P)
                    last = pe.matmul(k.ps[:, 4 + g, j * P:(j + 1) * P], kk, kk, start=True, stop=True)
                last.then_inc(s["kk"], 1)
            for g in range(NG):
                pe.wait_ge(s["attn"], g + 1)
                pe.wait_ge(s["G"], 1)
                for j in range(4):
                    last = pe.matmul(k.ps[:, g, j * P:(j + 1) * P], one(G, g, j), cum, start=True, stop=True)
                last.then_inc(s["cs"], 1)
            for g in range(NG):
                pe.wait_ge(s["L"], g + 1)
                for j in range(4):
                    last = pe.transpose(k.ps[:, 4 + g, j * P:(j + 1) * P], one(L, g, j), k.const(C_ID))
                last.then_inc(s["LT"], 1)
            for g in range(NG):
                pe.wait_ge(s["TT"], g + 1)
                for j in range(4):
                    last = pe.transpose(k.ps[:, g, j * P:(j + 1) * P], one(TmT, g, j), k.const(C_ID))
                last.then_inc(s["T0"], 1)
            for lv in range(1, LEVELS):
                done = (lv - 1) * NG
                for g in range(NG):
                    pe.wait_ge(s["C"], done + g + 1)
                    pe.wait_ge(s["T"], done + g + 1)
                    for j in range(4):
                        last = pe.matmul(k.ps[:, g, j * P:(j + 1) * P], one(Cm, g, j), one(Tm, g, j), start=True,
                                         stop=True)
                    last.then_inc(s["Y"], 1)
                for g in range(NG):
                    pe.wait_ge(s["Ys"], done + g + 1)
                    for j in range(4):
                        last = pe.matmul(k.ps[:, 4 + g, j * P:(j + 1) * P], one(Y, g, j), one(TmT, g, j), start=True,
                                         stop=True)
                    last.then_inc(s["ZT"], 1)
                    if lv < LEVELS - 1:
                        for j in range(4):
                            last = pe.matmul(k.ps[:, g, j * P:(j + 1) * P], one(TmT, g, j), one(Y, g, j), start=True,
                                             stop=True)
                        last.then_inc(s["Z"], 1)
            for g in range(NG):
                t = g // 2
                pe.wait_ge(s["TT"], LEVELS * NG - NG + g + 1)
                for j in range(4):
                    last = pe.matmul(k.ps[:, g, j * P:(j + 1) * P], one(TmT, g, j), one(vbeta, g, j), start=True,
                                     stop=True)
                last.then_inc(s["u"], 1)
                for j in range(4):
                    last = pe.matmul(k.ps[:, 4 + g, j * P:(j + 1) * P], one(kbe, g, j), one(TmT, g, j), start=True,
                                     stop=True)
                last.then_inc(s["w"], 1)

        @block.scalar
        def _(act):
            for g in range(NG):
                act.wait_ge(s["logT"], g + 1)
                act.activation(group(decT, g), k.ps[:, g, :], ACT.Exp).then_inc(s["decT"], 1)
                act.wait_ge(s["log"], g + 1)
                act.activation(group(dec, g), k.ps[:, 4 + g, :], ACT.Exp).then_inc(s["dec"], 1)
            for g in range(NG):
                act.wait_ge(s["cs"], g + 1)
                act.activation(group(ecs, g), k.ps[:, g, :], ACT.Exp).then_inc(s["ecs"], 1)
            for g in range(NG):
                act.wait_ge(s["LT"], g + 1)
                act.copy(group(LT, g), k.ps[:, 4 + g, :]).then_inc(s["LTs"], 1)
            for g in range(NG):
                act.wait_ge(s["T0"], g + 1)
                act.copy(group(Tm, g), k.ps[:, g, :]).then_inc(s["T"], 1)
            for lv in range(1, LEVELS):
                for g in range(NG):
                    act.wait_ge(s["Y"], (lv - 1) * NG + g + 1)
                    act.copy(group(Y, g), k.ps[:, g, :]).then_inc(s["Ys"], 1)
            for g in range(NG):
                act.wait_ge(s["w"], g + 1)
                act.copy(group(S4, g), k.ps[:, 4 + g, :]).then_inc(s["ws"], 1)

        @block.vector
        def _(dve):
            for t in range(TT):
                for h in range(H):
                    last = dve.tensor_scalar(G[:, t, h * P:(h + 1) * P], k.const(C_ONES), sc["g"][:, t, h:h + 1],
                                             None, ALU.mult)
            last.then_inc(s["G"], 1)
            for g in range(NG):
                dve.wait_ge(s["decT"], g + 1)
                last = dve.tensor_tensor(four(group(decT, g)), four(group(decT, g)), each(C_CUM), ALU.mult)
                dve.wait_ge(s["dec"], g + 1)
                last = dve.tensor_tensor(four(group(dec, g)), four(group(dec, g)), each(C_AFT), ALU.mult)
            k.then(dve, "dve", last)
            for g in range(NG):
                dve.wait_ge(s["qk"], g + 1)
                dve.tensor_tensor(group(decT, g), k.ps[:, g, :], group(decT, g), ALU.mult).then_inc(s["attn"], 1)
            for g in range(NG):
                dve.wait_ge(s["kk"], g + 1)
                for j in range(4):
                    h = 4 * (g % 2) + j
                    last = dve.scalar_tensor_tensor(one(L, g, j), k.ps[:, 4 + g, j * P:(j + 1) * P],
                                                    sc["beta"][:, g // 2, h:h + 1], one(dec, g, j), ALU.mult,
                                                    ALU.mult)
                last.then_inc(s["L"], 1)
            for g in range(NG):
                dve.wait_ge(s["ecs"], g + 1)
                t, q = g // 2, g % 2
                qT = S0[:, q, :].rearrange("p (j n) -> p j n", j=4)[:, :, t * P:(t + 1) * P]
                last = dve.tensor_tensor(qT, qT, four(group(ecs, g)), ALU.mult)
            k.then(dve, "dve", last)
            for g in range(NG):
                dve.wait_ge(s["LTs"], g + 1)
                k.then(dve, "dve", dve.tensor_tensor(four(group(TmT, g)), four(group(LT, g)), each(C_LVL), ALU.mult))
                dve.tensor_tensor(four(group(TmT, g)), each(C_ID), four(group(TmT, g)), ALU.subtract)\
                    .then_inc(s["TT"], 1)
            for g in range(NG):
                dve.tensor_tensor(four(group(Cm, g)), four(group(LT, g)), each(C_LVL + 1), ALU.mult)\
                    .then_inc(s["C"], 1)
            for lv in range(1, LEVELS):
                done = (lv - 1) * NG
                for g in range(NG):
                    dve.wait_ge(s["ZT"], done + g + 1)
                    if lv < LEVELS - 1:
                        dve.wait_ge(s["Z"], done + g + 1)
                    dve.wait_ge(s["TT"], done + g + 1)
                    dve.tensor_tensor(group(TmT, g), group(TmT, g), k.ps[:, 4 + g, :], ALU.subtract)\
                        .then_inc(s["TT"], 1)
                    if lv < LEVELS - 1:
                        dve.wait_ge(s["T"], done + g + 1)
                        dve.tensor_tensor(group(Tm, g), group(Tm, g), k.ps[:, g, :], ALU.subtract)\
                            .then_inc(s["T"], 1)
                        dve.tensor_tensor(four(group(Cm, g)), four(group(LT, g)), each(C_LVL + lv + 1), ALU.mult)\
                            .then_inc(s["C"], 1)
            for g in range(NG):
                dve.wait_ge(s["u"], g + 1)
                dve.tensor_copy(group(S5, g), k.ps[:, g, :]).then_inc(s["us"], 1)


def delta_recurrence(k, proj, slab, sc, s, sp_work):
    nc = k.nc
    H = HEADS2
    S0, S1, S2, S3, S4, S5 = (proj[:, :, 1024 * n:1024 * (n + 1)] for n in range(6))
    ktail, vbeta, khatT, kbe, A = slab
    attn, wT, u, vn, o = S3, S4, S5, S2, A
    state = khatT[:, 0, :]

    with nc.Block() as block:
        @block.sync
        def _(sp):
            sp_work(sp)

        @block.tensor
        def _(pe):
            for c in range(4):
                t, p = c // 2, CH * (c % 2)
                rows = slice(p, p + CH)
                if c:
                    pe.wait_ge(s["S"], c)
                    for h in range(H):
                        last = pe.matmul(k.ps[rows, h // 4, (h % 4) * P:(h % 4 + 1) * P],
                                         wT[:, t, h * P + p:h * P + p + CH], state[:, h * P:(h + 1) * P],
                                         start=True, stop=True)
                    last.then_inc(s["wS"], 1)
                    pe.wait_ge(s["o"], c)
                    for h in range(H):
                        q = S0[:, h // 4, (h % 4) * T + c * CH:(h % 4) * T + (c + 1) * CH]
                        last = pe.matmul(k.ps[rows, 6 + h // 4, (h % 4) * P:(h % 4 + 1) * P], q,
                                         state[:, h * P:(h + 1) * P], start=True, stop=True)
                    last.then_inc(s["qS"], 1)
                pe.wait_ge(s["vn"], c + 1)
                if c < 3:
                    for h in range(H):
                        last = pe.matmul(k.ps[:, 4 + h // 4, (h % 4) * P:(h % 4 + 1) * P],
                                         ktail[rows, t, h * P:(h + 1) * P], vn[rows, t, h * P:(h + 1) * P],
                                         start=True, stop=True)
                    last.then_inc(s["kv"], 1)
                for h in range(H):
                    last = pe.matmul(k.ps[rows, 2 + h // 4, (h % 4) * P:(h % 4 + 1) * P],
                                     attn[rows, t, h * P + p:h * P + p + CH], vn[rows, t, h * P:(h + 1) * P],
                                     start=True, stop=True)
                last.then_inc(s["av"], 1)

        @block.scalar
        def _(act):
            for c in range(4):
                t, p = c // 2, CH * (c % 2)
                act.wait_ge(s["av"], c + 1)
                act.copy(o[p:p + CH, t, :], k.ps[p:p + CH, 2:4, :].rearrange("p b n -> p (b n)"))\
                    .then_inc(s["o"], 1)
            act.wait_ge(s["scaled"], 1)
            for t in range(TT):
                for h in range(H):
                    at = slice(h * P, (h + 1) * P)
                    last = act.activation(S1[:, t, at], o[:, t, at], ACT.Square,
                                          accum_out=sc["oss"][:, t * H + h:t * H + h + 1])
            last.then_inc(s["oss"], 1)
            act.wait_ge(s["oss"], 2)
            act.activation(sc["oss"], sc["oss"], ACT.Sqrt).then_inc(s["oss"], 1)

        @block.vector
        def _(dve):
            for c in range(4):
                t, p = c // 2, CH * (c % 2)
                rows = slice(p, p + CH)
                if c == 0:
                    dve.tensor_copy(vn[rows, t, :], u[rows, t, :]).then_inc(s["vn"], 1)
                else:
                    dve.wait_ge(s["wS"], c)
                    dve.tensor_tensor(vn[rows, t, :], u[rows, t, :],
                                      k.ps[rows, 0:2, :].rearrange("p b n -> p (b n)"), ALU.subtract)\
                        .then_inc(s["vn"], 1)
                if c < 3:
                    dve.wait_ge(s["kv"], c + 1)
                    kv = k.ps[:, 4:6, :].rearrange("p b n -> p (b n)")
                    if c == 0:
                        dve.tensor_copy(state, kv).then_inc(s["S"], 1)
                    else:
                        dve.wait_ge(s["qS"], c)
                        dve.wait_ge(s["S"], c)
                        for h in range(H):
                            at = slice(h * P, (h + 1) * P)
                            last = dve.scalar_tensor_tensor(state[:, at], state[:, at],
                                                            sc["exps"][:, 32 + 8 * c + h:33 + 8 * c + h], kv[:, at],
                                                            ALU.mult, ALU.add)
                        last.then_inc(s["S"], 1)
                if c:
                    dve.wait_ge(s["o"], c + 1)
                    dve.wait_ge(s["qS"], c)
                    last = dve.tensor_tensor(o[rows, t, :], o[rows, t, :],
                                             k.ps[rows, 6:8, :].rearrange("p b n -> p (b n)"), ALU.add)
                    last.then_inc(s["oS"], 1)
            dve.wait_ge(s["oS"], 3)
            for t in range(TT):
                for h in range(H):
                    at = slice(h * P, (h + 1) * P)
                    last = dve.tensor_scalar(o[:, t, at], o[:, t, at], sc["rnorms"][:, t * H + h:t * H + h + 1], None,
                                             ALU.mult)
            last.then_inc(s["scaled"], 1)
            dve.wait_ge(s["oss"], 1)
            dve.tensor_scalar(sc["oss"], sc["oss"], 1.0 / P, EPS, ALU.mult, ALU.add).then_inc(s["oss"], 1)
            dve.wait_ge(s["oss"], 3)
            k.then(dve, "dve", dve.reciprocal(sc["orn"], sc["oss"]))
            for t in range(TT):
                for h in range(H):
                    at = slice(h * P, (h + 1) * P)
                    last = dve.scalar_tensor_tensor(o[:, t, at], o[:, t, at], sc["orn"][:, t * H + h:t * H + h + 1],
                                                    proj[:, t, GZ + h * P:GZ + (h + 1) * P], ALU.mult, ALU.mult)
            k.then(dve, "dve", last)
    return o


def gated_delta(k, ctx, proj, sp_work):
    names = ("ba_in", "ba_rows", "taps", "channels", "squares", "sums", "silu", "khat", "vbeta", "rows", "g", "gsums", "khatT", "beta",
             "x", "tap0", "sums2", "exps", "ready", "logT", "log", "decT", "dec", "qk", "kk", "attn", "G", "cs",
             "L", "LT", "TT", "T0", "C", "T", "Y", "Ys", "ZT", "Z", "u", "w", "ecs", "LTs", "us", "ws", "S", "wS",
             "o", "qS", "vn", "kv", "av", "scaled", "oss", "oS")
    s = {n: k.sem(f"delta_{n}") for n in names}
    slab = [k.sb(f"delta_{n}", [P, TT, 1024], F32, ctx) for n in ("khat", "vbeta", "khatT", "kbe", "A")]
    sc = {}
    for n, shape in (("beta", [TT, 8]), ("x", [TT, 8]), ("ln", [TT, 8]), ("g", [TT, 8]), ("be", [TT, 8]),
                     ("ea", [8]), ("norms", [32]), ("rnorms", [32]), ("exps", [64]), ("oss", [16]), ("orn", [16])):
        sc[n] = k.sb(f"delta_s_{n}", [P, *shape], F32, ctx)[:]
    sc["baT"] = k.sb("delta_s_baT", [16, T], F32, ctx)[:]
    delta_inputs(k, proj, slab, sc, s)
    delta_matrices(k, proj, slab, sc, s)
    k.narrow_done += Narrow.STEPS
    return delta_recurrence(k, proj, slab, sc, s, sp_work)


def memory_attention(k, q, kv, xa_hi, xa_lo, sp_work):
    nc = k.nc
    H = 4
    scale = float(P) ** -0.5
    s = {n: k.sem(f"mem_{n}") for n in ("qk", "qT", "kT", "scored", "neg", "exp", "normed", "pt", "ptc", "out", "hi",
                                        "lo")}
    with ExitStack() as ctx:
        qT = k.sb("mem_qT", [P, H, T], F32, ctx)
        kT = k.sb("mem_kT", [P, H, T], F32, ctx)
        pr = k.sb("mem_p", [P, 2 * H, T], F32, ctx)
        pt = k.sb("mem_pT", [P, 2 * H, T], F32, ctx)
        st = k.sb("mem_st", [P, 4, 2 * H], F32, ctx)
        with nc.Block() as block:
            @block.sync
            def _(sp):
                sp_work(sp)

            @block.tensor
            def _(pe):
                for bank, x in ((0, q), (2, kv)):
                    for h in range(H):
                        for t in range(TT):
                            last = pe.transpose(
                                k.ps[:, bank + h // 2, (h % 2) * T + t * P:(h % 2) * T + (t + 1) * P],
                                x[:, t, h * P:(h + 1) * P], k.const(C_ID))
                last.then_inc(s["qk"], 1)
                pe.wait_ge(s["qT"], 1)
                pe.wait_ge(s["kT"], 1)
                for h in range(H):
                    for t in range(TT):
                        last = pe.matmul(k.ps[:, 4 + h, t * T:(t + 1) * T], qT[:, h, t * P:(t + 1) * P], kT[:, h, :],
                                         start=True, stop=True)
                last.then_inc(s["scored"], 1)
                pe.wait_ge(s["normed"], 1)
                for h in range(H):
                    for m in range(TT):
                        for t in range(TT):
                            last = pe.transpose(k.ps[:, h, m * T + t * P:m * T + (t + 1) * P],
                                                pr[:, TT * h + t, m * P:(m + 1) * P], k.const(C_ID))
                last.then_inc(s["pt"], 1)
                pe.wait_ge(s["ptc"], 2)
                for h in range(H):
                    for m in range(TT):
                        last = pe.matmul(k.ps[:, 4 + h // 2, (h % 2) * T:(h % 2 + 1) * T],
                                         kv[:, m, 512 + h * P:512 + (h + 1) * P], pt[:, TT * h + m, :],
                                         start=(m == 0), stop=(m == 1))
                last.then_inc(s["out"], 1)

            @block.scalar
            def _(act):
                act.wait_ge(s["qk"], 1)
                act.activation(qT[:], k.ps[:, 0:2, :].rearrange("p b (j n) -> p (b j) n", j=2), ACT.Copy,
                               scale=scale).then_inc(s["qT"], 1)
                act.wait_ge(s["neg"], 1)
                for n in range(2 * H):
                    last = act.activation(pr[:, n, :], k.ps[:, 4 + n // 2, (n % 2) * T:(n % 2 + 1) * T], ACT.Exp,
                                          bias=st[:, 1, n:n + 1], accum_out=st[:, 2, n:n + 1])
                last.then_inc(s["exp"], 1)
                act.wait_ge(s["pt"], 1)
                act.copy(pt[:, 0:4, :], k.ps[:, 0:2, :].rearrange("p b (j n) -> p (b j) n", j=2))\
                    .then_inc(s["ptc"], 1)
                act.wait_ge(s["out"], 1)
                act.copy(xa_hi[:], k.ps[:, 4:6, :].rearrange("p b (j n) -> p (b j) n", j=2)).then_inc(s["hi"], 1)

            @block.vector
            def _(dve):
                dve.wait_ge(s["qk"], 1)
                dve.tensor_copy(kT[:], k.ps[:, 2:4, :].rearrange("p b (j n) -> p (b j) n", j=2)).then_inc(s["kT"], 1)
                dve.wait_ge(s["scored"], 1)
                k.then(dve, "dve", dve.tensor_reduce(st[:, 0, :],
                                                     k.ps[:, 4:8, :].rearrange("p b (j n) -> p (b j) n", j=2), AX.X,
                                                     ALU.max))
                dve.tensor_scalar(st[:, 1, :], st[:, 0, :], -1.0, None, ALU.mult).then_inc(s["neg"], 1)
                dve.wait_ge(s["exp"], 1)
                k.then(dve, "dve", dve.reciprocal(st[:, 3, :], st[:, 2, :]))
                for n in range(2 * H):
                    last = dve.tensor_scalar(pr[:, n, :], pr[:, n, :], st[:, 3, n:n + 1], None, ALU.mult)
                last.then_inc(s["normed"], 1)
                dve.wait_ge(s["pt"], 1)
                dve.tensor_copy(pt[:, 4:8, :], k.ps[:, 2:4, :].rearrange("p b (j n) -> p (b j) n", j=2))\
                    .then_inc(s["ptc"], 1)
                dve.wait_ge(s["hi"], 1)
                dve.tensor_tensor(xa_lo[:], k.ps[:, 4:6, :].rearrange("p b (j n) -> p (b j) n", j=2),
                                  xa_hi[:].bitcast(F32), ALU.subtract).then_inc(s["lo"], 1)


def conv_hidden(k, stage, cv, hT_hi, hT_lo, tb):
    s = {n: k.sem(f"ffn2_{n}") for n in ("turned", "tap0", "tap1", "taps", "silu", "hid", "hi", "lo")}
    flat_hi, flat_lo = (x.rearrange("p c n -> p (c n)") for x in (hT_hi, hT_lo))
    at0 = COLS["fconv"][0]

    def weight(i, n, tap):
        return k.cols[:, bass.ds(at0 + 3 * ((n // 4) * HC + n % 4) + tap + i * 12, 1)]

    def bias(i, n):
        return k.cols[:, bass.ds(COLS["fbias"][0] + (n // 4) * HC + n % 4 + i * 4, 1)]

    def pe_hook(pe, i):
        pe.wait_ge(k.act_free, 2 + tb + 1 + 2 * i)
        pe.wait_ge(k.dve_free, 2 + tb + 2 + 2 * i)
        pe.wait_ge(s["taps"], 4 * i)
        for b in range(4):
            for j in range(2):
                c = 2 * (b % 2) + j
                for t in range(TT):
                    last = pe.transpose(k.ps[:, 4 + b, j * T + t * P:j * T + (t + 1) * P],
                                        stage[:, b // 2, t, c * P:(c + 1) * P], k.ident[:])
        last.then_inc(s["turned"], 1)

    def tap0(b):
        def hook(act, i):
            if b == 0:
                act.wait_ge(s["turned"], 1 + i)
                act.wait_ge(s["lo"], i)
            for n in (2 * b, 2 * b + 1):
                last = act.activation(cv[:, n, :], k.ps[:, 4 + n // 2, (n % 2) * T:(n % 2 + 1) * T], ACT.Identity,
                                      scale=weight(i, n, 2), bias=bias(i, n))
            last.then_inc(s["tap0"], 1)
        return hook

    def taps(b):
        def hook(dve, i):
            dve.wait_ge(s["tap0"], 1 + b + 4 * i)
            for tap, sem in ((1, "tap1"), (2, "taps")):
                for n in (2 * b, 2 * b + 1):
                    y = cv[:, n, tap:T]
                    last = dve.scalar_tensor_tensor(y, k.ps[:, 4 + n // 2, (n % 2) * T:(n % 2 + 1) * T - tap],
                                                    weight(i, n, 2 - tap), y, ALU.mult, ALU.add)
                last.then_inc(s[sem], 1)
                if tap == 1:
                    dve.wait_ge(s["tap1"], 1 + b + 4 * i)
        return hook

    def silu(act, i):
        act.wait_ge(s["taps"], 2 + 4 * i)
        act.activation(cv[:, 0:4, :], cv[:, 0:4, :], ACT.Silu).then_inc(s["silu"], 1)

    def mult(dve, i):
        dve.wait_ge(s["silu"], 1 + i)
        dve.wait_ge(s["taps"], 4 + 4 * i)
        dve.tensor_tensor(cv[:, 0:4, :], cv[:, 0:4, :], cv[:, 4:8, :], ALU.mult).then_inc(s["hid"], 1)

    def part(x, i):
        return x[:, bass.ds(i * (4 * T), 4 * T)]

    def high(act, i):
        act.wait_ge(s["hid"], 1 + i)
        act.copy(part(flat_hi, i), cv[:, 0:4, :].rearrange("p c n -> p (c n)")).then_inc(s["hi"], 1)

    def low(dve, i):
        dve.wait_ge(s["hi"], 1 + i)
        dve.tensor_tensor(part(flat_lo, i), cv[:, 0:4, :].rearrange("p c n -> p (c n)"),
                          part(flat_hi, i).bitcast(F32), ALU.subtract).then_inc(s["lo"], 1)
    return s, [("pe", 5, pe_hook)] + [("act", 7 + b, tap0(b)) for b in range(4)] \
        + [("dve", 8 + b, taps(b)) for b in range(4)] \
        + [("act", 12, silu), ("dve", 13, mult), ("act", 14, high), ("dve", 15, low)]


def in2_tiles(w, hi, lo):
    return [Tile(w, DC, lambda i, m=m: i * (2 * NT) + m * NT, hi, lo) for m in range(2)]


def second_block_mix(k, a, hi, lo, xq_tiles_of):
    nc = k.nc
    tiles = in2_tiles(a["w_in_2"], hi, lo)
    out_tiles = square_tiles(a["w_out_2"], DC, hi, lo)
    with ExitStack() as life:
        proj = k.sb("proj2", [P, TT, 7 * 1024], F32, life)
        with ExitStack() as mid:
            low = Narrow(k, "low2", mid)
            mix = Rows(k, mid, k.h, DC, lambda c: k.col("g_mix2", c), hi, lo, normed=True, summed=True)
            ae, de = copy_evacs(proj, stream_col)
            product(k, "in2", tiles, 7, lambda e, m, i, b: ae(e, m, i, b, k.ps), lambda e, m, i, b: de(e, m, i, b, k.ps),
                    sp_first=lambda sp: low.load(sp, a["w_in_2"][:, GBA:GBA + 16]), pool_work=low.pad, rows=[mix],
                    once=[("act", 12, low.split_hi), ("dve", 13, low.split_lo)],
                    pe_last=lambda pe: low.product(pe, hi, lo))
        stick_breaking(k, proj, hi, lo, lambda sp: prefetch(k, sp, out_tiles, k.unit))
        delta = Rows(k, life, gated_delta(k, life, proj, lambda sp: None), HEADS2, lambda c: k.col("g_gdn"),
                     hi[:, 8:16, :], lo[:, 8:16, :])
        product(k, "out2", out_tiles, 2, *add_to_stream(k), after=xq_tiles_of, rows=[delta],
                rows_need=8 // UC)


def second_block_memory(k, a, hi, lo, mem_parts, xq_tiles, next_tiles):
    nc = k.nc
    m_hi, m_lo = mem_parts
    with ExitStack() as life:
        q = k.sb("mem_q", [P, TT, 512], F32, life)
        kv = k.sb("mem_kv", [P, TT, 1024], F32, life)
        xa = [k.sb(f"xa_{n}", [P, 4, T], F32R, life) for n in ("hi", "lo")]
        xo_tiles = [Tile(a["w_xo_2"], 4, lambda i, m=m: m * NT, *xa) for m in range(4)]
        mem_landed = k.sem("mem_landed")
        mem = k.sb("mem_rows", [P, TT, D], F32, life)
        rows = [Rows(k, life, k.h, DC, lambda c: k.col("g_x2", c), hi, lo, normed=True, summed=True),
                Rows(k, life, mem, DC, lambda c: k.col("g_mem2", c), m_hi, m_lo, normed=True, landed=mem_landed,
                     which=1)]

        def act_evac(act, m, i, bank):
            dst = q[:, 0, :] if m == 0 else kv[:, 0, (m - 1) * NT:m * NT]
            return act.copy(dst, k.ps[:, bank, :])

        def dve_evac(dve, m, i, bank):
            dst = q[:, 1, :] if m == 0 else kv[:, 1, (m - 1) * NT:m * NT]
            return dve.tensor_copy(dst, k.ps[:, bank + 1, :])
        product(k, "xqkv", xq_tiles, 1, act_evac, dve_evac, rows=rows, sp_first=lambda sp: sp.dma_start(
            mem[:], a["mem_2"].rearrange("b (t p) d -> p (b t) d", p=P)).then_inc(mem_landed, 16))
        memory_attention(k, q, kv, *xa, lambda sp: prefetch(k, sp, xo_tiles, k.unit))
        product(k, "xo", xo_tiles, 1, *add_to_stream(k, 4), after=next_tiles)


def second_block_ffn(k, a, out, hi, lo, tiles):
    nc = k.nc
    with ExitStack() as life:
        hT = [k.sb(f"hT2_{n}", [P, HC, T], F32R, life) for n in ("hi", "lo")]
        cv = k.sb("ffn2_conv", [P, 8, T], F32, life)
        down = down_tiles(a["w_down_2"], *hT)
        with ExitStack() as mid:
            stage = k.sb("ffn2_rows", [P, 2, TT, NT], F32, mid)
            ffn = Rows(k, mid, k.h, DC, lambda c: k.col("g_ffn2", c), hi, lo, normed=True, summed=True)
            tb = k.tile
            s, hooks = conv_hidden(k, stage, cv, *hT, tb)

            def act_evac(act, m, i, bank):
                if m:
                    return None
                act.wait_ge(s["turned"], i)
                return act.copy(stage[:, 0], k.ps[:, bank:bank + 2, :])

            def dve_evac(dve, m, i, bank):
                if m == 0:
                    return None
                dve.wait_ge(s["turned"], i)
                return dve.tensor_copy(stage[:, 1], k.ps[:, bank:bank + 2, :])
            product(k, "ffn2", tiles, FF2 // NT, act_evac, dve_evac, after=down, hooks=hooks, rows=[ffn], hooks_in_next=True)
        gain = k.sb("gain_final2", [P, D], F32, life)
        s_gain, s_out = k.sem("gain_final2_landed"), k.sem("stored")
        last = FF2 // NT - 1
        late = [(e, u - 7, lambda eng, fn=fn: fn(eng, last)) for e, u, fn in hooks if e != "pe"]
        late.append(("pe_first", 4 * last // UC, lambda pe: pe.wait_ge(s["lo"], last + 1)))
        product(k, "down2", down, 2, *add_to_stream(k), once=late,
                sp_first=lambda sp: sp.dma_start(gain[:], a["g_final2"]).then_inc(s_gain, 16))
        norm_rows(k, gain, (s_gain, 16), hT[0], False)
        with nc.Block() as block:
            @block.sync
            def _(sp):
                sp.dma_start(out.rearrange("b (t p) d -> p (b t) d", p=P), k.h[:]).then_inc(s_out, 16)
                sp.wait_ge(s_out, 16)


def build_program(nc, a, out):
    with ExitStack() as ctx:
        k = Kernel(nc, ctx)
        hi = k.sb("act_hi", [P, DC, T], F32R)
        lo = k.sb("act_lo", [P, DC, T], F32R)
        tiles2 = in2_tiles(a["w_in_2"], hi, lo)
        up_tiles = [Tile(a["w_up_2"], DC, lambda i, m=m: i * NT + m * FF2, hi, lo) for m in range(2)]
        with ExitStack() as masks:
            k.consts = k.sb("masks", [P, N_CONST, P], F32, masks)
            first_block(k, a, hi, lo, tiles2)
            with ExitStack() as late:
                q_tiles = [Tile(a["w_xq_2"], DC, lambda i: 0, hi, lo)]
                m_parts = [None, None]

                class Later(Tile):
                    pass
                kv_tiles = [Later(a["w_xkv_2"], DC, lambda i, m=m: m * NT, None, None) for m in range(2)]
                second_block_mix(k, a, hi, lo, q_tiles + kv_tiles)
                m_parts = [k.sb(f"memT_{n}", [P, DC, T], F32R, late) for n in ("hi", "lo")]
                for t in kv_tiles:
                    t.hi, t.lo = m_parts
                second_block_memory(k, a, hi, lo, m_parts, q_tiles + kv_tiles, up_tiles)
        second_block_ffn(k, a, out, hi, lo, up_tiles)




def _masks():
    import numpy as np
    c = np.zeros((P, N_CONST, P), np.float32)
    r, q = np.arange(P)[:, None], np.arange(P)[None, :]
    same = r // CH == q // CH
    c[:, C_ID] = r == q
    c[:, C_CUM] = (r <= q) & same
    c[:, C_AFT] = (r > q) & same
    c[:, C_AFTALL] = r > q
    c[:, C_BEFALL] = r < q
    c[:, C_ONES] = 1
    c[:CH, C_HALF] = 1
    c[CH:, C_HALF + 1] = 1
    for level in range(LEVELS):
        s = 1 << level
        c[:, C_LVL + level] = (r // (2 * s) == q // (2 * s)) & (r // s % 2 == 0) & (q // s % 2 == 1)
    return c


def _buckets():
    import math

    import numpy as np
    o = np.zeros((33, 3 * P), np.float32)
    for n in range(3 * P):
        d = 2 * P - 1 - n
        if d < 0 or d >= P:
            o[32, n] = 1
        elif d < 16:
            o[d, n] = 1
        else:
            o[min(31, 16 + int(math.log(d / 16) / math.log(8) * 16)), n] = 1
    return o


def kernel(**inputs):
    import numpy as np
    import concourse.bacc as bacc
    from concourse.bass_utils import run_bass_kernel_spmd

    v = {n: np.asarray(x) for n, x in inputs.items()}

    def chunks(x):
        return x.reshape(-1, P).T

    def every(x):
        return np.broadcast_to(x.reshape(1, -1), (P, x.size))
    parts = {
        "g_mix": chunks(v["norm_mix_g"]), "g_ffn": chunks(v["norm_ffn_g"]), "g_mix2": chunks(v["mix_norm_2"]),
        "g_x2": chunks(v["xattn_norm_2"]), "g_mem2": chunks(v["mem_norm_2"]), "g_ffn2": chunks(v["ffn_norm_2"]),
        "g_gla": chunks(v["gla_norm_g"]), "g_gdn": chunks(v["gdn_norm_2"]),
        "conv": v["gdn_conv_2"].reshape(4, 24, P).transpose(2, 1, 0).reshape(P, 96),
        "fconv": v["ffn_conv_2"].reshape(3, 88, P).transpose(2, 1, 0).reshape(P, 264),
        "fbias": chunks(v["ffn_conv_bias_2"]),
        "sinks": every(v["sinks"]), "alog": every(v["gdn_a_log_2"]), "dtb": every(v["gdn_dt_bias_2"]),
    }
    given = {"consts": _masks(), "onehot": _buckets(),
             "cols": np.ascontiguousarray(np.concatenate([parts[n] for n in COLS], 1)),
             "g_final1": np.ascontiguousarray(every(v["norm_final_g"])),
             "g_final2": np.ascontiguousarray(every(v["final_norm_2"])),
             "x": v["x"], "mem_2": v["mem_2"], "rel_bias": v["rel_bias"], "b_gate": v["b_gate"]}
    for n in ("w_in", "w_gate_up", "w_proj_a", "w_proj_b", "w_out", "w_ffn_gate", "w_ffn_up", "w_ffn_down",
              "w_in_2", "w_out_2", "w_xq_2", "w_xkv_2", "w_xo_2", "w_up_2", "w_down_2"):
        given[n] = v[n][0]
    nc = bacc.Bacc("TRN2", target_bir_lowering=False, num_devices=1)
    arrays, a = {}, {}
    for n, x in given.items():
        arrays[f"in_{n}"] = np.ascontiguousarray(x)
        a[n] = nc.dram_tensor(f"in_{n}", x.shape, mybir.dt.from_np(x.dtype), kind="ExternalInput").ap()
    out = nc.dram_tensor("out_0", (1, T, D), F32, kind="ExternalOutput").ap()
    build_program(nc, a, out)
    r = run_bass_kernel_spmd(nc, [arrays], core_ids=[0])
    return r.results[0]["out_0"]
```

```python
from contextlib import ExitStack

import concourse.bass as bass
from concourse import mybir

ALU = mybir.AluOpType
ACT = mybir.ActivationFunctionType
AX = mybir.AxisListType
F32 = mybir.dt.float32
F32R = mybir.dt.float32r

P = 128
T = 256
TT = T // P
D = 2048
DC = D // P
NT = 512
UC = 2
SLOTS = 4
LATE = 3
EPS = 1e-6
FF1, FF2 = 5632, 5632
HC = FF1 // P
NEG = -1e30
BIG = 3e38

QA, KA, VA, QB, KB, VB, GL, OG, GA, GB = 0, 1024, 1280, 1536, 2048, 2560, 3584, 3600, 4624, 6672
C_ID, C_CUM, C_AFT, C_AFTALL, C_BEFALL, C_ONES, C_HALF, C_LVL = 0, 1, 2, 3, 4, 5, 6, 8
LEVELS = 6
N_CONST = C_LVL + LEVELS
CH = 64

COLS = {}
_at = 0
for _name, _n in (("g_mix", DC), ("g_ffn", DC), ("g_mix2", DC), ("g_x2", DC), ("g_mem2", DC), ("g_ffn2", DC),
                  ("g_gla", 2), ("g_gdn", 1), ("conv", 96), ("fconv", 264), ("fbias", 88),
                  ("sinks", 16), ("alog", 8), ("dtb", 8)):
    COLS[_name] = (_at, _n)
    _at += _n
N_COLS = _at


def loop(eng, first, last, body):
    if last - first == 1:
        body(first)
    elif last > first:
        with eng.Fori(first, last) as i:
            body(i)


class Kernel:

    def __init__(self, nc, ctx):
        self.nc, self.ctx = nc, ctx
        self.unit = 0
        self.tile = 0
        self.steps = {"act": 0, "dve": 0, "pool": 0}
        self.t_done = 0
        self.n_sem = 0
        self.ring = self.sb("ring", [P, SLOTS, UC, NT], F32)
        self.w_hi = self.sb("w_hi", [P, SLOTS, UC, NT], F32R)
        self.w_lo = self.sb("w_lo", [P, SLOTS, UC, NT], F32R)
        self.h = self.sb("h", [P, TT, D], F32)
        self.ident = self.sb("ident", [P, P], F32)
        self.consts = None
        self.cols = self.sb("cols", [P, N_COLS], F32)
        self.small = self.sb("small", [P, 64], F32)
        self.ps = ctx.enter_context(nc.psum_tensor("ps", [P, 8, NT], F32))
        self.w_arrived = [self.sem(f"w_arrived{s}") for s in range(SLOTS)]
        self.hi_ready = self.sem("hi_ready")
        self.lo_ready = self.sem("lo_ready")
        self.unit_used = self.sem("unit_used")
        self.act_free = self.sem("act_free")
        self.dve_free = self.sem("dve_free")
        self.step = {e: self.sem(f"{e}_step") for e in self.steps}
        self.tp_done = self.sem("tp_done")
        self.tp_hi = self.sem("tp_hi")
        self.tp_lo = self.sem("tp_lo")
        self.narrow = self.sem("narrow")
        self.narrow_done = 0
        self.rms = self.sem("rms")
        self.rms_done = 0
        self.sums = self.sb("sums", [P, 2, TT, 4], F32)
        self.ahead = 0
        self.landed = self.sem("landed")

    def sb(self, name, shape, dt=F32, ctx=None):
        return (ctx or self.ctx).enter_context(self.nc.sbuf_tensor(name, shape, dt))

    def sem(self, name):
        self.n_sem += 1
        return self.ctx.enter_context(self.nc.semaphore(name))

    def const(self, c):
        return self.ident[:] if c == C_ID else self.consts[:, c, :]

    def col(self, name, i=0, n=1):
        at = COLS[name][0] + i
        return self.cols[:, at:at + n]

    def then(self, eng, key, ins):
        self.steps[key] += 1
        ins.then_inc(self.step[key], 1)
        eng.wait_ge(self.step[key], self.steps[key])


def weight_unit(w, row, col):
    return w[row:row + UC * P, bass.ds(col, NT)].rearrange("(c p) n -> p c n", p=P)


class Tile:

    def __init__(self, w, chunks, col, hi, lo, rows=0):
        self.w, self.chunks, self.col, self.hi, self.lo, self.rows = w, chunks, col, hi, lo, rows


def ahead_hi(k, act):
    for u in range(SLOTS):
        split_hi(k, act, u, k.unit + u)


def ahead_lo(k, dve):
    for u in range(SLOTS):
        split_lo(k, dve, u, k.unit + u)
    k.ahead = SLOTS


def load_unit(k, sp, tiles, i, u):
    n = u
    for tile in tiles:
        if n < tile.chunks // UC:
            break
        n -= tile.chunks // UC
    sp.dma_start(k.ring[:, u % SLOTS], weight_unit(tile.w, tile.rows + n * UC * P, tile.col(i)))\
        .then_inc(k.w_arrived[u % SLOTS], 16)


def prefetch(k, sp, tiles, base):
    for u in range(SLOTS):
        if base:
            sp.wait_ge(k.lo_ready, base + u - SLOTS + 1)
        load_unit(k, sp, tiles, 0, u)


class Rows:

    def __init__(self, k, ctx, src, chunks, gain, hi, lo, normed=False, landed=None, summed=False,
                 which=0, tail=None):
        self.k, self.src, self.pairs, self.gain, self.hi, self.lo, self.normed = k, src, chunks // 2, gain, hi, lo, normed
        self.summed, self.sums = summed, k.sums[:, which]
        self.tail = tail
        self.landed = landed
        k.t_done += self.pairs
        if normed:
            self.rms0 = k.rms_done
            k.rms_done += 4 if summed else 5
            self.rms_ready = (k.rms, self.rms0 + 4)
            self.stat = k.sb(f"rms_stat{self.rms0}", [P, 3, TT], F32, ctx)
            if not summed:
                self.diag = k.sb(f"rms_diag{self.rms0}", [P, TT, P], F32, ctx)

    def scale(self, t):
        return self.stat[:, 2, t:t + 1]

    def stats_act(self, act):
        k = self.k
        if self.tail:
            return self.tail[0](act)
        if not self.summed:
            for t in range(TT):
                act.wait_ge(self.landed[t], 16)
                last = act.activation(self.hi[:, t * 8:(t + 1) * 8, :].rearrange("p c n -> p (c n)"),
                                      self.src[:, t, :], ACT.Square, accum_out=self.sums[:, t, 0:1])
            last.then_inc(k.rms, 1)
            act.wait_ge(k.landed, 32)
        act.wait_ge(k.rms, self.rms0 + 2)
        act.activation(self.stat[:, 1, :], self.stat[:, 1, :], ACT.Sqrt).then_inc(k.rms, 1)

    def stats_dve(self, dve):
        k = self.k
        if self.tail:
            return self.tail[1](dve)
        if self.summed:
            dve.tensor_reduce(self.stat[:, 0, :], self.sums, AX.X, ALU.add).then_inc(k.rms, 1)
        dve.wait_ge(k.rms, self.rms0 + 1)
        sums = self.stat[:, 0, :] if self.summed else self.sums[:, :, 0]
        dve.tensor_scalar(self.stat[:, 1, :], sums, 1.0 / D, EPS, ALU.mult, ALU.add).then_inc(k.rms, 1)
        dve.wait_ge(k.rms, self.rms0 + 3)
        dve.reciprocal(self.stat[:, 2, :], self.stat[:, 1, :]).then_inc(k.rms, 1)
        dve.wait_ge(k.rms, self.rms0 + 4)
        if self.summed:
            return
        dve.wait_ge(k.landed, 32)
        for t in range(TT):
            last = dve.tensor_scalar(self.diag[:, t, :], k.ident[:], self.stat[:, 2, t:t + 1], None, ALU.mult)
        last.then_inc(k.rms, 1)

    def pair_pe(self, pe, s, bank):
        k = self.k
        if self.tail and s == 0:
            pe.wait_ge(*self.tail[2])
        if self.normed and not self.summed and s == 0:
            pe.wait_ge(k.rms, self.rms0 + 5)
        for c in range(2):
            for t in range(TT):
                out = k.ps[:, bank, c * T + t * P:c * T + (t + 1) * P]
                one = self.src[:, t, (2 * s + c) * P:(2 * s + c + 1) * P]
                if self.normed and not self.summed:
                    last = pe.matmul(out, one, self.diag[:, t, :], start=True, stop=True)
                else:
                    last = pe.transpose(out, one, k.ident[:])
        last.then_inc(k.tp_done, 1)

    def pair_act(self, act, s, bank):
        for c in range(2):
            at = 2 * s + c
            last = act.activation(self.hi[:, at, :], self.k.ps[:, bank, c * T:(c + 1) * T], ACT.Copy,
                                  scale=self.gain(at))
        last.then_inc(self.k.tp_hi, 1)

    def pair_dve(self, dve, s, bank):
        for c in range(2):
            at = 2 * s + c
            last = dve.scalar_tensor_tensor(self.lo[:, at, :], self.k.ps[:, bank, c * T:(c + 1) * T], self.gain(at),
                                            self.hi[:, at, :].bitcast(F32), ALU.mult, ALU.subtract)
        last.then_inc(self.k.tp_lo, 1)


def split_hi(k, act, s, count, more=0):
    act.wait_ge(k.w_arrived[s], 16 * (count // SLOTS + 1) + more * 16 // SLOTS)
    act.wait_ge(k.unit_used, count + 1 + more)
    act.copy(k.w_hi[:, s], k.ring[:, s]).then_inc(k.hi_ready, 1)


def split_lo(k, dve, s, count, more=0):
    dve.wait_ge(k.hi_ready, count + 1 + more)
    dve.tensor_tensor(k.w_lo[:, s], k.ring[:, s], k.w_hi[:, s].bitcast(F32), ALU.subtract).then_inc(k.lo_ready, 1)


def product(k, tiles, passes, act_evac, dve_evac, hooks=(), after=None, sp_first=None,
            pe_last=None, pool_work=None, once=(), rows=(), rows_at=0, rows_need=0,
            hooks_in_next=False):
    nc = k.nc
    sizes = [t.chunks // UC for t in tiles]
    units = sum(sizes)
    nt = len(tiles)
    base, tbase = k.unit, k.tile
    done, k.ahead = k.ahead, (SLOTS if after else 0)
    assert units % SLOTS == 0 and (nt % 2 == 0 or passes == 1) and base % SLOTS == 0
    k.unit += units * passes
    k.tile += nt * passes
    ends = [sum(sizes[:m + 1]) for m in range(nt)]
    pairs = [(r, n) for r in rows for n in range(r.pairs)]
    early = bool(rows) and (rows[0].tail or (rows[0].normed and not rows[0].summed))
    starts = {2: rows[0]} if rows and rows[0].summed else {}
    if len(rows) > 1:
        starts[rows[0].pairs - 2] = rows[1]
    t0 = k.t_done - len(pairs)
    assert not rows or rows_at + len(pairs) + 2 <= units
    evac_at = {}
    for m in range(nt):
        at = ends[m] - 1 + LATE
        evac_at.setdefault((at // units, at % units), []).append(m)

    def stream(eng, which, unit_step, evac, stats, pair):
        mine = [(u, fn) for e, u, fn in hooks if e == which]
        mine_once = [(u, fn) for e, u, fn in once if e == which]

        def pair_step(j):
            if j in starts and starts[j].normed:
                stats(starts[j])
            pair(j)

        def body(i, first=False):
            for u in range(units):
                if first and 0 <= u - rows_at - 2 < len(pairs):
                    pair_step(u - rows_at - 2)
                if not (first and u < done):
                    unit_step(i, u)
                if first:
                    for at, fn in mine_once:
                        if at == u:
                            fn(eng)
                else:
                    for m in evac_at.get((1, u), ()):
                        evac(m, i - 1)
                    for at, fn in mine:
                        if at == u:
                            fn(eng, i - 1)
                for m in evac_at.get((0, u), ()):
                    evac(m, i)

        if early:
            stats(rows[0])
        body(0, True)
        loop(eng, 1, passes, body)
        for u in range(units):
            if u < k.ahead:
                unit_step(passes, u)
            for m in evac_at.get((1, u), ()):
                evac(m, passes - 1)
            for at, fn in mine:
                if at == u and not hooks_in_next:
                    fn(eng, passes - 1)

    with nc.Block() as block:
        @block.sync
        def _(sp):
            if sp_first:
                sp_first(sp)

            def body(i, more=True):
                for u in range(SLOTS, units + SLOTS * more):
                    paired = () if isinstance(i, int) else [e for e in ends[:-1] if e > SLOTS]
                    if u not in paired:
                        ahead = (u + 1) in paired
                        sp.wait_ge(k.lo_ready, base + u - SLOTS + 1 + ahead + i * units)
                    if u < units:
                        load_unit(k, sp, tiles, i, u)
                    else:
                        load_unit(k, sp, tiles, i + 1, u - units)
            loop(sp, 0, passes - 1, body)
            body(passes - 1, False)
            if after:
                prefetch(k, sp, after, k.unit)

        if pool_work:
            @block.gpsimd
            def _(pool):
                pool_work(pool)

        @block.scalar
        def _(act):
            def evac(m, i):
                act.wait_ge(k.unit_used, SLOTS + base + ends[m] + i * units)
                last = act_evac(act, m, i, 2 * ((tbase + m) % 2))
                (last.then_inc if last is not None else lambda *a: act.sem_inc(*a))(k.act_free, 1)

            def pair(j):
                act.wait_ge(k.tp_done, t0 + j + 1)
                pairs[j][0].pair_act(act, pairs[j][1], 4 + j % 4)
            stream(act, "act", lambda i, u: split_hi(k, act, u % SLOTS, base + u, i * units), evac, lambda r: r.stats_act(act), pair)

        @block.vector
        def _(dve):
            def evac(m, i):
                dve.wait_ge(k.unit_used, SLOTS + base + ends[m] + i * units)
                last = dve_evac(dve, m, i, 2 * ((tbase + m) % 2))
                (last.then_inc if last is not None else lambda *a: dve.sem_inc(*a))(k.dve_free, 1)

            def pair(j):
                dve.wait_ge(k.tp_hi, t0 + j + 1)
                pairs[j][0].pair_dve(dve, pairs[j][1], 4 + j % 4)
            stream(dve, "dve", lambda i, u: split_lo(k, dve, u % SLOTS, base + u, i * units), evac, lambda r: r.stats_dve(dve), pair)

        @block.tensor
        def _(pe):
            mine = [(u, fn) for e, u, fn in hooks if e == "pe"]

            def pair(j):
                if j < len(pairs):
                    if j >= 4:
                        pe.wait_ge(k.tp_lo, t0 + j - 3)
                    pairs[j][0].pair_pe(pe, pairs[j][1], 4 + j % 4)

            def body(i, first=False):
                u = 0
                for m, tile in enumerate(tiles):
                    bank = 2 * ((tbase + m) % 2)
                    pe.wait_ge(k.act_free, tbase + m + 1 + i * nt)
                    pe.wait_ge(k.dve_free, tbase + m + 1 + i * nt)
                    for n in range(sizes[m]):
                        s = u % SLOTS
                        if first:
                            for e, at, fn in once:
                                if e == "pe_first" and at == u:
                                    fn(pe)
                        if first and u == rows_at:
                            for j in range(4):
                                pair(j)
                        if first and 0 <= u - rows_need < len(pairs):
                            pe.wait_ge(k.tp_lo, t0 + u - rows_need + 1)
                        pe.wait_ge(k.lo_ready, base + u + 1 + i * units)
                        for c in range(UC):
                            kc = n * UC + c
                            for t in range(TT):
                                acc = k.ps[:, bank + t, :]
                                hi = tile.hi[:, kc, t * P:(t + 1) * P]
                                lo = tile.lo[:, kc, t * P:(t + 1) * P]
                                pe.matmul(acc, hi, k.w_hi[:, s, c, :], start=(kc == 0), stop=False)
                                pe.matmul(acc, hi, k.w_lo[:, s, c, :], start=False, stop=False)
                                last = pe.matmul(acc, lo, k.w_hi[:, s, c, :], start=False,
                                                 stop=(kc == tile.chunks - 1))
                        last.then_inc(k.unit_used, 1)
                        if first and u >= rows_at:
                            pair(u - rows_at + 4)
                        if not first:
                            for at, fn in mine:
                                if at == u:
                                    fn(pe, i - 1)
                        u += 1
            if mine or rows or once:
                body(0, True)
                loop(pe, 1, passes, body)
                for _, fn in mine:
                    fn(pe, passes - 1)
            else:
                loop(pe, 0, passes, body)
            if pe_last:
                pe_last(pe)


class Narrow:
    STEPS = 5

    def __init__(self, k, name, ctx):
        self.k = k
        self.raw = k.sb(f"{name}_raw", [P, DC, 16], F32, ctx)
        self.hi = k.sb(f"{name}_hi", [P, DC, P], F32R, ctx)
        self.lo = k.sb(f"{name}_lo", [P, DC, P], F32R, ctx)
        self.landed = k.sem(f"{name}_landed")

    def load(self, sp, w):
        sp.dma_start(self.raw[:], w.rearrange("(c p) n -> p c n", p=P)).then_inc(self.landed, 16)

    def pad(self, pool):
        pool.memset(self.hi[:].bitcast(F32), 0.0).then_inc(self.k.narrow, 1)
        pool.memset(self.lo[:].bitcast(F32), 0.0).then_inc(self.k.narrow, 1)

    def split_hi(self, act):
        act.wait_ge(self.landed, 16)
        act.wait_ge(self.k.narrow, self.k.narrow_done + 2)
        act.copy(self.hi[:, :, 0:16], self.raw[:]).then_inc(self.k.narrow, 1)

    def split_lo(self, dve):
        dve.wait_ge(self.k.narrow, self.k.narrow_done + 3)
        dve.tensor_tensor(self.lo[:, :, 0:16], self.raw[:], self.hi[:, :, 0:16].bitcast(F32), ALU.subtract)\
            .then_inc(self.k.narrow, 1)

    def product(self, pe, hi, lo):
        k = self.k
        pe.wait_ge(k.narrow, k.narrow_done + 4)
        acc = k.ps[:, 7, 0:T]
        for c in range(DC):
            pe.matmul(acc, self.hi[:, c, :], hi[:, c, :], start=(c == 0), stop=False)
            pe.matmul(acc, self.hi[:, c, :], lo[:, c, :], start=False, stop=False)
            last = pe.matmul(acc, self.lo[:, c, :], hi[:, c, :], start=False, stop=(c == DC - 1))
        last.then_inc(k.narrow, 1)


def sliding_window(k, proj, bias_rows, oa_hi, oa_lo):
    nc = k.nc
    G, HD, NG = 4, 64, 4
    scale = HD ** -0.5
    with ExitStack() as ctx:
        qT = k.sb("swa_qT", [HD, G, T], F32, ctx)
        kT = k.sb("swa_kT", [HD, T], F32, ctx)
        S2 = k.sb("swa_S", [P, 2, G, 3 * P], F32, ctx)
        PT = k.sb("swa_PT", [P, 3 * G, P], F32, ctx)
        bias = k.sb("swa_bias", [P, 2, G, T], F32, ctx)
        bias_landed = [k.sem(f"swa_bias_landed{n}") for n in range(2)]
        st = k.sb("swa_st", [P, 2, 6, 2 * G], F32, ctx)
        qk_t, qk_c, sc_d, sb_d, ngm, ex_d, nm_d, pt_t, pt_c, ov_d, oh_d, ol_d = (
            k.sem(f"swa_{n}") for n in ("qk_transposed", "qk_copied", "scored", "biased", "neg_max", "exped",
                                        "normed", "p_transposed", "p_copied", "summed", "o_hi", "o_lo"))
        with nc.Block() as block:
            @block.sync
            def _(sp):
                for g in range(NG):
                    if g >= 2:
                        sp.wait_ge(nm_d, g - 1)
                    sp.dma_start(bias[:, g % 2], bass.AP(tensor=bias_rows, offset=G * g * 3 * P + P - 1,
                                                         ap=[[16 * 3 * P - 1, P], [3 * P, G], [1, T]]))\
                        .then_inc(bias_landed[g % 2], 16)

            @block.tensor
            def _(pe):
                ident = k.const(C_ID)

                def queries_keys(g):
                    if g >= NG:
                        return
                    if g >= 2:
                        pe.wait_ge(pt_c, 2 * (g - 1))
                    if g == 1:
                        pe.wait_ge(qk_c, 2)
                    for j in range(G):
                        for t in range(TT):
                            pe.transpose(k.ps[0:HD, j // 2, (j % 2) * T + t * P:(j % 2) * T + (t + 1) * P],
                                         proj[:, t, QA + (G * g + j) * HD:QA + (G * g + j + 1) * HD], ident)
                    for t in range(TT):
                        last = pe.transpose(k.ps[0:HD, 2, t * P:(t + 1) * P],
                                            proj[:, t, KA + g * HD:KA + (g + 1) * HD], ident)
                    last.then_inc(qk_t, 1)

                def scores(g):
                    if g >= NG:
                        return
                    pe.wait_ge(qk_c, 2 * (g + 1))
                    if g:
                        pe.wait_ge(sb_d, g)
                    for j in range(G):
                        pe.matmul(k.ps[:, 3, j * P:(j + 1) * P], qT[:, j, 0:P], kT[:, 0:P], start=True, stop=True)
                    for j in range(G):
                        last = pe.matmul(k.ps[:, 4 + j // 2, (j % 2) * T:(j % 2 + 1) * T], qT[:, j, P:T], kT[:],
                                         start=True, stop=True)
                    last.then_inc(sc_d, 1)

                queries_keys(0)
                scores(0)
                queries_keys(1)
                scores(1)
                for g in range(NG):
                    S = S2[:, g % 2]
                    pe.wait_ge(nm_d, g + 1)
                    if g + 1 < NG:
                        pe.wait_ge(qk_c, 2 * (g + 2))
                    for b in range(3):
                        for j in range(G):
                            last = pe.transpose(k.ps[:, b, j * P:(j + 1) * P], S[:, j, b * P:(b + 1) * P], ident)
                    last.then_inc(pt_t, 1)
                    pe.wait_ge(pt_c, 2 * (g + 1))
                    if g:
                        pe.wait_ge(ol_d, g)
                    for j in range(G):
                        at = HD * (j % 2)
                        for b, kb in enumerate((0, 0, 1)):
                            q = 0 if b == 0 else P
                            last = pe.matmul(k.ps[at:at + HD, 6, (j // 2) * T + q:(j // 2) * T + q + P],
                                             proj[:, kb, VA + g * HD:VA + (g + 1) * HD], PT[:, b * G + j, :],
                                             start=(b < 2), stop=(b != 1))
                    last.then_inc(ov_d, 1)
                    queries_keys(g + 2)
                    scores(g + 2)

            @block.scalar
            def _(act):
                def queries_keys(g):
                    if g >= NG:
                        return
                    act.wait_ge(qk_t, g + 1)
                    if g:
                        act.wait_ge(sc_d, g)
                    act.activation(qT[:], k.ps[0:HD, 0:2, :].rearrange("p b (j n) -> p (b j) n", j=2), ACT.Copy,
                                   scale=scale).then_inc(qk_c, 1)
                    act.copy(kT[:], k.ps[0:HD, 2, 0:T]).then_inc(qk_c, 1)

                def exponentials(g):
                    if g >= NG:
                        return
                    S, (mx, neg, den, esk, rec, dif) = S2[:, g % 2], (st[:, g % 2, n, :] for n in range(6))
                    act.wait_ge(ngm, g + 1)
                    for b, (lo, hi) in enumerate(((0, P), (P, 3 * P))):
                        for j in range(G):
                            at = b * G + j
                            act.activation(S[:, j, lo:hi], S[:, j, lo:hi], ACT.Exp, bias=neg[:, at:at + 1],
                                           accum_out=den[:, at:at + 1])
                    act.activation(esk, dif, ACT.Exp).then_inc(ex_d, 1)

                queries_keys(0)
                queries_keys(1)
                exponentials(0)
                exponentials(1)
                for g in range(NG):
                    act.wait_ge(pt_t, g + 1)
                    act.copy(PT[:, 0:2 * G, :], k.ps[:, 0:2, :].rearrange("p b (j n) -> p (b j) n", j=G))\
                        .then_inc(pt_c, 1)
                    act.wait_ge(ov_d, g + 1)
                    act.copy(oa_hi[:, 2 * g:2 * g + 2, :], k.ps[:, 6, :].rearrange("p (c n) -> p c n", c=2))\
                        .then_inc(oh_d, 1)
                    queries_keys(g + 2)
                    exponentials(g + 2)

            @block.vector
            def _(dve):
                def maxima(g):
                    if g >= NG:
                        return
                    S, (mx, neg, den, esk, rec, dif) = S2[:, g % 2], (st[:, g % 2, n, :] for n in range(6))
                    dve.wait_ge(bias_landed[g % 2], 16 * (g // 2 + 1))
                    dve.wait_ge(sc_d, g + 1)
                    if g >= 2:
                        dve.wait_ge(pt_t, g - 1)
                    dve.tensor_tensor(S[:, :, 0:P], k.ps[:, 3, :].rearrange("p (j n) -> p j n", j=G),
                                      bias[:, g % 2, :, P:T], ALU.add)
                    dve.tensor_tensor(
                        S[:, :, P:3 * P], k.ps[:, 4:6, :].rearrange("p b (j n) -> p (b j) n", j=2),
                        bias[:, g % 2], ALU.add).then_inc(sb_d, 1)
                    dve.wait_ge(sb_d, g + 1)
                    dve.tensor_reduce(mx[:, 0:G], S[:, :, 0:P], AX.X, ALU.max)
                    k.then(dve, "dve", dve.tensor_reduce(mx[:, G:2 * G], S[:, :, P:3 * P], AX.X, ALU.max))
                    sink = k.col("sinks", G * g, G)
                    dve.tensor_tensor(mx[:, 0:G], mx[:, 0:G], sink, ALU.max)
                    k.then(dve, "dve", dve.tensor_tensor(mx[:, G:2 * G], mx[:, G:2 * G], sink, ALU.max))
                    dve.tensor_tensor(dif[:, 0:G], sink, mx[:, 0:G], ALU.subtract)
                    dve.tensor_tensor(dif[:, G:2 * G], sink, mx[:, G:2 * G], ALU.subtract)
                    dve.tensor_scalar(neg, mx, -1.0, None, ALU.mult).then_inc(ngm, 1)

                def low(g):
                    dve.wait_ge(oh_d, g + 1)
                    dve.tensor_tensor(oa_lo[:, 2 * g:2 * g + 2, :], k.ps[:, 6, :].rearrange("p (c n) -> p c n", c=2),
                                      oa_hi[:, 2 * g:2 * g + 2, :].bitcast(F32), ALU.subtract).then_inc(ol_d, 1)

                def normed(g):
                    if g >= NG:
                        return
                    S, (mx, neg, den, esk, rec, dif) = S2[:, g % 2], (st[:, g % 2, n, :] for n in range(6))
                    dve.wait_ge(ex_d, g + 1)
                    k.then(dve, "dve", dve.tensor_tensor(den, den, esk, ALU.add))
                    k.then(dve, "dve", dve.reciprocal(rec, den))
                    for b, (lo, hi) in enumerate(((0, P), (P, 3 * P))):
                        for j in range(G):
                            at = b * G + j
                            last = dve.tensor_scalar(S[:, j, lo:hi], S[:, j, lo:hi], rec[:, at:at + 1], None,
                                                     ALU.mult)
                    last.then_inc(nm_d, 1)

                maxima(0)
                maxima(1)
                normed(0)
                for g in range(NG):
                    dve.wait_ge(pt_t, g + 1)
                    dve.tensor_copy(PT[:, 2 * G:3 * G, :], k.ps[:, 2, :].rearrange("p (j n) -> p j n", j=G))\
                        .then_inc(pt_c, 1)
                    normed(g + 1)
                    low(g)
                    maxima(g + 2)


def gated_linear(k, life, proj, og, w_up, b_up, hi, lo, sp_work):
    nc = k.nc
    H, DV = 4, 256
    inv_tau = 1.0 / 16.0
    scale = float(P) ** -0.5
    st = k.sb("gla_st", [P, 3, TT * H], F32, life)
    y = proj[:, :, QB:VB]
    with ExitStack() as ctx:
        gate_w = k.sb("gla_gate_w", [16, 2, 512], F32, ctx)
        gate_landed = k.sem("gla_gate_landed")
        glT = k.sb("gla_glT", [16, T], F32, ctx)
        la = at = proj[:, :, 0:H * P]
        ex = proj[:, :, H * P:2 * H * P]
        ks = proj[:, :, 2 * H * P:3 * H * P]
        up = k.sb("gla_up", [P, H, T], F32, ctx)
        dn = k.sb("gla_dn", [P, H, T], F32, ctx)
        qd = k.sb("gla_qd", [P, H, T], F32, ctx)
        kd = dn
        state = k.sb("gla_state", [P, 3, H, DV], F32, ctx)
        names = ("gl_in", "z", "abs_done", "la", "b", "sfx", "exps", "qk", "decayed", "scored",
                 "masked", "grown", "state", "out", "squares", "root", "y")
        s = {n: k.sem(f"gla_{n}") for n in names}
        with nc.Block() as block:
            @block.sync
            def _(sp):
                sp.dma_start(gate_w[:, 0, :], w_up).then_inc(gate_landed, 16)
                sp.dma_start(gate_w[0:1, 1, :], b_up).then_inc(gate_landed, 16)
                sp_work(sp)

            @block.tensor
            def _(pe):
                pe.wait_ge(s["gl_in"], 1)
                pe.wait_ge(gate_landed, 32)
                for t in range(TT):
                    pe.matmul(k.ps[:, t, :], glT[:, t * P:(t + 1) * P], gate_w[0:16, 0, :], start=True, stop=False)
                    last = pe.matmul(k.ps[:, t, :], k.consts[0:1, C_ONES, :], gate_w[0:1, 1, :], start=False, stop=True)
                last.then_inc(s["z"], 1)
                for base, bank in ((QB, 4), (KB, 6)):
                    for h in range(H):
                        for t in range(TT):
                            last = pe.transpose(k.ps[:, bank + h // 2, (h % 2) * T + t * P:(h % 2) * T + (t + 1) * P],
                                                proj[:, t, base + h * P:base + (h + 1) * P], k.const(C_ID))
                last.then_inc(s["qk"], 1)
                pe.wait_ge(s["la"], 1)
                for h in range(H):
                    for t in range(TT):
                        last = pe.matmul(k.ps[:, 2 + h // 2, (h % 2) * T + t * P:(h % 2) * T + (t + 1) * P],
                                         la[:, t, h * P:(h + 1) * P], k.const(C_CUM), start=True, stop=True)
                last.then_inc(s["b"], 1)
                for t in range(TT):
                    last = pe.matmul(k.ps[:, t, :], k.const(C_AFT), la[:, t, :], start=True, stop=True)
                last.then_inc(s["sfx"], 1)
                pe.wait_ge(s["decayed"], 1)
                for t in range(TT):
                    for h in range(H):
                        last = pe.matmul(k.ps[:, 2 + t, h * P:(h + 1) * P], kd[:, h, t * P:(t + 1) * P],
                                         qd[:, h, t * P:(t + 1) * P], start=True, stop=True)
                last.then_inc(s["scored"], 1)
                pe.wait_ge(s["decayed"], 2)
                for c in range(3):
                    t, p = c // 2, CH * (c % 2)
                    for h in range(H):
                        last = pe.matmul(k.ps[:, (4 + 2 * c) % 8 + h // 2, (h % 2) * DV:(h % 2 + 1) * DV],
                                         ks[p:p + CH, t, h * P:(h + 1) * P],
                                         proj[p:p + CH, t, VB + h * DV:VB + (h + 1) * DV], start=True, stop=True)
                    last.then_inc(s["grown"], 1)
                pe.wait_ge(s["masked"], 1)
                pe.wait_ge(s["state"], 3)
                for t in range(TT):
                    for h in range(H):
                        bank, lo = 4 + 2 * t + h // 2, (h % 2) * DV
                        for c in range(2 * t, 2 * t + 2):
                            p = CH * (c % 2)
                            last = pe.matmul(k.ps[p:p + CH, bank, lo:lo + DV], at[:, t, h * P + p:h * P + p + CH],
                                             proj[:, t, VB + h * DV:VB + (h + 1) * DV], start=True, stop=(c == 0))
                            if c:
                                last = pe.matmul(k.ps[p:p + CH, bank, lo:lo + DV], qd[:, h, c * CH:(c + 1) * CH],
                                                 state[:, c - 1, h, :], start=False, stop=True)
                last.then_inc(s["out"], 1)

            @block.scalar
            def _(act):
                act.wait_ge(k.narrow, k.narrow_done + Narrow.STEPS)
                act.copy(glT[:], k.ps[0:16, 7, 0:T]).then_inc(s["gl_in"], 1)
                act.wait_ge(s["z"], 1)
                k.then(act, "act", act.activation(ex, k.ps[:, 0:2, :], ACT.Abs))
                k.then(act, "act", act.activation(ex, ex, ACT.Exp, scale=-1.0))
                act.activation(ex, ex, ACT.Ln, bias=1.0).then_inc(s["abs_done"], 1)
                act.wait_ge(s["b"], 1)
                b = k.ps[:, 2:4, :].rearrange("p b (j n) -> p (b j) n", j=2)
                act.activation(up[:], b, ACT.Exp, scale=inv_tau)
                act.activation(dn[:], b, ACT.Exp, scale=-inv_tau).then_inc(s["exps"], 1)
                act.wait_ge(s["sfx"], 1)
                act.wait_ge(s["la"], 1)
                act.activation(ex, k.ps[:, 0:2, :], ACT.Exp, scale=inv_tau).then_inc(s["exps"], 1)
                ahead_hi(k, act)

            @block.vector
            def _(dve):
                dve.wait_ge(s["abs_done"], 1)
                for t in range(TT):
                    last = dve.scalar_tensor_tensor(la[:, t, :], k.ps[:, t, :], 0.0, ex[:, t, :], ALU.min, ALU.subtract)
                last.then_inc(s["la"], 1)
                dve.wait_ge(s["qk"], 1)
                dve.wait_ge(s["exps"], 1)
                for b in range(2):
                    for j in range(2):
                        dve.scalar_tensor_tensor(qd[:, 2 * b + j, :], k.ps[:, 4 + b, j * T:(j + 1) * T], scale,
                                                 up[:, 2 * b + j, :], ALU.mult, ALU.mult)
                last = dve.tensor_tensor(kd[:], k.ps[:, 6:8, :].rearrange("p b (j n) -> p (b j) n", j=2), dn[:],
                                         ALU.mult)
                last.then_inc(s["decayed"], 1)
                dve.wait_ge(s["exps"], 2)
                dve.tensor_tensor(ks, proj[:, :, KB:KB + H * P], ex, ALU.mult).then_inc(s["decayed"], 1)
                dve.wait_ge(s["scored"], 1)
                k.then(dve, "dve", dve.tensor_scalar(at, k.ps[:, 2:4, :],
                                                     BIG, -BIG, ALU.min, ALU.max))
                for t in range(TT):
                    for h in range(H):
                        one = at[:, t, h * P:(h + 1) * P]
                        last = dve.tensor_tensor(one, one, k.const(C_CUM), ALU.mult)
                last.then_inc(s["masked"], 1)
                for c in range(3):
                    dve.wait_ge(s["grown"], c + 1)
                    grown = k.ps[:, (4 + 2 * c) % 8:(4 + 2 * c) % 8 + 2, :].rearrange("p b (j n) -> p (b j) n", j=2)
                    if c == 0:
                        dve.tensor_copy(state[:, 0, :, :], grown).then_inc(s["state"], 1)
                    else:
                        dve.wait_ge(s["state"], c)
                        for h in range(H):
                            last = dve.scalar_tensor_tensor(
                                state[:, c, h, :], state[:, c - 1, h, :], up[:, h, CH * (c + 1) - 1:CH * (c + 1)],
                                grown[:, h, :], ALU.mult, ALU.add)
                        last.then_inc(s["state"], 1)
                ahead_lo(k, dve)
        k.narrow_done += Narrow.STEPS

    def out(t, h):
        return k.ps[:, 4 + 2 * t + h // 2, (h % 2) * DV:(h % 2 + 1) * DV]

    def tail_act(act):
        act.wait_ge(s["out"], 1)
        for t in range(TT):
            for h in range(H):
                last = act.activation(y[:, t, h * DV:(h + 1) * DV], out(t, h), ACT.Square,
                                      accum_out=st[:, 0, t * H + h:t * H + h + 1])
        last.then_inc(s["squares"], 1)
        act.wait_ge(s["root"], 1)
        act.activation(st[:, 1, :], st[:, 1, :], ACT.Sqrt).then_inc(s["root"], 1)

    def tail_dve(dve):
        dve.wait_ge(s["squares"], 1)
        dve.tensor_scalar(st[:, 1, :], st[:, 0, :], 1.0 / DV, EPS, ALU.mult, ALU.add).then_inc(s["root"], 1)
        dve.wait_ge(s["root"], 2)
        k.then(dve, "dve", dve.reciprocal(st[:, 2, :], st[:, 1, :]))
        for t in range(TT):
            for h in range(H):
                last = dve.scalar_tensor_tensor(y[:, t, h * DV:(h + 1) * DV], out(t, h),
                                                st[:, 2, t * H + h:t * H + h + 1], og[:, t, h * DV:(h + 1) * DV],
                                                ALU.mult, ALU.mult)
        last.then_inc(s["y"], 1)
    return Rows(k, life, y, H * DV // P, lambda c: k.col("g_gla", c % 2), hi, lo, tail=(tail_act, tail_dve, (s["y"], 1)))


def norm_rows(k, gain, landed, room, again):
    nc = k.nc
    act0, dve0 = k.steps["act"], k.steps["dve"]
    with nc.Block() as block:
        @block.scalar
        def _(act):
            act.wait_ge(k.step["dve"], dve0 + 2)
            act.activation(k.small[:, 2:4], k.small[:, 2:4], ACT.Sqrt).then_inc(k.step["act"], 1)
            k.steps["act"] += 1
            if again:
                for t in range(TT):
                    act.wait_ge(k.step["dve"], dve0 + 4 + t)
                    act.activation(room[:, 8 * t:8 * (t + 1), :].rearrange("p c n -> p (c n)"), k.h[:, t, :],
                                   ACT.Square, accum_out=k.sums[:, 0, t, 0:1])

        @block.vector
        def _(dve):
            k.then(dve, "dve", dve.tensor_reduce(k.small[:, 0:2], k.sums[:, 0], AX.X, ALU.add))
            k.then(dve, "dve", dve.tensor_scalar(k.small[:, 2:4], k.small[:, 0:2], 1.0 / D, EPS, ALU.mult, ALU.add))
            dve.wait_ge(k.step["act"], act0 + 1)
            k.then(dve, "dve", dve.reciprocal(k.small[:, 4:6], k.small[:, 2:4]))
            if again:
                dve.memset(k.sums[:, 0, :, 1:4], 0.0)
            dve.wait_ge(*landed)
            for t in range(TT):
                k.then(dve, "dve", dve.scalar_tensor_tensor(k.h[:, t, :], k.h[:, t, :], k.small[:, 4 + t:5 + t],
                                                            gain[:], ALU.mult, ALU.mult))


def start(k, x, consts, cols, first_tiles):
    nc = k.nc
    x_landed = [k.sem(f"x_landed{t}") for t in range(TT)]
    with nc.Block() as block:
        @block.sync
        def _(sp):
            for t in range(TT):
                sp.dma_start(k.h[:, t, :], x[0, t * P:(t + 1) * P, :]).then_inc(x_landed[t], 16)
            sp.dma_start(k.ident[:], consts[:, C_ID, :]).then_inc(k.landed, 16)
            sp.dma_start(k.cols[:], cols).then_inc(k.landed, 16)
            prefetch(k, sp, first_tiles, 0)

        @block.vector
        def _(dve):
            dve.memset(k.small[:, 0:1], 0.0).then_inc(k.unit_used, SLOTS)
            dve.memset(k.small[:, 1:2], 0.0).then_inc(k.act_free, 2)
            dve.memset(k.small[:, 2:3], 0.0).then_inc(k.dve_free, 2)
    return x_landed


class BiasRows:
    H, N = 16, 3 * P

    def __init__(self, k, ctx):
        self.k = k
        self.rel = k.sb("rel_bias_sb", [33, self.H], F32, ctx)
        self.onehot = k.sb("onehot_sb", [33, self.N], F32, ctx)
        self.table = k.sb("bias_table_sb", [self.H, self.N], F32, ctx)
        self.row = k.nc.dram_tensor("bias_row", [self.H, self.N], F32, kind="Internal")
        self.rows = k.nc.dram_tensor("bias_rows", [P, self.H * self.N], F32, kind="Internal")
        self.landed, self.masked, self.done, self.stored = (
            k.sem(f"bias_{n}") for n in ("landed", "masked", "done", "stored"))

    def load(self, sp, rel, onehot):
        sp.dma_start(self.rel[0:32, :], rel).then_inc(self.landed, 16)
        sp.dma_start(self.onehot[:], onehot).then_inc(self.landed, 16)

    def mask(self, pool):
        pool.memset(self.rel[32:33, :], NEG).then_inc(self.masked, 1)
        pool.wait_ge(self.masked, 1)

    def product(self, pe):
        pe.wait_ge(self.landed, 32)
        pe.wait_ge(self.masked, 1)
        pe.matmul(self.k.ps[0:self.H, 7, 0:self.N], self.rel[:], self.onehot[:], start=True, stop=True)\
            .then_inc(self.done, 1)

    def copy(self, act):
        act.wait_ge(self.done, 1)
        act.copy(self.table[:], self.k.ps[0:self.H, 7, 0:self.N]).then_inc(self.done, 1)

    def store(self, pool):
        pool.wait_ge(self.done, 2)
        pool.dma_start(self.row.ap(), self.table[:]).then_inc(self.stored, 16)
        pool.wait_ge(self.stored, 16)
        pool.dma_start(self.rows.ap(), bass.AP(tensor=self.row, offset=0, ap=[[0, P], [1, self.H * self.N]]))\
            .then_inc(self.stored, 16)
        pool.wait_ge(self.stored, 32)


def add_to_stream(k, per_pass=2):
    tb = k.tile

    def columns(m, i):
        return slice((i * per_pass + m) * NT, (i * per_pass + m + 1) * NT)

    def act_evac(act, m, i, bank):
        act.wait_ge(k.dve_free, 2 + tb + m + 1 + i * per_pass)
        for t in range(TT):
            last = act.activation(k.ps[:, 4 + t, :], k.h[:, t, columns(m, i)], ACT.Square,
                                  accum_out=k.sums[:, 0, t, i * per_pass + m:i * per_pass + m + 1])
        return last

    def dve_evac(dve, m, i, bank):
        for t in range(TT):
            at = k.h[:, t, columns(m, i)]
            last = dve.tensor_tensor(at, at, k.ps[:, bank + t, :], ALU.add)
        return last
    return act_evac, dve_evac


def copy_evacs(k, dst, col, rows=None):
    def act_evac(act, m, i, bank):
        at = dst[:, 0, bass.ds(col(m, i), NT)]
        if not rows:
            return act.copy(at, k.ps[:, bank, :])
        act.wait_ge(*rows.rms_ready)
        return act.activation(at, k.ps[:, bank, :], ACT.Copy, scale=rows.scale(0))

    def dve_evac(dve, m, i, bank):
        at = dst[:, 1, bass.ds(col(m, i), NT)]
        if not rows:
            return dve.tensor_copy(at, k.ps[:, bank + 1, :])
        return dve.tensor_scalar(at, k.ps[:, bank + 1, :], rows.scale(1), None, ALU.mult)
    return act_evac, dve_evac


def ffn1_tiles(w_gate, w_up, hi, lo):
    return [Tile(w_gate, DC, lambda i: i * NT, hi, lo), Tile(w_up, DC, lambda i: i * NT, hi, lo)]


def down_tiles(w_down, hi, lo):
    return [Tile(w_down, HC, lambda i, m=m: i * (2 * NT) + m * NT, hi, lo) for m in range(2)]


def square_tiles(w, chunks, hi, lo):
    return [Tile(w, chunks, lambda i, m=m: i * (2 * NT) + m * NT, hi, lo) for m in range(2)]


def stream_col(m, i):
    return i * (2 * NT) + m * NT


def hidden_transposed(k, hid, hT_hi, hT_lo, t0, hid_ready):
    def pe_hook(pe, i):
        hid_ready(pe, i)
        pe.wait_ge(k.tp_lo, t0 + 2 * i)
        for s in range(2):
            for c in range(2):
                for t in range(TT):
                    at = (2 * s + c) * P
                    last = pe.transpose(k.ps[:, 4 + s, c * T + t * P:c * T + (t + 1) * P], hid[:, t, at:at + P],
                                        k.const(C_ID))
            last.then_inc(k.tp_done, 1)

    def at(i, s):
        return bass.ds(i * (4 * T) + s * 2 * T, 2 * T)

    def act_hook(act, i):
        for s in range(2):
            act.wait_ge(k.tp_done, t0 + 1 + s + 2 * i)
            act.copy(hT_hi.rearrange("p c n -> p (c n)")[:, at(i, s)], k.ps[:, 4 + s, :]).then_inc(k.tp_hi, 1)

    def dve_hook(dve, i):
        for s in range(2):
            dve.wait_ge(k.tp_hi, t0 + 1 + s + 2 * i)
            dve.tensor_tensor(hT_lo.rearrange("p c n -> p (c n)")[:, at(i, s)], k.ps[:, 4 + s, :],
                              hT_hi.rearrange("p c n -> p (c n)")[:, at(i, s)].bitcast(F32), ALU.subtract)\
                .then_inc(k.tp_lo, 1)
    return pe_hook, act_hook, dve_hook


def first_block(k, a, hi, lo, next_tiles):
    nc = k.nc
    w_in = a["w_in"]
    head = [Tile(w_in, DC, lambda i: QA, hi, lo), Tile(w_in, DC, lambda i: OG, hi, lo),
            Tile(w_in, DC, lambda i: OG + NT, hi, lo)]
    body = [Tile(w_in, DC, lambda i, m=m: NT + i * (2 * NT) + m * NT, hi, lo) for m in range(2)]
    with ExitStack() as life:
        og = k.sb("og", [P, TT, 1024], F32, life)
        oa = [k.sb(f"oa_{n}", [P, 8, T], F32R, life) for n in ("hi", "lo")]
        ob = [k.sb(f"ob_{n}", [P, 8, T], F32R, life) for n in ("hi", "lo")]
        merge = [Tile(w_in, DC, lambda i: GA + i * NT, hi, lo), Tile(w_in, DC, lambda i: GB + i * NT, hi, lo),
                 Tile(a["w_proj_a"], 8, lambda i: i * NT, *oa), Tile(a["w_proj_b"], 8, lambda i: i * NT, *ob)]
        out_tiles = square_tiles(a["w_out"], DC, hi, lo)
        ffn_tiles = ffn1_tiles(a["w_ffn_gate"], a["w_ffn_up"], hi, lo)
        with ExitStack() as mid:
            proj = k.sb("proj", [P, TT, GL], F32, mid)
            with ExitStack() as early:
                low = Narrow(k, "low", early)
                bias = BiasRows(k, early)
                masks_landed = k.sem("masks_landed")
                x_landed = start(k, a["x"], a["consts"], a["cols"], head)
                mix = Rows(k, early, k.h, DC, lambda c: k.col("g_mix", c), hi, lo, normed=True, landed=x_landed)

                def loads(sp):
                    low.load(sp, w_in[:, GL:OG])
                    bias.load(sp, a["rel_bias"], a["onehot"])
                    sp.dma_start(k.consts[:], a["consts"]).then_inc(masks_landed, 16)

                def pool_work(pool):
                    bias.mask(pool)
                    low.pad(pool)
                    bias.store(pool)
                    pool.wait_ge(masks_landed, 16)

                def last_product(pe):
                    pe.wait_ge(bias.done, 2)
                    low.product(pe, hi, lo)

                def act_evac(act, m, i, bank):
                    if m == 0:
                        return act.copy(proj[:, 0, 0:NT], k.ps[:, bank, :])
                    for t in range(TT):
                        last = act.activation(og[:, t, (m - 1) * NT:m * NT], k.ps[:, bank + t, :], ACT.Silu)
                    return last

                def dve_evac(dve, m, i, bank):
                    return dve.tensor_copy(proj[:, 1, 0:NT], k.ps[:, bank + 1, :]) if m == 0 else None
                product(k, head, 1, act_evac, dve_evac, after=body, sp_first=loads, pool_work=pool_work,
                        rows=[mix], pe_last=last_product,
                        once=[("pe_first", 12, bias.product), ("act", 12, bias.copy), ("act", 13, low.split_hi),
                              ("dve", 14, low.split_lo)])

                product(k, body, 3, *copy_evacs(k, proj, lambda m, i: NT + i * (2 * NT) + m * NT))
            sliding_window(k, proj, bias.rows, *oa)
            linear = gated_linear(k, mid, proj, og, a["w_gate_up"], a["b_gate"], *ob,
                                  lambda sp: prefetch(k, sp, merge, k.unit))
            merged = k.sb("merged", [P, TT, D], F32, mid)
            sg = k.sb("gates", [P, 2, TT, NT], F32, mid)
            term = k.sb("term", [P, TT, NT], F32, mid)
            term_done = k.sem("merge_term")
            tb = k.tile

            def act_evac(act, m, i, bank):
                if m > 1:
                    return None
                act.wait_ge(k.dve_free, tb + m + 1 + 4 * i)
                return act.activation(sg[:, m, :, :], k.ps[:, bank:bank + 2, :], ACT.Sigmoid)

            def dve_evac(dve, m, i, bank):
                if m < 2:
                    return None
                dve.wait_ge(k.act_free, 2 + tb + m - 1 + 4 * i)
                acc = k.ps[:, bank:bank + 2, :]
                at = merged[:, :, bass.ds(i * NT, NT)]
                if m == 2:
                    return dve.tensor_tensor(at, acc, sg[:, 0, :, :], ALU.mult)
                dve.tensor_tensor(term[:], acc, sg[:, 1, :, :], ALU.mult).then_inc(term_done, 1)
                dve.wait_ge(term_done, 1 + i)
                dve.wait_ge(k.dve_free, 2 + tb + 3 + 4 * i)
                return dve.tensor_tensor(at, at, term[:], ALU.add)
            product(k, merge, 4, act_evac, dve_evac, after=out_tiles, rows=[linear], rows_at=8,
                    rows_need=(2 * DC + 8) // UC)
            product(k, out_tiles, 2, *add_to_stream(k), after=ffn_tiles,
                    rows=[Rows(k, mid, merged, DC, lambda c: 1.0, hi, lo)])
    with ExitStack() as life:
        hT = [k.sb(f"hT_{n}", [P, HC, T], F32R, life) for n in ("hi", "lo")]
        down = down_tiles(a["w_ffn_down"], *hT)
        with ExitStack() as mid:
            hid = k.sb("hid", [P, TT, NT], F32, mid)
            sg = k.sb("ffn_silu", [P, TT, NT], F32, mid)
            ffn = Rows(k, mid, k.h, DC, lambda c: k.col("g_ffn", c), hi, lo, normed=True, summed=True)
            tb, t0 = k.tile, k.t_done

            def act_evac(act, m, i, bank):
                if m:
                    return None
                act.wait_ge(k.dve_free, tb + 2 + 2 * i)
                act.wait_ge(*ffn.rms_ready)
                for t in range(TT):
                    last = act.activation(sg[:, t, :], k.ps[:, bank + t, :], ACT.Silu, scale=ffn.scale(t))
                return last

            def dve_evac(dve, m, i, bank):
                if m == 0:
                    return None
                dve.wait_ge(k.act_free, 2 + tb + 1 + 2 * i)
                dve.wait_ge(k.tp_done, t0 + 2 * i)
                for t in range(TT):
                    last = dve.scalar_tensor_tensor(hid[:, t, :], k.ps[:, bank + t, :], ffn.scale(t), sg[:, t, :],
                                                    ALU.mult, ALU.mult)
                return last
            pe_hook, act_hook, dve_hook = hidden_transposed(
                k, hid, *hT, t0, lambda pe, i: pe.wait_ge(k.dve_free, 2 + tb + 2 + 2 * i))
            product(k, ffn_tiles, FF1 // NT, act_evac, dve_evac, after=down, rows=[ffn],
                    hooks=[("pe", 5, pe_hook), ("act", 7, act_hook), ("dve", 8, dve_hook)], hooks_in_next=True)
            k.t_done += 2 * (FF1 // NT)
        gain = k.sb("gain_final1", [P, D], F32, life)
        s_gain = k.sem("gain_final1_landed")
        last = FF1 // NT - 1
        late = [("act", 0, lambda act: act_hook(act, last)), ("dve", 1, lambda dve: dve_hook(dve, last)),
                ("pe_first", 4 * last // UC, lambda pe: pe.wait_ge(k.tp_lo, t0 + 2 * (last + 1)))]
        product(k, down, 2, *add_to_stream(k), after=next_tiles, once=late,
                sp_first=lambda sp: sp.dma_start(gain[:], a["g_final1"]).then_inc(s_gain, 16))
        norm_rows(k, gain, (s_gain, 16), hT[0], True)


SQ, SK, SV, GQ, GK, GV, GZ, GBA = (1024 * n for n in range(8))
HEADS2 = 8


def stick_breaking(k, proj, ba, hi, lo, sp_work):
    nc = k.nc
    G, W, NG = 2, T + P, HEADS2 // 2
    scale = float(P) ** -0.5
    names = ("ba", "qk", "qT", "kT", "z", "log", "stay", "later", "exponent", "exp", "weights", "out", "hi", "lo")
    s = {n: k.sem(f"stick_{n}") for n in names}
    with ExitStack() as ctx:
        def pair(name, width):
            x = k.sb(f"stick_{name}", [P, 2, G, width], F32, ctx)
            return [x[:, 0], x[:, 1]]
        qT, kT = pair("qT", T), pair("kT", T)
        ln = pair("ln", W)
        lb = pair("lb", W)
        st = pair("st", W)

        def bank(g, n):
            return k.ps[:, 4 * (g % 2) + n, :]

        def scores(g):
            return (bank(g, 2).rearrange("p (j n) -> p j n", j=G), bank(g, 3)[:, 0:G * P].rearrange("p (j n) -> p j n", j=G))
        before = k.const(C_BEFALL)
        with nc.Block() as block:
            @block.sync
            def _(sp):
                sp_work(sp)

            @block.tensor
            def _(pe):
                def transposes(g):
                    if g >= NG:
                        return
                    if g >= 2:
                        pe.wait_ge(s["lo"], g - 1)
                    for n, base in ((0, SQ), (1, SK)):
                        for j in range(G):
                            for t in range(TT):
                                last = pe.transpose(bank(g, n)[:, j * T + t * P:j * T + (t + 1) * P],
                                                    proj[:, t, base + (G * g + j) * P:base + (G * g + j + 1) * P],
                                                    k.const(C_ID))
                    last.then_inc(s["qk"], 1)

                def products(g):
                    if g >= NG:
                        return
                    z0, z1 = scores(g)
                    pe.wait_ge(s["qT"], g + 1)
                    pe.wait_ge(s["kT"], g + 1)
                    if g == 1:
                        pe.wait_ge(s["ba"], 1)
                    if g >= 2:
                        pe.wait_ge(s["exponent"], g - 1)
                    for j in range(G):
                        pe.matmul(z0[:, j, :], kT[g % 2][:, j, 0:P], qT[g % 2][:, j, :], start=True, stop=True)
                    for j in range(G):
                        last = pe.matmul(z1[:, j, :], kT[g % 2][:, j, P:T], qT[g % 2][:, j, P:T], start=True, stop=True)
                    last.then_inc(s["z"], 1)

                def later(g):
                    if g >= NG:
                        return
                    z0, z1 = scores(g)
                    stay = st[g % 2]
                    pe.wait_ge(s["stay"], g + 1)
                    for j in range(G):
                        pe.matmul(z0[:, j, 0:P], k.const(C_AFTALL), stay[:, j, 0:P], start=True, stop=True)
                        pe.matmul(z0[:, j, P:T], k.const(C_AFTALL), stay[:, j, P:T], start=True, stop=False)
                        pe.matmul(z0[:, j, P:T], k.const(C_ONES), stay[:, j, T:W], start=False, stop=True)
                    for j in range(G):
                        last = pe.matmul(z1[:, j, :], k.const(C_AFTALL), stay[:, j, T:W], start=True, stop=True)
                    last.then_inc(s["later"], 1)

                def outputs(g):
                    pe.wait_ge(s["weights"], g + 1)
                    w = lb[g % 2]
                    for j in range(G):
                        v = [proj[:, t, SV + (G * g + j) * P:SV + (G * g + j + 1) * P] for t in range(TT)]
                        out, at = bank(g, 0), j * T
                        pe.matmul(out[:, at:at + P], v[0], w[:, j, 0:P], start=True, stop=True)
                        pe.matmul(out[:, at + P:at + T], v[0], w[:, j, P:T], start=True, stop=False)
                        last = pe.matmul(out[:, at + P:at + T], v[1], w[:, j, T:W], start=False, stop=True)
                    last.then_inc(s["out"], 1)

                transposes(0)
                products(0)
                transposes(1)
                for g in range(NG):
                    products(g + 1)
                    later(g)
                    outputs(g)
                    transposes(g + 2)

            @block.scalar
            def _(act):
                def queries(g):
                    if g < NG:
                        act.wait_ge(s["qk"], g + 1)
                        act.activation(qT[g % 2], bank(g, 0).rearrange("p (j n) -> p j n", j=G), ACT.Copy, scale=scale)\
                            .then_inc(s["qT"], 1)

                def magnitudes(g):
                    if g >= NG:
                        return
                    z0, z1 = scores(g)
                    x = ln[g % 2]
                    act.wait_ge(s["z"], g + 1)
                    if g >= 2:
                        act.wait_ge(s["stay"], g - 1)
                    act.activation(x[:, :, 0:T], z0, ACT.Abs)
                    k.then(act, "act", act.activation(x[:, :, T:W], z1, ACT.Abs))
                    k.then(act, "act", act.activation(x, x, ACT.Exp, scale=-1.0))

                def logarithms(g):
                    if g < NG:
                        act.activation(ln[g % 2], ln[g % 2], ACT.Ln, bias=1.0).then_inc(s["log"], 1)

                act.wait_ge(k.narrow, k.narrow_done + Narrow.STEPS)
                act.copy(ba, k.ps[0:16, 7, 0:T]).then_inc(s["ba"], 1)
                queries(0)
                magnitudes(0)
                logarithms(0)
                queries(1)
                for g in range(NG):
                    magnitudes(g + 1)
                    act.wait_ge(s["exponent"], g + 1)
                    act.activation(lb[g % 2], lb[g % 2], ACT.Exp).then_inc(s["exp"], 1)
                    act.wait_ge(s["out"], g + 1)
                    act.copy(hi[:, G * g:G * (g + 1), :], bank(g, 0).rearrange("p (j n) -> p j n", j=G))\
                        .then_inc(s["hi"], 1)
                    logarithms(g + 1)
                    queries(g + 2)

            @block.vector
            def _(dve):
                def keys(g):
                    if g < NG:
                        dve.wait_ge(s["qk"], g + 1)
                        dve.tensor_copy(kT[g % 2], bank(g, 1).rearrange("p (j n) -> p j n", j=G)).then_inc(s["kT"], 1)

                def splits(g):
                    if g >= NG:
                        return
                    stay, w, x = st[g % 2], lb[g % 2], ln[g % 2]
                    dve.wait_ge(s["log"], g + 1)
                    if g >= 2:
                        dve.wait_ge(s["out"], g - 1)
                    for z, a, b in zip(scores(g), (0, T), (T, W)):
                        dve.scalar_tensor_tensor(stay[:, :, a:b], z, 0.0, x[:, :, a:b], ALU.max, ALU.add)
                        last = dve.scalar_tensor_tensor(w[:, :, a:b], z, 0.0, x[:, :, a:b], ALU.min, ALU.subtract)
                    k.then(dve, "dve", last)
                    for j in range(G):
                        for a in (0, T):
                            last = dve.tensor_tensor(stay[:, j, a:a + P], stay[:, j, a:a + P], before, ALU.mult)
                    last.then_inc(s["stay"], 1)

                def exponents(g):
                    if g >= NG:
                        return
                    z0, z1 = scores(g)
                    w = lb[g % 2]
                    dve.wait_ge(s["later"], g + 1)
                    dve.tensor_tensor(w[:, :, 0:T], w[:, :, 0:T], z0, ALU.subtract)
                    dve.tensor_tensor(w[:, :, T:W], w[:, :, T:W], z1, ALU.subtract).then_inc(s["exponent"], 1)

                def weights(g):
                    if g >= NG:
                        return
                    w = lb[g % 2]
                    dve.wait_ge(s["exp"], g + 1)
                    for j in range(G):
                        for a in (0, T):
                            last = dve.tensor_tensor(w[:, j, a:a + P], w[:, j, a:a + P], before, ALU.mult)
                    last.then_inc(s["weights"], 1)

                keys(0)
                keys(1)
                splits(0)
                for g in range(NG):
                    exponents(g)
                    weights(g)
                    dve.wait_ge(s["hi"], g + 1)
                    dve.tensor_tensor(lo[:, G * g:G * (g + 1), :], bank(g, 0).rearrange("p (j n) -> p j n", j=G),
                                      hi[:, G * g:G * (g + 1), :].bitcast(F32), ALU.subtract).then_inc(s["lo"], 1)
                    keys(g + 2)
                    splits(g + 1)


def delta_inputs(k, proj, baT, slab, sc, s, mix):
    nc = k.nc
    H = HEADS2
    S0, S1, S2, S3, S4, S5 = (proj[:, :, 1024 * n:1024 * (n + 1)] for n in range(6))
    khat, vbeta, khatT, kbe, A = slab

    def head(x, h, a=0, b=T):
        return x[:, h // 4, (h % 4) * T + a:(h % 4) * T + b]

    order = [4, 5, 6, 7, 0, 1, 2, 3, 8, 9, 10, 11]
    k_banks, v_banks, kT_banks = (3, 5, 6, 7), (0, 1, 2, 3), (5, 6, 7, 4)

    with nc.Block() as block:
        @block.tensor
        def _(pe):
            for t in range(TT):
                last = pe.transpose(k.ps[:, 7, t * 16:(t + 1) * 16], baT[:, t * P:(t + 1) * P],
                                    k.ident[0:16, 0:16])
            last.then_inc(s["ba_rows"], 1)

            def rows(x, n, bank):
                t, q = n // 2, n % 2
                for j in range(4):
                    last = pe.transpose(k.ps[:, bank, j * P:(j + 1) * P], head(x, 4 * q + j, t * P, (t + 1) * P),
                                        k.const(C_ID))
                last.then_inc(s["rows"], 1)

            for n, c in enumerate(order):
                if n == 10:
                    pe.wait_ge(s["silu"], 1)
                    pe.wait_ge(s["x"], 1)
                    for m, bank in enumerate(k_banks):
                        rows(S1, m, bank)
                if n >= 3:
                    pe.wait_ge(s["taps"], n - 2)
                for j in range(2):
                    for t in range(TT):
                        last = pe.transpose(k.ps[:, n % 3, j * T + t * P:j * T + (t + 1) * P],
                                            proj[:, t, GQ + (2 * c + j) * P:GQ + (2 * c + j + 1) * P], k.const(C_ID))
                last.then_inc(s["channels"], 1)
            pe.wait_ge(s["squares"], 2)
            for n, x in enumerate((S3, S4)):
                for h in range(H):
                    for t in range(TT):
                        at = n * 16 + t * H + h
                        last = pe.matmul(k.ps[:, 4, at:at + 1], head(x, h, t * P, (t + 1) * P),
                                         k.consts[:, C_ONES, 0:1], start=True, stop=True)
            last.then_inc(s["sums"], 1)
            pe.wait_ge(s["g"], 1)
            pe.wait_ge(s["sums2"], 1)
            for t in range(TT):
                pe.matmul(k.ps[:, 4, 64 + 8 * t:72 + 8 * t], k.const(C_CUM), sc["g"][:, t, :], start=True, stop=True)
                pe.matmul(k.ps[:, 4, 80 + 8 * t:88 + 8 * t], k.const(C_AFT), sc["g"][:, t, :], start=True, stop=True)
            for c in range(4):
                last = pe.matmul(k.ps[:, 4, 96 + 8 * c:104 + 8 * c], k.const(C_HALF + c % 2), sc["g"][:, c // 2, :],
                                 start=True, stop=True)
            last.then_inc(s["gsums"], 1)
            pe.wait_ge(s["silu"], 3)
            for m, bank in enumerate(v_banks):
                if bank == 3:
                    pe.wait_ge(s["khat"], 1)
                rows(S2, m, bank)
            pe.wait_ge(s["khat"], 4)
            for n, bank in enumerate(kT_banks):
                if bank == 4:
                    pe.wait_ge(s["exps"], 1)
                for j in range(2):
                    for t in range(TT):
                        h = 2 * n + j
                        last = pe.transpose(k.ps[:, bank, j * T + t * P:j * T + (t + 1) * P],
                                            khat[:, t, h * P:(h + 1) * P], k.const(C_ID))
                last.then_inc(s["khatT"], 1)

        @block.scalar
        def _(act):
            act.wait_ge(s["ba_rows"], 1)
            ba = k.ps[:, 7, 0:32].rearrange("p (t n) -> p t n", t=TT)
            for t in range(TT):
                last = act.activation(sc["beta"][:, t, :], ba[:, t, 0:8], ACT.Sigmoid, scale=mix.scale(t))
            last.then_inc(s["beta"], 1)
            act.wait_ge(s["x"], 1)
            k.then(act, "act", act.activation(sc["ln"], sc["x"], ACT.Abs))
            k.then(act, "act", act.activation(sc["ln"], sc["ln"], ACT.Exp, scale=-1.0))
            act.activation(sc["ln"], sc["ln"], ACT.Ln, bias=1.0)
            act.activation(sc["ea"], k.col("alog", 0, 8), ACT.Exp).then_inc(s["x"], 1)

            def silu(x, count, squares=None):
                act.wait_ge(s["taps"], 4 * count)
                act.activation(x, x, ACT.Silu).then_inc(s["silu"], 1)
                if squares is not None:
                    act.wait_ge(s["silu"], count)
                    act.activation(squares, x, ACT.Square).then_inc(s["squares"], 1)

            for n, c in enumerate(order):
                if n == 6:
                    silu(S1, 1, S4)
                if n == 10:
                    silu(S0, 2, S3)
                act.wait_ge(s["channels"], n + 1)
                for j in range(2):
                    m = 2 * c + j
                    last = act.activation(head((S0, S1, S2)[m // 8], m % 8), k.ps[:, n % 3, j * T:(j + 1) * T],
                                          ACT.Copy, scale=k.col("conv", 4 * m + 3))
                last.then_inc(s["tap0"], 1)
            act.activation(proj[:, :, GZ:GZ + 1024], proj[:, :, GZ:GZ + 1024], ACT.Silu)
            silu(S2, 3)
            act.wait_ge(s["sums2"], 1)
            act.activation(sc["norms"], sc["norms"], ACT.Sqrt).then_inc(s["sums2"], 1)
            act.wait_ge(s["gsums"], 1)
            act.activation(sc["exps"], k.ps[:, 4, 64:128], ACT.Exp).then_inc(s["exps"], 1)
            for n in range(4):
                act.wait_ge(s["rows"], 5 + n)
                t, q = n // 2, n % 2
                for j in range(4):
                    h = 4 * q + j
                    last = act.activation(vbeta[:, t, h * P:(h + 1) * P],
                                          k.ps[:, v_banks[n], j * P:(j + 1) * P], ACT.Copy,
                                          scale=sc["beta"][:, t, h:h + 1])
            for n in (1, 3):
                act.wait_ge(s["khatT"], n + 1)
                act.copy(khatT[:, n // 2, (n % 2) * 2 * T:(n % 2 + 1) * 2 * T], k.ps[:, kT_banks[n], :])

        @block.gpsimd
        def _(pool):
            pool.wait_ge(s["g"], 1)
            for t in range(TT):
                for h in range(H):
                    pool.tensor_scalar(A[:, t, h * P:(h + 1) * P], k.const(C_AFT), sc["g"][:, t, h:h + 1], None,
                                       ALU.mult)

        @block.vector
        def _(dve):
            dve.wait_ge(s["beta"], 1)
            ba = k.ps[:, 7, 0:32].rearrange("p (t n) -> p t n", t=TT)
            for t in range(TT):
                last = dve.scalar_tensor_tensor(sc["x"][:, t, :], ba[:, t, 8:16], mix.scale(t), k.col("dtb", 0, 8),
                                                ALU.mult, ALU.add)
            last.then_inc(s["x"], 1)
            dve.wait_ge(s["x"], 2)
            k.then(dve, "dve", dve.scalar_tensor_tensor(sc["x"], sc["x"], 0.0, sc["ln"], ALU.max, ALU.add))
            for t in range(TT):
                last = dve.scalar_tensor_tensor(sc["g"][:, t, :], sc["x"][:, t, :], -1.0, sc["ea"], ALU.mult, ALU.mult)
            last.then_inc(s["g"], 1)
            for n, c in enumerate(order):
                dve.wait_ge(s["tap0"], n + 1)
                for tap in range(1, 4):
                    for j in range(2):
                        m = 2 * c + j
                        y = head((S0, S1, S2)[m // 8], m % 8, tap, T)
                        last = dve.scalar_tensor_tensor(y, k.ps[:, n % 3, j * T:(j + 1) * T - tap],
                                                        k.col("conv", 4 * m + 3 - tap), y, ALU.mult, ALU.add)
                    if tap < 3:
                        k.then(dve, "dve", last)
                last.then_inc(s["taps"], 1)
            dve.wait_ge(s["sums"], 1)
            dve.tensor_scalar(sc["norms"], k.ps[:, 4, 0:32], EPS, None, ALU.add).then_inc(s["sums2"], 1)
            dve.wait_ge(s["sums2"], 2)
            k.then(dve, "dve", dve.reciprocal(sc["rnorms"], sc["norms"]))
            for n in range(4):
                dve.wait_ge(s["rows"], n + 1)
                t, q = n // 2, n % 2
                for j in range(4):
                    h = 4 * q + j
                    last = dve.tensor_scalar(khat[:, t, h * P:(h + 1) * P], k.ps[:, k_banks[n], j * P:(j + 1) * P],
                                             sc["rnorms"][:, 16 + t * H + h:17 + t * H + h], None, ALU.mult)
                last.then_inc(s["khat"], 1)
            dve.wait_ge(s["exps"], 1)
            dve.tensor_tensor(sc["be"], sc["beta"], sc["exps"][:, 0:16].rearrange("p (t n) -> p t n", t=TT), ALU.mult)
            dve.tensor_scalar(sc["rnorms"][:, 0:16], sc["rnorms"][:, 0:16], float(P) ** -0.5, None, ALU.mult)
            for n in (0, 2):
                dve.wait_ge(s["khatT"], n + 1)
                dve.tensor_copy(khatT[:, n // 2, (n % 2) * 2 * T:(n % 2 + 1) * 2 * T], k.ps[:, kT_banks[n], :])


def delta_matrices(k, proj, slab, sc, s):
    nc = k.nc
    H, NG = HEADS2, 4
    S0, S1, S2, S3, S4, S5 = (proj[:, :, 1024 * n:1024 * (n + 1)] for n in range(6))
    khat, vbeta, khatT, kbe, A = slab
    decT, dec, L, LT, Tm, TmT, Cm, Y, G, ecs = S3, S4, S5, S2, S4, S1, A, khatT, S1, A

    def head(x, h, a=0, b=T):
        return x[:, h // 4, (h % 4) * T + a:(h % 4) * T + b]

    def group(x, g):
        return x[:, g // 2, (g % 2) * 512:(g % 2 + 1) * 512]

    def one(x, g, j):
        return x[:, g // 2, (g % 2) * 512 + j * P:(g % 2) * 512 + (j + 1) * P]

    def each(c):
        return k.const(c).unsqueeze(1).broadcast_to([P, 4, P])

    def four(x):
        return x.rearrange("p (j n) -> p j n", j=4)

    with nc.Block() as block:
        @block.tensor
        def _(pe):
            cum = k.const(C_CUM)
            for g in range(NG):
                for j in range(4):
                    last = pe.matmul(k.ps[:, g, j * P:(j + 1) * P], one(A, g, j), cum, start=True, stop=True)
                last.then_inc(s["logT"], 1)
                pe.matmul(k.ps[:, 4 + g, :], cum, group(A, g), start=True, stop=True).then_inc(s["log"], 1)
            for g in range(NG):
                t = g // 2
                pe.wait_ge(s["decT"], g + 1)
                for j in range(4):
                    h = 4 * (g % 2) + j
                    last = pe.matmul(k.ps[:, g, j * P:(j + 1) * P], head(khatT, h, t * P, (t + 1) * P),
                                     head(S0, h, t * P, (t + 1) * P), start=True, stop=True)
                last.then_inc(s["qk"], 1)
            for g in range(NG):
                t = g // 2
                pe.wait_ge(s["dec"], g + 1)
                for j in range(4):
                    h = 4 * (g % 2) + j
                    kk = head(khatT, h, t * P, (t + 1) * P)
                    last = pe.matmul(k.ps[:, 4 + g, j * P:(j + 1) * P], kk, kk, start=True, stop=True)
                last.then_inc(s["kk"], 1)
            for g in range(NG):
                pe.wait_ge(s["attn"], g + 1)
                pe.wait_ge(s["G"], 1)
                for j in range(4):
                    last = pe.matmul(k.ps[:, g, j * P:(j + 1) * P], one(G, g, j), cum, start=True, stop=True)
                last.then_inc(s["cs"], 1)
            for g in range(NG):
                pe.wait_ge(s["L"], g + 1)
                for j in range(4):
                    last = pe.transpose(k.ps[:, 4 + g, j * P:(j + 1) * P], one(L, g, j), k.const(C_ID))
                last.then_inc(s["LT"], 1)
            for g in range(NG):
                pe.wait_ge(s["TT"], g + 1)
                for j in range(4):
                    last = pe.transpose(k.ps[:, g, j * P:(j + 1) * P], one(TmT, g, j), k.const(C_ID))
                last.then_inc(s["T0"], 1)
            for lv in range(1, LEVELS):
                done = (lv - 1) * NG
                for g in range(NG):
                    pe.wait_ge(s["C"], done + g + 1)
                    pe.wait_ge(s["T"], done + g + 1)
                    for j in range(4):
                        last = pe.matmul(k.ps[:, g, j * P:(j + 1) * P], one(Cm, g, j), one(Tm, g, j), start=True,
                                         stop=True)
                    last.then_inc(s["Y"], 1)
                for g in range(NG):
                    pe.wait_ge(s["Ys"], done + g + 1)
                    for j in range(4):
                        last = pe.matmul(k.ps[:, 4 + g, j * P:(j + 1) * P], one(Y, g, j), one(TmT, g, j), start=True,
                                         stop=True)
                    last.then_inc(s["ZT"], 1)
                    if lv < LEVELS - 1:
                        for j in range(4):
                            last = pe.matmul(k.ps[:, g, j * P:(j + 1) * P], one(TmT, g, j), one(Y, g, j), start=True,
                                             stop=True)
                        last.then_inc(s["Z"], 1)
            for g in range(NG):
                t = g // 2
                pe.wait_ge(s["TT"], LEVELS * NG - NG + g + 1)
                for j in range(4):
                    last = pe.matmul(k.ps[:, g, j * P:(j + 1) * P], one(TmT, g, j), one(vbeta, g, j), start=True,
                                     stop=True)
                last.then_inc(s["u"], 1)
                if g == 0:
                    pe.wait_ge(s["kbe"], 1)
                for j in range(4):
                    last = pe.matmul(k.ps[:, 4 + g, j * P:(j + 1) * P], one(kbe, g, j), one(TmT, g, j), start=True,
                                     stop=True)
                last.then_inc(s["w"], 1)

        @block.gpsimd
        def _(pool):
            def scaled(dst, src, by):
                for t in range(TT):
                    for h in range(H):
                        at = slice(h * P, (h + 1) * P)
                        last = pool.tensor_scalar(dst[:, t, at], src(t, at), by(t, h), None, ALU.mult)
                return last
            scaled(G, lambda t, at: k.const(C_ONES), lambda t, h: sc["g"][:, t, h:h + 1]).then_inc(s["G"], 1)
            scaled(kbe, lambda t, at: khat[:, t, at], lambda t, h: sc["be"][:, t, h:h + 1]).then_inc(s["kbe"], 1)
            pool.wait_ge(s["kbe"], 1)
            scaled(khat, lambda t, at: khat[:, t, at], lambda t, h: sc["exps"][:, 16 + t * H + h:17 + t * H + h])

        @block.scalar
        def _(act):
            for g in range(NG):
                act.wait_ge(s["logT"], g + 1)
                act.activation(group(decT, g), k.ps[:, g, :], ACT.Exp).then_inc(s["decT"], 1)
                act.wait_ge(s["log"], g + 1)
                act.activation(group(dec, g), k.ps[:, 4 + g, :], ACT.Exp).then_inc(s["dec"], 1)
            for g in range(NG):
                act.wait_ge(s["cs"], g + 1)
                act.activation(group(ecs, g), k.ps[:, g, :], ACT.Exp).then_inc(s["ecs"], 1)
            ahead_hi(k, act)
            for g in range(NG):
                act.wait_ge(s["LT"], g + 1)
                act.copy(group(LT, g), k.ps[:, 4 + g, :]).then_inc(s["LTs"], 1)
            for g in range(NG):
                act.wait_ge(s["T0"], g + 1)
                act.copy(group(Tm, g), k.ps[:, g, :]).then_inc(s["T"], 1)
            for lv in range(1, LEVELS):
                for g in range(NG):
                    act.wait_ge(s["Y"], (lv - 1) * NG + g + 1)
                    act.copy(group(Y, g), k.ps[:, g, :]).then_inc(s["Ys"], 1)
            for g in range(NG):
                act.wait_ge(s["w"], g + 1)
                act.copy(group(S4, g), k.ps[:, 4 + g, :]).then_inc(s["ws"], 1)

        @block.vector
        def _(dve):
            for g in range(NG):
                dve.wait_ge(s["decT"], g + 1)
                last = dve.tensor_tensor(four(group(decT, g)), four(group(decT, g)), each(C_CUM), ALU.mult)
                dve.wait_ge(s["dec"], g + 1)
                last = dve.tensor_tensor(four(group(dec, g)), four(group(dec, g)), each(C_AFT), ALU.mult)
            k.then(dve, "dve", last)
            for g in range(NG):
                dve.wait_ge(s["qk"], g + 1)
                dve.tensor_tensor(group(decT, g), k.ps[:, g, :], group(decT, g), ALU.mult).then_inc(s["attn"], 1)
            for g in range(NG):
                dve.wait_ge(s["kk"], g + 1)
                for j in range(4):
                    h = 4 * (g % 2) + j
                    last = dve.scalar_tensor_tensor(one(L, g, j), k.ps[:, 4 + g, j * P:(j + 1) * P],
                                                    sc["beta"][:, g // 2, h:h + 1], one(dec, g, j), ALU.mult,
                                                    ALU.mult)
                last.then_inc(s["L"], 1)
            for g in range(NG):
                dve.wait_ge(s["ecs"], g + 1)
                t, q = g // 2, g % 2
                qT = S0[:, q, :].rearrange("p (j n) -> p j n", j=4)[:, :, t * P:(t + 1) * P]
                last = dve.tensor_tensor(qT, qT, four(group(ecs, g)), ALU.mult)
            k.then(dve, "dve", last)
            for g in range(NG):
                dve.wait_ge(s["LTs"], g + 1)
                k.then(dve, "dve", dve.tensor_tensor(four(group(TmT, g)), four(group(LT, g)), each(C_LVL), ALU.mult))
                dve.tensor_tensor(four(group(TmT, g)), each(C_ID), four(group(TmT, g)), ALU.subtract)\
                    .then_inc(s["TT"], 1)
            for g in range(NG):
                dve.tensor_tensor(four(group(Cm, g)), four(group(LT, g)), each(C_LVL + 1), ALU.mult)\
                    .then_inc(s["C"], 1)
            ahead_lo(k, dve)
            for lv in range(1, LEVELS):
                done = (lv - 1) * NG
                for g in range(NG):
                    dve.wait_ge(s["ZT"], done + g + 1)
                    if lv < LEVELS - 1:
                        dve.wait_ge(s["Z"], done + g + 1)
                    dve.wait_ge(s["TT"], done + g + 1)
                    dve.tensor_tensor(group(TmT, g), group(TmT, g), k.ps[:, 4 + g, :], ALU.subtract)\
                        .then_inc(s["TT"], 1)
                    if lv < LEVELS - 1:
                        dve.wait_ge(s["T"], done + g + 1)
                        dve.tensor_tensor(group(Tm, g), group(Tm, g), k.ps[:, g, :], ALU.subtract)\
                            .then_inc(s["T"], 1)
                        dve.tensor_tensor(four(group(Cm, g)), four(group(LT, g)), each(C_LVL + lv + 1), ALU.mult)\
                            .then_inc(s["C"], 1)
            for g in range(NG):
                dve.wait_ge(s["u"], g + 1)
                dve.tensor_copy(group(S5, g), k.ps[:, g, :]).then_inc(s["us"], 1)


def delta_recurrence(k, proj, slab, sc, s):
    nc = k.nc
    H = HEADS2
    S0, S1, S2, S3, S4, S5 = (proj[:, :, 1024 * n:1024 * (n + 1)] for n in range(6))
    ktail, vbeta, khatT, kbe, A = slab
    attn, wT, u, vn, o = S3, S4, S5, S2, A
    state = khatT[:, 0, :]

    with nc.Block() as block:
        @block.tensor
        def _(pe):
            for c in range(4):
                t, p = c // 2, CH * (c % 2)
                rows = slice(p, p + CH)
                if c:
                    pe.wait_ge(s["S"], c)
                    for h in range(H):
                        last = pe.matmul(k.ps[rows, h // 4, (h % 4) * P:(h % 4 + 1) * P],
                                         wT[:, t, h * P + p:h * P + p + CH], state[:, h * P:(h + 1) * P],
                                         start=True, stop=True)
                    last.then_inc(s["wS"], 1)
                    pe.wait_ge(s["o"], c)
                    for h in range(H):
                        q = S0[:, h // 4, (h % 4) * T + c * CH:(h % 4) * T + (c + 1) * CH]
                        last = pe.matmul(k.ps[rows, 6 + h // 4, (h % 4) * P:(h % 4 + 1) * P], q,
                                         state[:, h * P:(h + 1) * P], start=True, stop=True)
                    last.then_inc(s["qS"], 1)
                pe.wait_ge(s["vn"], c + 1)
                if c < 3:
                    for h in range(H):
                        last = pe.matmul(k.ps[:, 4 + h // 4, (h % 4) * P:(h % 4 + 1) * P],
                                         ktail[rows, t, h * P:(h + 1) * P], vn[rows, t, h * P:(h + 1) * P],
                                         start=True, stop=True)
                    last.then_inc(s["kv"], 1)
                for h in range(H):
                    last = pe.matmul(k.ps[rows, 2 + h // 4, (h % 4) * P:(h % 4 + 1) * P],
                                     attn[rows, t, h * P + p:h * P + p + CH], vn[rows, t, h * P:(h + 1) * P],
                                     start=True, stop=True)
                last.then_inc(s["av"], 1)

        @block.scalar
        def _(act):
            for c in range(4):
                t, p = c // 2, CH * (c % 2)
                act.wait_ge(s["av"], c + 1)
                act.copy(o[p:p + CH, t, :], k.ps[p:p + CH, 2:4, :].rearrange("p b n -> p (b n)"))\
                    .then_inc(s["o"], 1)

        @block.vector
        def _(dve):
            for c in range(4):
                t, p = c // 2, CH * (c % 2)
                rows = slice(p, p + CH)
                if c == 0:
                    dve.tensor_copy(vn[rows, t, :], u[rows, t, :]).then_inc(s["vn"], 1)
                else:
                    dve.wait_ge(s["wS"], c)
                    dve.tensor_tensor(vn[rows, t, :], u[rows, t, :],
                                      k.ps[rows, 0:2, :].rearrange("p b n -> p (b n)"), ALU.subtract)\
                        .then_inc(s["vn"], 1)
                if c < 3:
                    dve.wait_ge(s["kv"], c + 1)
                    kv = k.ps[:, 4:6, :].rearrange("p b n -> p (b n)")
                    if c == 0:
                        dve.tensor_copy(state, kv).then_inc(s["S"], 1)
                    else:
                        dve.wait_ge(s["qS"], c)
                        dve.wait_ge(s["S"], c)
                        for h in range(H):
                            at = slice(h * P, (h + 1) * P)
                            last = dve.scalar_tensor_tensor(state[:, at], state[:, at],
                                                            sc["exps"][:, 32 + 8 * c + h:33 + 8 * c + h], kv[:, at],
                                                            ALU.mult, ALU.add)
                        last.then_inc(s["S"], 1)
                if c:
                    dve.wait_ge(s["o"], c + 1)
                    dve.wait_ge(s["qS"], c)
                    last = dve.tensor_tensor(o[rows, t, :], o[rows, t, :],
                                             k.ps[rows, 6:8, :].rearrange("p b n -> p (b n)"), ALU.add)
                    last.then_inc(s["oS"], 1)

    def tail_act(act):
        for t in range(TT):
            for h in range(H):
                at = slice(h * P, (h + 1) * P)
                last = act.activation(S1[:, t, at], o[:, t, at], ACT.Square,
                                      accum_out=sc["oss"][:, t * H + h:t * H + h + 1])
        last.then_inc(s["oss"], 1)
        act.wait_ge(s["oss"], 2)
        act.activation(sc["oss"], sc["oss"], ACT.Sqrt).then_inc(s["oss"], 1)

    def tail_dve(dve):
        rn = sc["rnorms"][:, 0:16]
        k.then(dve, "dve", dve.tensor_tensor(sc["rn2"], rn, rn, ALU.mult))
        dve.wait_ge(s["oss"], 1)
        k.then(dve, "dve", dve.tensor_tensor(sc["oss"], sc["oss"], sc["rn2"], ALU.mult))
        dve.tensor_scalar(sc["oss"], sc["oss"], 1.0 / P, EPS, ALU.mult, ALU.add).then_inc(s["oss"], 1)
        dve.wait_ge(s["oss"], 3)
        k.then(dve, "dve", dve.reciprocal(sc["orn"], sc["oss"]))
        k.then(dve, "dve", dve.tensor_tensor(sc["orn"], sc["orn"], rn, ALU.mult))
        for t in range(TT):
            for h in range(H):
                at = slice(h * P, (h + 1) * P)
                last = dve.scalar_tensor_tensor(o[:, t, at], o[:, t, at], sc["orn"][:, t * H + h:t * H + h + 1],
                                                proj[:, t, GZ + h * P:GZ + (h + 1) * P], ALU.mult, ALU.mult)
        last.then_inc(s["y"], 1)
    return o, (tail_act, tail_dve, (s["y"], 1))


def gated_delta(k, ctx, proj, baT, mix):
    names = ("ba_rows", "taps", "channels", "squares", "sums", "silu", "khat", "rows", "g", "gsums", "khatT", "beta",
             "x", "tap0", "sums2", "exps", "kbe", "logT", "log", "decT", "dec", "qk", "kk", "attn", "G", "cs",
             "L", "LT", "TT", "T0", "C", "T", "Y", "Ys", "ZT", "Z", "u", "w", "ecs", "LTs", "us", "ws", "S", "wS",
             "o", "qS", "vn", "kv", "av", "y", "oss", "oS")
    s = {n: k.sem(f"delta_{n}") for n in names}
    slab = [k.sb(f"delta_{n}", [P, TT, 1024], F32, ctx) for n in ("khat", "vbeta", "khatT", "kbe", "A")]
    sc = {}
    for n, shape in (("beta", [TT, 8]), ("x", [TT, 8]), ("ln", [TT, 8]), ("g", [TT, 8]), ("be", [TT, 8]),
                     ("ea", [8]), ("norms", [32]), ("rnorms", [32]), ("exps", [64]), ("oss", [16]), ("rn2", [16]), ("orn", [16])):
        sc[n] = k.sb(f"delta_s_{n}", [P, *shape], F32, ctx)[:]
    delta_inputs(k, proj, baT, slab, sc, s, mix)
    delta_matrices(k, proj, slab, sc, s)
    return delta_recurrence(k, proj, slab, sc, s)


def memory_attention(k, q, kv, xa_hi, xa_lo, sp_work):
    nc = k.nc
    H = 4
    scale = float(P) ** -0.5
    s = {n: k.sem(f"mem_{n}") for n in ("qk", "qT", "kT", "scored", "neg", "exp", "normed", "pt", "ptc", "out", "hi",
                                        "lo")}
    with ExitStack() as ctx:
        qT = k.sb("mem_qT", [P, H, T], F32, ctx)
        kT = k.sb("mem_kT", [P, H, T], F32, ctx)
        pr = k.sb("mem_p", [P, 2 * H, T], F32, ctx)
        pt = k.sb("mem_pT", [P, 2 * H, T], F32, ctx)
        st = k.sb("mem_st", [P, 4, 2 * H], F32, ctx)
        with nc.Block() as block:
            @block.sync
            def _(sp):
                sp_work(sp)

            @block.tensor
            def _(pe):
                for bank, x in ((0, q), (2, kv)):
                    for h in range(H):
                        for t in range(TT):
                            last = pe.transpose(
                                k.ps[:, bank + h // 2, (h % 2) * T + t * P:(h % 2) * T + (t + 1) * P],
                                x[:, t, h * P:(h + 1) * P], k.const(C_ID))
                last.then_inc(s["qk"], 1)
                pe.wait_ge(s["qT"], 1)
                pe.wait_ge(s["kT"], 1)
                for h in range(H):
                    for t in range(TT):
                        last = pe.matmul(k.ps[:, 4 + h, t * T:(t + 1) * T], qT[:, h, t * P:(t + 1) * P], kT[:, h, :],
                                         start=True, stop=True)
                last.then_inc(s["scored"], 1)
                pe.wait_ge(s["normed"], 1)
                for h in range(H):
                    for m in range(TT):
                        for t in range(TT):
                            last = pe.transpose(k.ps[:, h, m * T + t * P:m * T + (t + 1) * P],
                                                pr[:, TT * h + t, m * P:(m + 1) * P], k.const(C_ID))
                last.then_inc(s["pt"], 1)
                pe.wait_ge(s["ptc"], 2)
                for h in range(H):
                    for m in range(TT):
                        last = pe.matmul(k.ps[:, 4 + h // 2, (h % 2) * T:(h % 2 + 1) * T],
                                         kv[:, m, 512 + h * P:512 + (h + 1) * P], pt[:, TT * h + m, :],
                                         start=(m == 0), stop=(m == 1))
                last.then_inc(s["out"], 1)

            @block.scalar
            def _(act):
                act.wait_ge(s["qk"], 1)
                act.activation(qT[:], k.ps[:, 0:2, :].rearrange("p b (j n) -> p (b j) n", j=2), ACT.Copy,
                               scale=scale).then_inc(s["qT"], 1)
                act.wait_ge(s["neg"], 1)
                for n in range(2 * H):
                    last = act.activation(pr[:, n, :], k.ps[:, 4 + n // 2, (n % 2) * T:(n % 2 + 1) * T], ACT.Exp,
                                          bias=st[:, 1, n:n + 1], accum_out=st[:, 2, n:n + 1])
                last.then_inc(s["exp"], 1)
                ahead_hi(k, act)
                act.wait_ge(s["pt"], 1)
                act.copy(pt[:, 0:4, :], k.ps[:, 0:2, :].rearrange("p b (j n) -> p (b j) n", j=2))\
                    .then_inc(s["ptc"], 1)
                act.wait_ge(s["out"], 1)
                act.copy(xa_hi[:], k.ps[:, 4:6, :].rearrange("p b (j n) -> p (b j) n", j=2)).then_inc(s["hi"], 1)

            @block.vector
            def _(dve):
                dve.wait_ge(s["qk"], 1)
                dve.tensor_copy(kT[:], k.ps[:, 2:4, :].rearrange("p b (j n) -> p (b j) n", j=2)).then_inc(s["kT"], 1)
                dve.wait_ge(s["scored"], 1)
                k.then(dve, "dve", dve.tensor_reduce(st[:, 0, :],
                                                     k.ps[:, 4:8, :].rearrange("p b (j n) -> p (b j) n", j=2), AX.X,
                                                     ALU.max))
                dve.tensor_scalar(st[:, 1, :], st[:, 0, :], -1.0, None, ALU.mult).then_inc(s["neg"], 1)
                dve.wait_ge(s["exp"], 1)
                k.then(dve, "dve", dve.reciprocal(st[:, 3, :], st[:, 2, :]))
                for n in range(2 * H):
                    last = dve.tensor_scalar(pr[:, n, :], pr[:, n, :], st[:, 3, n:n + 1], None, ALU.mult)
                last.then_inc(s["normed"], 1)
                ahead_lo(k, dve)
                dve.wait_ge(s["pt"], 1)
                dve.tensor_copy(pt[:, 4:8, :], k.ps[:, 2:4, :].rearrange("p b (j n) -> p (b j) n", j=2))\
                    .then_inc(s["ptc"], 1)
                dve.wait_ge(s["hi"], 1)
                dve.tensor_tensor(xa_lo[:], k.ps[:, 4:6, :].rearrange("p b (j n) -> p (b j) n", j=2),
                                  xa_hi[:].bitcast(F32), ALU.subtract).then_inc(s["lo"], 1)


def conv_hidden(k, stage, cv, hT_hi, hT_lo, tb):
    s = {n: k.sem(f"ffn2_{n}") for n in ("turned", "tap0", "tap1", "taps", "silu", "hid", "hi", "lo")}
    flat_hi, flat_lo = (x.rearrange("p c n -> p (c n)") for x in (hT_hi, hT_lo))
    at0 = COLS["fconv"][0]

    def weight(i, n, tap):
        return k.cols[:, bass.ds(at0 + 3 * ((n // 4) * HC + n % 4) + tap + i * 12, 1)]

    def bias(i, n):
        return k.cols[:, bass.ds(COLS["fbias"][0] + (n // 4) * HC + n % 4 + i * 4, 1)]

    def pe_hook(pe, i):
        pe.wait_ge(k.act_free, 2 + tb + 1 + 2 * i)
        pe.wait_ge(k.dve_free, 2 + tb + 2 + 2 * i)
        pe.wait_ge(s["taps"], 4 * i)
        for b in range(4):
            for j in range(2):
                c = 2 * (b % 2) + j
                for t in range(TT):
                    last = pe.transpose(k.ps[:, 4 + b, j * T + t * P:j * T + (t + 1) * P],
                                        stage[:, b // 2, t, c * P:(c + 1) * P], k.ident[:])
        last.then_inc(s["turned"], 1)

    def tap0(b):
        def hook(act, i):
            if b == 0:
                act.wait_ge(s["turned"], 1 + i)
                act.wait_ge(s["lo"], i)
            for n in (2 * b, 2 * b + 1):
                last = act.activation(cv[:, n, :], k.ps[:, 4 + n // 2, (n % 2) * T:(n % 2 + 1) * T], ACT.Identity,
                                      scale=weight(i, n, 2), bias=bias(i, n))
            last.then_inc(s["tap0"], 1)
        return hook

    def taps(b):
        def hook(dve, i):
            dve.wait_ge(s["tap0"], 1 + b + 4 * i)
            for tap, sem in ((1, "tap1"), (2, "taps")):
                for n in (2 * b, 2 * b + 1):
                    y = cv[:, n, tap:T]
                    last = dve.scalar_tensor_tensor(y, k.ps[:, 4 + n // 2, (n % 2) * T:(n % 2 + 1) * T - tap],
                                                    weight(i, n, 2 - tap), y, ALU.mult, ALU.add)
                last.then_inc(s[sem], 1)
                if tap == 1:
                    dve.wait_ge(s["tap1"], 1 + b + 4 * i)
        return hook

    def silu(act, i):
        act.wait_ge(s["taps"], 2 + 4 * i)
        act.activation(cv[:, 0:4, :], cv[:, 0:4, :], ACT.Silu).then_inc(s["silu"], 1)

    def mult(dve, i):
        dve.wait_ge(s["silu"], 1 + i)
        dve.wait_ge(s["taps"], 4 + 4 * i)
        dve.tensor_tensor(cv[:, 0:4, :], cv[:, 0:4, :], cv[:, 4:8, :], ALU.mult).then_inc(s["hid"], 1)

    def part(x, i):
        return x[:, bass.ds(i * (4 * T), 4 * T)]

    def high(act, i):
        act.wait_ge(s["hid"], 1 + i)
        act.copy(part(flat_hi, i), cv[:, 0:4, :].rearrange("p c n -> p (c n)")).then_inc(s["hi"], 1)

    def low(dve, i):
        dve.wait_ge(s["hi"], 1 + i)
        dve.tensor_tensor(part(flat_lo, i), cv[:, 0:4, :].rearrange("p c n -> p (c n)"),
                          part(flat_hi, i).bitcast(F32), ALU.subtract).then_inc(s["lo"], 1)
    return s, [("pe", 5, pe_hook)] + [("act", 7 + b, tap0(b)) for b in range(4)] \
        + [("dve", 8 + b, taps(b)) for b in range(4)] \
        + [("act", 12, silu), ("dve", 13, mult), ("act", 14, high), ("dve", 15, low)]


def in2_tiles(w, hi, lo):
    return [Tile(w, DC, lambda i, m=m: i * (2 * NT) + m * NT, hi, lo) for m in range(2)]


def second_block_mix(k, a, hi, lo, xq_tiles_of):
    nc = k.nc
    tiles = in2_tiles(a["w_in_2"], hi, lo)
    out_tiles = square_tiles(a["w_out_2"], DC, hi, lo)
    with ExitStack() as life:
        proj = k.sb("proj2", [P, TT, 7 * 1024], F32, life)
        mix = Rows(k, life, k.h, DC, lambda c: k.col("g_mix2", c), hi, lo, normed=True, summed=True)
        with ExitStack() as mid:
            low = Narrow(k, "low2", mid)
            product(k, tiles, 7, *copy_evacs(k, proj, stream_col, mix),
                    sp_first=lambda sp: low.load(sp, a["w_in_2"][:, GBA:GBA + 16]), pool_work=low.pad, rows=[mix],
                    once=[("act", 12, low.split_hi), ("dve", 13, low.split_lo)],
                    pe_last=lambda pe: low.product(pe, hi, lo))
        ba = k.sb("narrow_out", [16, T], F32, life)
        stick_breaking(k, proj, ba[:], hi, lo, lambda sp: prefetch(k, sp, out_tiles, k.unit))
        k.narrow_done += Narrow.STEPS
        o, tail = gated_delta(k, life, proj, ba[:], mix)
        delta = Rows(k, life, o, HEADS2, lambda c: k.col("g_gdn"), hi[:, 8:16, :], lo[:, 8:16, :], tail=tail)
        product(k, out_tiles, 2, *add_to_stream(k), after=xq_tiles_of, rows=[delta],
                rows_at=8 // UC - 1, rows_need=8 // UC)


def second_block_memory(k, a, hi, lo, mem_parts, xq_tiles, next_tiles):
    nc = k.nc
    m_hi, m_lo = mem_parts
    with ExitStack() as life:
        q = k.sb("mem_q", [P, TT, 512], F32, life)
        kv = k.sb("mem_kv", [P, TT, 1024], F32, life)
        xa = [k.sb(f"xa_{n}", [P, 4, T], F32R, life) for n in ("hi", "lo")]
        xo_tiles = [Tile(a["w_xo_2"], 4, lambda i, m=m: m * NT, *xa) for m in range(4)]
        mem_landed = [k.sem(f"mem_landed{t}") for t in range(TT)]
        mem = k.sb("mem_rows", [P, TT, D], F32, life)
        rows = [Rows(k, life, k.h, DC, lambda c: k.col("g_x2", c), hi, lo, normed=True, summed=True),
                Rows(k, life, mem, DC, lambda c: k.col("g_mem2", c), m_hi, m_lo, normed=True, landed=mem_landed,
                     which=1)]

        def act_evac(act, m, i, bank):
            if m:
                return act.copy(kv[:, 0, (m - 1) * NT:m * NT], k.ps[:, bank, :])
            act.wait_ge(*rows[0].rms_ready)
            return act.activation(q[:, 0, :], k.ps[:, bank, :], ACT.Copy, scale=rows[0].scale(0))

        def dve_evac(dve, m, i, bank):
            if m:
                return dve.tensor_copy(kv[:, 1, (m - 1) * NT:m * NT], k.ps[:, bank + 1, :])
            return dve.tensor_scalar(q[:, 1, :], k.ps[:, bank + 1, :], rows[0].scale(1), None, ALU.mult)

        def load_memory(sp):
            for t in range(TT):
                sp.dma_start(mem[:, t, :], a["mem_2"][0, t * P:(t + 1) * P, :]).then_inc(mem_landed[t], 16)
        product(k, xq_tiles, 1, act_evac, dve_evac, rows=rows, sp_first=load_memory)
        memory_attention(k, q, kv, *xa, lambda sp: prefetch(k, sp, xo_tiles, k.unit))
        product(k, xo_tiles, 1, *add_to_stream(k, 4), after=next_tiles)


def second_block_ffn(k, a, out, hi, lo, tiles):
    nc = k.nc
    with ExitStack() as life:
        hT = [k.sb(f"hT2_{n}", [P, HC, T], F32R, life) for n in ("hi", "lo")]
        cv = k.sb("ffn2_conv", [P, 8, T], F32, life)
        down = down_tiles(a["w_down_2"], *hT)
        with ExitStack() as mid:
            stage = k.sb("ffn2_rows", [P, 2, TT, NT], F32, mid)
            ffn = Rows(k, mid, k.h, DC, lambda c: k.col("g_ffn2", c), hi, lo, normed=True, summed=True)
            tb = k.tile
            s, hooks = conv_hidden(k, stage, cv, *hT, tb)

            def act_evac(act, m, i, bank):
                if m:
                    return None
                act.wait_ge(s["turned"], i)
                act.wait_ge(*ffn.rms_ready)
                for t in range(TT):
                    last = act.activation(stage[:, 0, t, :], k.ps[:, bank + t, :], ACT.Copy, scale=ffn.scale(t))
                return last

            def dve_evac(dve, m, i, bank):
                if m == 0:
                    return None
                dve.wait_ge(s["turned"], i)
                for t in range(TT):
                    last = dve.tensor_scalar(stage[:, 1, t, :], k.ps[:, bank + t, :], ffn.scale(t), None, ALU.mult)
                return last
            product(k, tiles, FF2 // NT, act_evac, dve_evac, after=down, hooks=hooks, rows=[ffn], hooks_in_next=True)
        gain = k.sb("gain_final2", [P, D], F32, life)
        s_gain, s_out = k.sem("gain_final2_landed"), k.sem("stored")
        last = FF2 // NT - 1
        late = [(e, u - 7, lambda eng, fn=fn: fn(eng, last)) for e, u, fn in hooks if e != "pe"]
        late.append(("pe_first", 4 * last // UC, lambda pe: pe.wait_ge(s["lo"], last + 1)))
        product(k, down, 2, *add_to_stream(k), once=late,
                sp_first=lambda sp: sp.dma_start(gain[:], a["g_final2"]).then_inc(s_gain, 16))
        norm_rows(k, gain, (s_gain, 16), hT[0], False)
        with nc.Block() as block:
            @block.sync
            def _(sp):
                sp.dma_start(out.rearrange("b (t p) d -> p (b t) d", p=P), k.h[:]).then_inc(s_out, 16)
                sp.wait_ge(s_out, 16)


def build_program(nc, a, out):
    with ExitStack() as ctx:
        k = Kernel(nc, ctx)
        hi = k.sb("act_hi", [P, DC, T], F32R)
        lo = k.sb("act_lo", [P, DC, T], F32R)
        tiles2 = in2_tiles(a["w_in_2"], hi, lo)
        up_tiles = [Tile(a["w_up_2"], DC, lambda i, m=m: i * NT + m * FF2, hi, lo) for m in range(2)]
        with ExitStack() as masks:
            k.consts = k.sb("masks", [P, N_CONST, P], F32, masks)
            first_block(k, a, hi, lo, tiles2)
            with ExitStack() as late:
                q_tiles = [Tile(a["w_xq_2"], DC, lambda i: 0, hi, lo)]
                m_parts = [None, None]

                class Later(Tile):
                    pass
                kv_tiles = [Later(a["w_xkv_2"], DC, lambda i, m=m: m * NT, None, None) for m in range(2)]
                second_block_mix(k, a, hi, lo, q_tiles + kv_tiles)
                m_parts = [k.sb(f"memT_{n}", [P, DC, T], F32R, late) for n in ("hi", "lo")]
                for t in kv_tiles:
                    t.hi, t.lo = m_parts
                second_block_memory(k, a, hi, lo, m_parts, q_tiles + kv_tiles, up_tiles)
        second_block_ffn(k, a, out, hi, lo, up_tiles)




def _masks():
    import numpy as np
    c = np.zeros((P, N_CONST, P), np.float32)
    r, q = np.arange(P)[:, None], np.arange(P)[None, :]
    same = r // CH == q // CH
    c[:, C_ID] = r == q
    c[:, C_CUM] = (r <= q) & same
    c[:, C_AFT] = (r > q) & same
    c[:, C_AFTALL] = r > q
    c[:, C_BEFALL] = r < q
    c[:, C_ONES] = 1
    c[:CH, C_HALF] = 1
    c[CH:, C_HALF + 1] = 1
    for level in range(LEVELS):
        s = 1 << level
        c[:, C_LVL + level] = (r // (2 * s) == q // (2 * s)) & (r // s % 2 == 0) & (q // s % 2 == 1)
    return c


def _buckets():
    import math

    import numpy as np
    o = np.zeros((33, 3 * P), np.float32)
    for n in range(3 * P):
        d = 2 * P - 1 - n
        if d < 0 or d >= P:
            o[32, n] = 1
        elif d < 16:
            o[d, n] = 1
        else:
            o[min(31, 16 + int(math.log(d / 16) / math.log(8) * 16)), n] = 1
    return o


def kernel(**inputs):
    import numpy as np
    import concourse.bacc as bacc
    from concourse.bass_utils import run_bass_kernel_spmd

    v = {n: np.asarray(x) for n, x in inputs.items()}

    def chunks(x):
        return x.reshape(-1, P).T

    def every(x):
        return np.broadcast_to(x.reshape(1, -1), (P, x.size))
    parts = {
        "g_mix": chunks(v["norm_mix_g"]), "g_ffn": chunks(v["norm_ffn_g"]), "g_mix2": chunks(v["mix_norm_2"]),
        "g_x2": chunks(v["xattn_norm_2"]), "g_mem2": chunks(v["mem_norm_2"]), "g_ffn2": chunks(v["ffn_norm_2"]),
        "g_gla": chunks(v["gla_norm_g"]), "g_gdn": chunks(v["gdn_norm_2"]),
        "conv": v["gdn_conv_2"].reshape(4, 24, P).transpose(2, 1, 0).reshape(P, 96),
        "fconv": v["ffn_conv_2"].reshape(3, 88, P).transpose(2, 1, 0).reshape(P, 264),
        "fbias": chunks(v["ffn_conv_bias_2"]),
        "sinks": every(v["sinks"]), "alog": every(v["gdn_a_log_2"]), "dtb": every(v["gdn_dt_bias_2"]),
    }
    given = {"consts": _masks(), "onehot": _buckets(),
             "cols": np.ascontiguousarray(np.concatenate([parts[n] for n in COLS], 1)),
             "g_final1": np.ascontiguousarray(every(v["norm_final_g"])),
             "g_final2": np.ascontiguousarray(every(v["final_norm_2"])),
             "x": v["x"], "mem_2": v["mem_2"], "rel_bias": v["rel_bias"], "b_gate": v["b_gate"]}
    for n in ("w_in", "w_gate_up", "w_proj_a", "w_proj_b", "w_out", "w_ffn_gate", "w_ffn_up", "w_ffn_down",
              "w_in_2", "w_out_2", "w_xq_2", "w_xkv_2", "w_xo_2", "w_up_2", "w_down_2"):
        given[n] = v[n][0]
    nc = bacc.Bacc("TRN2", target_bir_lowering=False, num_devices=1)
    arrays, a = {}, {}
    for n, x in given.items():
        arrays[f"in_{n}"] = np.ascontiguousarray(x)
        a[n] = nc.dram_tensor(f"in_{n}", x.shape, mybir.dt.from_np(x.dtype), kind="ExternalInput").ap()
    out = nc.dram_tensor("out_0", (1, T, D), F32, kind="ExternalOutput").ap()
    build_program(nc, a, out)
    r = run_bass_kernel_spmd(nc, [arrays], core_ids=[0])
    return r.results[0]["out_0"]
```
